# Optimizing a Trainium2 kernel written in Bass

```python
import math
import jax
import jax.numpy as jnp
from jax import lax
import numpy as np

D_MODEL = 1024
BATCH = 1
SEQ = 1024
DEPTH = 2
DEC_BATCH = 8
DEC_SEQ = 16
PAST_LEN = 256

CHUNK = 64
HGRN_BLOCK = 16
N_AB = (DEPTH + 1) // 2
N_C = DEPTH // 2
H_A = 8
HD_A = 64
W_A = H_A * HD_A
LORA_W = 64
LORA_A = 64
LORA_G = 128
A_COLS = 3 * W_A + LORA_W + LORA_A + LORA_G
A_SPLITS = (W_A, 2 * W_A, 3 * W_A, 3 * W_A + LORA_W, 3 * W_A + LORA_W + LORA_A)
LNX_EPS = 64e-5
H_B = 16
HD_B = 64
W_B = H_B * HD_B
G_B = 2
N_B = 128
CONV_W = 4
XBC = W_B + 2 * G_B * N_B
B_COLS = W_B + XBC + H_B
IN_AB = A_COLS + B_COLS
MIX_AB = W_A + W_B
H_C = 8
DK_C = 128
DV_C = 128
W_C = H_C * DK_C
IN_C = 4 * W_C
D_FF = -(-8 * D_MODEL // (3 * 256)) * 256

kernel_name = 'rwkv7_mamba2_hgrn2_streaming_encoder_step'

def rms_norm(x, w, eps=1e-6):
    x32 = x.astype(jnp.float32)
    y = x32 * lax.rsqrt(jnp.mean(x32 * x32, axis=-1, keepdims=True) + eps)
    return (y * w.astype(jnp.float32)).astype(x.dtype)

def group_rms_norm(x, w, groups, eps=1e-5):
    shp = x.shape
    x32 = x.astype(jnp.float32).reshape(*shp[:-1], groups, shp[-1] // groups)
    y = x32 * lax.rsqrt(jnp.mean(x32 * x32, axis=-1, keepdims=True) + eps)
    return y.reshape(shp) * w.astype(jnp.float32)

def split_heads(u, n_heads):
    return u.astype(jnp.float32).reshape(*u.shape[:-1], n_heads, u.shape[-1] // n_heads)

def causal_dwconv(u, prev, w, b):
    up = jnp.concatenate([prev.astype(u.dtype), u], axis=1)
    y = lax.conv_general_dilated(up, w[:, None, :].astype(u.dtype), (1,), 'VALID',
                                 dimension_numbers=('NWC', 'WIO', 'NWC'),
                                 feature_group_count=u.shape[-1])
    return y + b, up[:, up.shape[1] - (CONV_W - 1):]

def rwkv7_scan(r, decay, k, v, kk, a, s0):
    def step(s, inp):
        r_t, d_t, k_t, v_t, kk_t, a_t = inp
        sa = jnp.einsum('bhvk,bhk->bhv', s, -kk_t)
        s = (s * d_t[:, :, None, :] + sa[..., None] * (kk_t * a_t)[:, :, None, :]
             + v_t[..., None] * k_t[:, :, None, :])
        return s, jnp.einsum('bhvk,bhk->bhv', s, r_t)
    xs = tuple(jnp.moveaxis(u, 1, 0) for u in (r, decay, k, v, kk, a))
    s_last, o = lax.scan(step, s0.astype(jnp.float32), xs)
    return jnp.moveaxis(o, 0, 1), s_last

def rwkv7_mixer(p, shift_prev, s0, mu, w0, w2, a0, a2, g2, k_k, k_a, r_k, lnx_w, lnx_b):
    bsz, t, _ = p.shape
    p_prev = jnp.concatenate([shift_prev[:, None, :].astype(p.dtype), p[:, :-1]], axis=1)
    pm = p + (p_prev - p) * mu
    r, k, v, xw, xa, xg = jnp.split(pm, A_SPLITS, axis=-1)
    w = -jax.nn.softplus(-(w0 + jnp.tanh(xw) @ w2)) - 0.5
    decay = jnp.exp(-jnp.exp(w.astype(jnp.float32)))
    a = jax.nn.sigmoid(a0 + xa @ a2)
    g = jax.nn.sigmoid(xg) @ g2
    kk = split_heads(k * k_k, H_A)
    kk = kk / jnp.maximum(jnp.sqrt(jnp.sum(kk * kk, axis=-1, keepdims=True)), 1e-12)
    k = k * (1.0 + (a - 1.0) * k_a)
    rh, kh, vh, ah, dh = (split_heads(u, H_A) for u in (r, k, v, a, decay))
    o, s_new = rwkv7_scan(rh, dh, kh, vh, kk, ah, s0)
    mean = jnp.mean(o, axis=-1, keepdims=True)
    var = jnp.mean(jnp.square(o - mean), axis=-1, keepdims=True)
    o = ((o - mean) * lax.rsqrt(var + LNX_EPS)).reshape(bsz, t, W_A) * lnx_w + lnx_b
    bonus = jnp.sum(rh * kh * r_k, axis=-1, keepdims=True) * vh
    out = (o + bonus.reshape(bsz, t, W_A)) * g
    return out, p[:, -1], s_new

def ssd_chunked(x, dt, a_neg, bm, cm, s0, chunk):
    bsz, t = x.shape[:2]
    nc = t // chunk
    hg = H_B // G_B
    xd = (x * dt[..., None]).reshape(bsz, nc, chunk, G_B, hg, HD_B)
    la = (dt * a_neg).reshape(bsz, nc, chunk, G_B, hg)
    bc = bm.reshape(bsz, nc, chunk, G_B, N_B)
    cc = cm.reshape(bsz, nc, chunk, G_B, N_B)
    acum = jnp.cumsum(la, axis=2)
    causal = jnp.tril(jnp.ones((chunk, chunk), bool))[None, None, :, :, None, None]
    seg = acum[:, :, :, None] - acum[:, :, None, :]
    decay_ls = jnp.where(causal, jnp.exp(jnp.where(causal, seg, 0.0)), 0.0)
    cb = jnp.einsum('bclgn,bcsgn->bclsg', cc, bc)
    y_intra = jnp.einsum('bclsg,bclsgh,bcsghp->bclghp', cb, decay_ls, xd)
    to_end = jnp.exp(acum[:, :, -1:] - acum)
    chunk_states = jnp.einsum('bclgn,bclgh,bclghp->bcghpn', bc, to_end, xd)
    chunk_decay = jnp.exp(acum[:, :, -1])

    def step(s, inp):
        st, dec = inp
        return s * dec[..., None, None] + st, s
    s_last, s_in = lax.scan(step, s0.astype(jnp.float32).reshape(bsz, G_B, hg, HD_B, N_B),
                            (jnp.moveaxis(chunk_states, 1, 0), jnp.moveaxis(chunk_decay, 1, 0)))
    s_in = jnp.moveaxis(s_in, 0, 1)
    y_inter = jnp.einsum('bclgn,bcghpn,bclgh->bclghp', cc, s_in, jnp.exp(acum))
    y = (y_intra + y_inter).reshape(bsz, t, H_B, HD_B)
    return y, s_last.reshape(bsz, H_B, HD_B, N_B)

def mamba2_mixer(p, conv_prev, s0, conv_w, conv_b, dt_bias, a_log, d_skip, norm_w, chunk):
    z, xbc, dt = jnp.split(p, (W_B, W_B + XBC), axis=-1)
    xbc_c, conv_new = causal_dwconv(xbc, conv_prev, conv_w, conv_b)
    xbc_c = jax.nn.silu(xbc_c)
    xs, bm, cm = jnp.split(xbc_c, (W_B, W_B + G_B * N_B), axis=-1)
    xs = split_heads(xs, H_B)
    dt = jax.nn.softplus(dt.astype(jnp.float32) + dt_bias.astype(jnp.float32))
    y, s_new = ssd_chunked(xs, dt, -jnp.exp(a_log.astype(jnp.float32)),
                           split_heads(bm, G_B), split_heads(cm, G_B), s0, chunk)
    y = y + d_skip[:, None] * xs
    y = y.reshape(*y.shape[:2], W_B) * jax.nn.silu(z.astype(jnp.float32))
    return group_rms_norm(y, norm_w, G_B), conv_new, s_new

def gla_chunked(q, k, v, log_f, s0, chunk):
    bsz, t = q.shape[:2]
    nc = t // chunk
    q, k, v, log_f = (u.reshape(bsz, nc, chunk, H_C, u.shape[-1]) for u in (q, k, v, log_f))
    bcum = jnp.cumsum(log_f, axis=2)
    causal = jnp.tril(jnp.ones((chunk, chunk), bool))[:, :, None, None]
    seg = bcum[:, :, :, None] - bcum[:, :, None, :]
    decay_ls = jnp.where(causal, jnp.exp(jnp.where(causal, seg, 0.0)), 0.0)
    att = jnp.einsum('bclhk,bcshk,bclshk->bchls', q, k, decay_ls)
    o_intra = jnp.einsum('bchls,bcshv->bclhv', att, v)
    chunk_states = jnp.einsum('bclhk,bclhv->bchkv', k * jnp.exp(bcum[:, :, -1:] - bcum), v)
    chunk_decay = jnp.exp(bcum[:, :, -1])

    def step(s, inp):
        st, dec = inp
        return s * dec[..., None] + st, s
    s_last, s_in = lax.scan(step, s0.astype(jnp.float32),
                            (jnp.moveaxis(chunk_states, 1, 0), jnp.moveaxis(chunk_decay, 1, 0)))
    s_in = jnp.moveaxis(s_in, 0, 1)
    o_inter = jnp.einsum('bclhk,bchkv->bclhv', q * jnp.exp(bcum), s_in)
    return (o_intra + o_inter).reshape(bsz, t, H_C, DV_C), s_last

def hgrn2_mixer(p, s0, lb, norm_w, chunk):
    q, f, i, g = jnp.split(p, 4, axis=-1)
    f = f.astype(jnp.float32)
    lb = lb.astype(jnp.float32)
    log_f = jnp.log(lb + (1.0 - lb) * jax.nn.sigmoid(f))
    k = (1.0 - lb) * jax.nn.sigmoid(-f)
    o, s_new = gla_chunked(split_heads(jax.nn.silu(q), H_C), split_heads(k, H_C),
                           split_heads(i, H_C), split_heads(log_f, H_C), s0, chunk)
    o = group_rms_norm(o.reshape(*o.shape[:2], W_C), norm_w, H_C) * jax.nn.silu(g.astype(jnp.float32))
    return o, s_new

def trunk(x, c, st_rwkv, st_shift, st_ssm, st_conv, st_hgrn,
          norm_mix_w, norm_ffn_w, norm_out_w, ada_w, ada_b,
          w_in_ab, w_out_ab, mu_a, w0, w2, a0, a2, g2, k_k, k_a, r_k, lnx_w, lnx_b,
          conv_w, conv_b, dt_bias, a_log, d_skip, norm_b_w,
          w_in_c, w_out_c, lb_param, norm_c_w,
          w_gate, w_up, w_down):
    chunk = math.gcd(CHUNK, x.shape[1])
    chunk_c = math.gcd(HGRN_BLOCK, x.shape[1])
    lb_soft = jax.nn.softmax(lb_param.astype(jnp.float32), axis=0)
    lb_all = jnp.cumsum(lb_soft, axis=0) - lb_soft[0]
    new_rwkv, new_shift, new_ssm, new_conv, new_hgrn = [], [], [], [], []
    for layer in range(DEPTH):
        j = layer // 2
        mod = jax.nn.silu(c) @ ada_w[layer] + ada_b[layer]
        sh_m, sc_m, g_m, sh_f, sc_f, g_f = jnp.split(mod[:, None, :], 6, axis=-1)
        h = rms_norm(x, norm_mix_w[layer]) * (1.0 + sc_m) + sh_m
        if layer % 2 == 0:
            proj = h @ w_in_ab[j]
            oa, shift_new, rwkv_new = rwkv7_mixer(proj[..., :A_COLS], st_shift[:, j], st_rwkv[:, j],
                                                  mu_a[j], w0[j], w2[j], a0[j], a2[j], g2[j],
                                                  k_k[j], k_a[j], r_k[j], lnx_w[j], lnx_b[j])
            ob, conv_new, ssm_new = mamba2_mixer(proj[..., A_COLS:], st_conv[:, j], st_ssm[:, j],
                                                 conv_w[j], conv_b[j], dt_bias[j], a_log[j],
                                                 d_skip[j], norm_b_w[j], chunk)
            mix = jnp.concatenate([oa.astype(x.dtype), ob.astype(x.dtype)], axis=-1) @ w_out_ab[j]
            new_rwkv.append(rwkv_new)
            new_shift.append(shift_new)
            new_ssm.append(ssm_new)
            new_conv.append(conv_new)
        else:
            oc, hgrn_new = hgrn2_mixer(h @ w_in_c[j], st_hgrn[:, j], lb_all[j], norm_c_w[j], chunk_c)
            mix = oc.astype(x.dtype) @ w_out_c[j]
            new_hgrn.append(hgrn_new)
        x = x + g_m * mix
        h = rms_norm(x, norm_ffn_w[layer]) * (1.0 + sc_f) + sh_f
        x = x + g_f * ((jax.nn.silu(h @ w_gate[layer]) * (h @ w_up[layer])) @ w_down[layer])
    y = rms_norm(x, norm_out_w)
    return (y, jnp.stack(new_rwkv, axis=1), jnp.stack(new_shift, axis=1), jnp.stack(new_ssm, axis=1),
            jnp.stack(new_conv, axis=1), jnp.stack(new_hgrn, axis=1))

def setup_inputs(seed: int = 0) -> dict:
    key = jax.random.key(seed)
    ks = iter(jax.random.split(key, 64))

    def nrm(shape, scale):
        return jax.random.normal(next(ks), shape, jnp.float32) * scale

    def unif(shape, lo, hi):
        return jax.random.uniform(next(ks), shape, jnp.float32, lo, hi)

    d = D_MODEL
    inputs = {}
    inputs['x_prompt'] = nrm((BATCH, SEQ, d), 1.0)
    inputs['x_sample'] = nrm((DEC_BATCH, DEC_SEQ, d), 1.0)
    inputs['state_rwkv'] = nrm((DEC_BATCH, N_AB, H_A, HD_A, HD_A), 0.3)
    inputs['state_rwkv_shift'] = nrm((DEC_BATCH, N_AB, A_COLS), 1.0)
    inputs['state_ssm'] = nrm((DEC_BATCH, N_AB, H_B, HD_B, N_B), 0.1)
    inputs['state_conv'] = nrm((DEC_BATCH, N_AB, CONV_W - 1, XBC), 1.0)
    inputs['state_hgrn'] = nrm((DEC_BATCH, N_C, H_C, DK_C, DV_C), 0.3)
    inputs['c_prompt'] = nrm((BATCH, d), 1.0)
    inputs['c_sample'] = nrm((DEC_BATCH, d), 1.0)
    inputs['norm_mix_w'] = 1.0 + nrm((DEPTH, d), 0.02)
    inputs['norm_ffn_w'] = 1.0 + nrm((DEPTH, d), 0.02)
    inputs['norm_out_w'] = 1.0 + nrm((d,), 0.02)
    inputs['ada_w'] = nrm((DEPTH, d, 6 * d), 0.5 * d ** -0.5)
    inputs['ada_b'] = nrm((DEPTH, 6 * d), 0.02)
    inputs['w_in_ab'] = nrm((N_AB, d, IN_AB), d ** -0.5)
    inputs['w_out_ab'] = nrm((N_AB, MIX_AB, d), MIX_AB ** -0.5)
    inputs['mu_a'] = unif((N_AB, A_COLS), 0.0, 1.0)
    inputs['w0'] = unif((N_AB, W_A), -5.0, 0.0)
    inputs['w2'] = nrm((N_AB, LORA_W, W_A), 0.1)
    inputs['a0'] = nrm((N_AB, W_A), 0.5)
    inputs['a2'] = nrm((N_AB, LORA_A, W_A), 0.1)
    inputs['g2'] = nrm((N_AB, LORA_G, W_A), LORA_G ** -0.5)
    inputs['k_k'] = 0.85 + nrm((N_AB, W_A), 0.02)
    inputs['k_a'] = 1.0 + nrm((N_AB, W_A), 0.02)
    inputs['r_k'] = nrm((N_AB, H_A, HD_A), 0.1)
    inputs['lnx_w'] = 1.0 + nrm((N_AB, W_A), 0.02)
    inputs['lnx_b'] = nrm((N_AB, W_A), 0.02)
    inputs['conv_w'] = nrm((N_AB, CONV_W, XBC), CONV_W ** -0.5)
    inputs['conv_b'] = nrm((N_AB, XBC), 0.02)
    dt0 = jnp.exp(unif((N_AB, H_B), math.log(1e-3), math.log(1e-1)))
    inputs['dt_bias'] = dt0 + jnp.log(-jnp.expm1(-dt0))
    inputs['a_log'] = jnp.log(unif((N_AB, H_B), 1.0, 16.0))
    inputs['d_skip'] = 1.0 + nrm((N_AB, H_B), 0.1)
    inputs['norm_b_w'] = 1.0 + nrm((N_AB, W_B), 0.02)
    inputs['w_in_c'] = nrm((N_C, d, IN_C), d ** -0.5)
    inputs['w_out_c'] = nrm((N_C, W_C, d), W_C ** -0.5)
    inputs['lb_param'] = nrm((N_C, W_C), 0.1)
    inputs['norm_c_w'] = 1.0 + nrm((N_C, W_C), 0.02)
    inputs['w_gate'] = nrm((DEPTH, d, D_FF), d ** -0.5)
    inputs['w_up'] = nrm((DEPTH, d, D_FF), d ** -0.5)
    inputs['w_down'] = nrm((DEPTH, D_FF, d), D_FF ** -0.5)
    return inputs

def reference(x_prompt, x_sample, state_rwkv, state_rwkv_shift, state_ssm, state_conv, state_hgrn,
              c_prompt, c_sample, norm_mix_w, norm_ffn_w, norm_out_w, ada_w, ada_b,
              w_in_ab, w_out_ab, mu_a, w0, w2, a0, a2, g2, k_k, k_a, r_k, lnx_w, lnx_b,
              conv_w, conv_b, dt_bias, a_log, d_skip, norm_b_w,
              w_in_c, w_out_c, lb_param, norm_c_w, w_gate, w_up, w_down):
    weights = (norm_mix_w, norm_ffn_w, norm_out_w, ada_w, ada_b,
               w_in_ab, w_out_ab, mu_a, w0, w2, a0, a2, g2, k_k, k_a, r_k, lnx_w, lnx_b,
               conv_w, conv_b, dt_bias, a_log, d_skip, norm_b_w,
               w_in_c, w_out_c, lb_param, norm_c_w, w_gate, w_up, w_down)
    bp = x_prompt.shape[0]
    z_rwkv = jnp.zeros((bp, N_AB, H_A, HD_A, HD_A), jnp.float32)
    z_shift = jnp.zeros((bp, N_AB, A_COLS), x_prompt.dtype)
    z_ssm = jnp.zeros((bp, N_AB, H_B, HD_B, N_B), jnp.float32)
    z_conv = jnp.zeros((bp, N_AB, CONV_W - 1, XBC), x_prompt.dtype)
    z_hgrn = jnp.zeros((bp, N_C, H_C, DK_C, DV_C), jnp.float32)
    y_prompt, p_rwkv, p_shift, p_ssm, p_conv, p_hgrn = trunk(
        x_prompt, c_prompt, z_rwkv, z_shift, z_ssm, z_conv, z_hgrn, *weights)
    y_sample, s_rwkv, s_shift, s_ssm, s_conv, s_hgrn = trunk(
        x_sample, c_sample, state_rwkv, state_rwkv_shift, state_ssm, state_conv, state_hgrn, *weights)
    return (y_prompt, y_sample, p_rwkv, p_shift, p_ssm, p_conv, p_hgrn,
            s_rwkv, s_shift, s_ssm, s_conv, s_hgrn)


_drawn_inputs = setup_inputs


def setup_inputs(seed=0):
    import zlib

    import numpy as np

    out = dict(_drawn_inputs(seed))
    spreads = {}
    factors = {'state_hgrn': 8.0,
     'norm_ffn_w': 7.223,
     'norm_out_w': 7.994,
     'lnx_w': 36.747,
     'lnx_b': 41.259,
     'd_skip': 3.604,
     'norm_b_w': 8.0,
     'norm_c_w': 64.0,
     'r_k': 2.782}
    for name, (base, spread) in spreads.items():
        noise = np.random.default_rng([zlib.crc32(name.encode()), seed]).standard_normal(out[name].shape)
        drawn = base * np.exp(spread * noise) if base else spread * noise
        out[name] = jnp.asarray(drawn.astype(out[name].dtype))
    for name, factor in factors.items():
        out[name] = (out[name] * factor).astype(out[name].dtype)
    return out
```

```python
import math
from contextlib import ExitStack, contextmanager

import concourse.bass as bass
from concourse import mybir

F32 = mybir.dt.float32
ACT = mybir.ActivationFunctionType
ALU = mybir.AluOpType
ds = bass.ds

P = 128
D = 1024
KD = D // P
TP = 1024
NS, LS = 8, 16
T = TP + NS * LS
NT = T // P
NTP = TP // P
CH = 384
NCH = T // CH
SEQS = 1 + NS
BLK = 16
NB = P // BLK
DEPTH = 2
FF = 2816
KF = FF // P
KACT = 12
SLAB = 256
BANK = 512

WA = 512
A_COLS = 1792
NA = A_COLS // P
JR, JK, JV, JWA, JG = 0, 4, 8, 12, 13
JZ, JX, JB, JC = 14, 22, 30, 32
XBC = 1536
NXBC = XBC // P
HB = 16
IN_AB = 4368
NAB = IN_AB // P
IN_C = 4096
NC_ = IN_C // P
HALO = 3
TAIL = 3
LNX_EPS = 64e-5
KAPPA = math.exp(-0.5)

ROW_A = {"ada_b": 0, "norm_mix_w": 96, "norm_ffn_w": 112}
ROW_B = {"norm_out_w": 0, "mu_a": 8, "w0": 22, "a0": 26, "k_k": 30, "k_a": 34, "r_k": 38, "lnx_w": 42,
         "lnx_b": 46, "conv_b": 50, "norm_b_w": 62, "norm_c_w": 70, "conv_w": 78}
NROW_B = 126


class Core:
    pass


def bc(ap, axis, n):
    ap = ap.unsqueeze(axis)
    shape = list(ap.shape)
    shape[axis] = n
    return ap.to_broadcast(shape)


class Phase:

    def __init__(self, nc, name):
        self.nc, self.name, self.ctx, self.own_sems = nc, name, ExitStack(), []

    def __enter__(self):
        return self

    def __exit__(self, *a):
        self.ctx.__exit__(*a)
        self.nc.clear_and_free_semaphores(self.own_sems)
        self.nc.all_engine_barrier(sem_only=True)

    def sb(self, name, shape, dt=F32):
        return self.ctx.enter_context(self.nc.sbuf_tensor(f"{self.name}_{name}", shape, dt))

    def ps(self, name, shape):
        return self.ctx.enter_context(self.nc.psum_tensor(f"{self.name}_{name}", shape, F32))

    def sems(self, names):
        new = [self.nc.alloc_semaphore(f"{self.name}_{n}") for n in names.split()]
        self.own_sems += new
        return new

    def block(self):
        return self.ctx.enter_context(self.nc.Block())


def constants(nc, g):
    with Phase(nc, "const") as ph:
        step, = ph.sems("step")
        block = ph.block()

        @block.gpsimd
        def _(pool):
            n = [0]

            def then(ins):
                ins.then_inc(step, 1)
                n[0] += 1
                pool.wait_ge(step, n[0])

            def keep(view, base, mult, pattern, op=ALU.is_ge, fill=0.0):
                then(nc.gpsimd.affine_select(out=view, in_=view, compare_op=op, fill=fill, base=base,
                                             pattern=pattern, channel_multiplier=mult))

            def blocks(ap, size):
                return ap.rearrange("p (b j) -> p b j", j=size)

            then(nc.gpsimd.memset(g.ident[:, :], 0.0))
            keep(g.ident[:, :], 0, 1, [[-1, P]], ALU.not_equal, 1.0)
            then(nc.gpsimd.memset(g.ones[:, :], 1.0))
            then(nc.gpsimd.memset(g.ones64[:, :], 1.0))
            v = blocks(g.ones64[:, :], 64)
            keep(v, 0, 1, [[-64, 2], [0, 64]])
            keep(v, 63, -1, [[64, 2], [0, 64]])
            then(nc.gpsimd.memset(g.blockmask[:, :], 1.0))
            keep(g.blockmask[:, :], 0, 1, [[-BLK, NB]])
            keep(g.blockmask[:, :], BLK - 1, -1, [[BLK, NB]])
            then(nc.gpsimd.memset(g.reset[:, :], 1.0))
            then(nc.gpsimd.memset(blocks(g.reset[:, :], BLK)[:, :, 0:1], 0.0))
            for m, strict in ((g.before, 1), (g.notafter, 0)):
                then(nc.gpsimd.memset(m[:, :], 1.0))
                v = blocks(m[:, :], BLK)
                keep(v, -strict, -1, [[BLK, NB], [1, BLK]])
                keep(v, 0, 1, [[-BLK, NB], [0, BLK]])
            then(nc.gpsimd.memset(g.after[:, :], 1.0))
            v = blocks(g.after[:, :], BLK)
            keep(v, -1, 1, [[-BLK, NB], [-1, BLK]])
            keep(v, BLK - 1, -1, [[BLK, NB], [0, BLK]])
            for i in range(2):
                then(nc.gpsimd.tensor_copy(g.gram_mask[:, i, 0, :], g.before[:, :]))
                then(nc.gpsimd.tensor_copy(g.gram_mask[:, i, 1, :], g.notafter[:, :]))
            then(nc.gpsimd.memset(g.notafter128[:, :], 1.0))
            keep(g.notafter128[:, :], 0, -1, [[1, P]])
            then(nc.gpsimd.memset(g.after128[:, :], 1.0))
            keep(g.after128[:, :], -1, 1, [[-1, P]])
            then(nc.gpsimd.memset(g.level_mask[:, :, :], 0.0))
            for i, h in enumerate((8, 4, 2, 1)):
                v = g.level_mask[:, i, :].rearrange("p (m u j) -> p m u j", u=2, j=h)[:, :, 1, :]
                then(nc.gpsimd.memset(v, 1.0))
                keep(v, 0, 1, [[-2 * h, P // (2 * h)], [0, h]])
                keep(v, h - 1, -1, [[2 * h, P // (2 * h)], [0, h]])
            then(nc.gpsimd.tensor_copy(g.level_mask[:, 4, :], g.ident[:, :]))


def load_inputs(nc, g, A):
    with Phase(nc, "load") as ph:
        rows_a = ph.sb("rows_a", [P, P])
        rows_b = ph.sb("rows_b", [NROW_B, P])
        c_rows = ph.sb("c_rows", [SEQS, D])
        sc_rows = ph.sb("sc_rows", [SEQS, D])
        shift_rows = ph.sb("shift_rows", [NS, A_COLS])
        conv_rows = ph.sb("conv_rows", [NS * 3, XBC])
        x_rows = ph.sb("x_rows", [P, 2, D])
        zeros = ph.sb("zeros", [P, NAB + 1, HALO])
        pt = ph.ps("pt", [P, 2, 2, BANK])
        pq = ph.ps("pq", [P, 3, BANK])
        (params_in, cond_in, states_in, silu_done, params_T, shift_T, conv_T,
         halo_zero, halo_out, x_in0, x_in1, x_T, x_out_a, x_out_v, small_in) = ph.sems(
            "params_in cond_in states_in silu_done params_T shift_T conv_T "
            "halo_zero halo_out x_in0 x_in1 x_T x_out_a x_out_v small_in")
        x_in = (x_in0, x_in1)
        block = ph.block()

        def rows(eng, dst, at, src, n):
            eng.dma_start(dst[at:at + n, :], src).then_inc(params_in, 16)

        n_params = 3 + len(ROW_B)

        @block.sync
        def _(sp):
            sp.dma_start(c_rows[0:1, :], A["c_prompt"]).then_inc(cond_in, 16)
            sp.dma_start(c_rows[1:SEQS, :], A["c_sample"]).then_inc(cond_in, 16)
            for name, at in ROW_A.items():
                src = A[name].rearrange("l (t p) -> (l t) p", p=P)
                rows(sp, rows_a, at, src, src.shape[0])
            for name, at in ROW_B.items():
                src = A[name]
                if name == "norm_out_w":
                    src = src.rearrange("(t p) -> t p", p=P)
                elif name == "r_k":
                    src = src.rearrange("l (t h) k -> (l t) (h k)", h=2)
                elif name == "conv_w":
                    src = src.rearrange("l w (t p) -> (l w t) p", p=P)
                else:
                    src = src.rearrange("l (t p) -> (l t) p", p=P)
                rows(sp, rows_b, at, src, src.shape[0])
            sp.dma_start(shift_rows[:, :], A["state_rwkv_shift"].rearrange("b l n -> (b l) n")).then_inc(states_in, 16)
            sp.dma_start(conv_rows[:, :], A["state_conv"].rearrange("b l w n -> (b l w) n")).then_inc(states_in, 16)
            xp = A["x_prompt"].rearrange("o (t p) d -> (o t) p d", p=P)

            def load_x(t, u, src, turn):
                if turn is not None:
                    sp.wait_ge(x_T, turn)
                sp.dma_start(x_rows[:, u, :], src).then_inc(x_in[u], 16)
            load_x(0, 0, xp[0], None)
            load_x(1, 1, xp[1], None)
            for t in range(2, NTP):
                load_x(t, t % 2, xp[t], t - 1)
            load_x(NTP, NTP % 2, A["x_sample"].rearrange("b s d -> (b s) d"), NTP - 1)
            sp.wait_ge(halo_zero, 1)
            sp.dma_start(g.pT[0:NAB * P, 0:HALO].rearrange("(j p) c -> p j c", p=P),
                         zeros[:, 0:NAB, :]).then_inc(halo_out, 16)
            sp.wait_ge(halo_out, 16)

        @block.gpsimd
        def _(pool):
            nc.gpsimd.memset(zeros[:, :, :], 0.0).then_inc(halo_zero, 1)
            for h in range(2):
                src = A["d_skip"].rearrange("o (t h) -> (o h) t", h=2)[h:h + 1, :]
                pool.dma_start(g.dskip[64 * h:64 * h + 64, :], src.to_broadcast([64, 8]),
                               allow_slow_non_contiguous=True).then_inc(small_in, 16)
            pool.dma_start(g.dt_bias[:, :], A["dt_bias"].rearrange("o h -> h o"), allow_slow_non_contiguous=True).then_inc(small_in, 16)
            pool.dma_start(g.a_log[:, :], A["a_log"].rearrange("o h -> h o"), allow_slow_non_contiguous=True).then_inc(small_in, 16)
            pool.wait_ge(small_in, 64)

        @block.scalar
        def _(act):
            act.wait_ge(cond_in, 32)
            nc.scalar.activation(sc_rows[:, :], c_rows[:, :], ACT.Silu).then_inc(silu_done, 1)
            for t in range(NT):
                act.wait_ge(x_T, t + 1)
                nc.scalar.copy(g.xT[:, 0:4, t * P:(t + 1) * P],
                               pt[:, t % 2, 0, :].rearrange("p (k c) -> p k c", c=P)).then_inc(x_out_a, 1)

        @block.vector
        def _(dve):
            dve.wait_ge(params_T, 1)
            nc.vector.tensor_copy(g.colA[:, :], pq[:, 0, 0:P])
            nc.vector.tensor_copy(g.colB[:, :], pq[:, 0, P:P + NROW_B])
            dve.wait_ge(shift_T, 1)
            nc.vector.tensor_copy(g.scT[:, :, :], pq[:, 1, 0:KD * SEQS].rearrange("p (k s) -> p k s", s=SEQS))
            nc.vector.tensor_copy(g.shiftT[:, :, :], pq[:, 1, P:P + NA * NS].rearrange("p (k s) -> p k s", s=NS))
            dve.wait_ge(conv_T, 1)
            nc.vector.tensor_copy(g.convT[:, :, :], pq[:, 2, 0:NXBC * NS * 3].rearrange("p (k s) -> p k s", s=NS * 3))
            for t in range(NT):
                dve.wait_ge(x_T, t + 1)
                nc.vector.tensor_copy(g.xT[:, 4:8, t * P:(t + 1) * P],
                                      pt[:, t % 2, 1, :].rearrange("p (k c) -> p k c", c=P)).then_inc(x_out_v, 1)

        @block.tensor
        def _(pe):
            pe.wait_ge(params_in, 16 * n_params)
            nc.tensor.transpose(pq[:, 0, 0:P], rows_a[:, :], g.ident[:, :])
            nc.tensor.transpose(pq[:, 0, P:P + NROW_B], rows_b[:, :], g.ident[0:NROW_B, 0:NROW_B]).then_inc(params_T, 1)
            pe.wait_ge(silu_done, 1)
            for k in range(KD):
                ins = nc.tensor.transpose(pq[:, 1, k * SEQS:(k + 1) * SEQS], sc_rows[:, k * P:(k + 1) * P],
                                          g.ident[0:SEQS, 0:SEQS])
            pe.wait_ge(states_in, 32)
            for j in range(NA):
                ins = nc.tensor.transpose(pq[:, 1, P + j * NS:P + (j + 1) * NS], shift_rows[:, j * P:(j + 1) * P],
                                          g.ident[0:NS, 0:NS])
            ins.then_inc(shift_T, 1)
            for j in range(NXBC):
                ins = nc.tensor.transpose(pq[:, 2, j * 24:(j + 1) * 24], conv_rows[:, j * P:(j + 1) * P],
                                          g.ident[0:24, 0:24])
            ins.then_inc(conv_T, 1)
            for t in range(NT):
                pe.wait_ge(x_in[t % 2], 16 * (t // 2 + 1))
                if t >= 2:
                    pe.wait_ge(x_out_a, t - 1)
                    pe.wait_ge(x_out_v, t - 1)
                for k in range(KD):
                    ins = nc.tensor.transpose(pt[:, t % 2, k // 4, (k % 4) * P:(k % 4 + 1) * P],
                                              x_rows[:, t % 2, k * P:(k + 1) * P], g.ident[:, :])
                ins.then_inc(x_T, 1)


def modulation(nc, g, A):
    GW = 512
    NG = 6 * D // GW
    with Phase(nc, "ada") as ph:
        w = ph.sb("w", [P, 2, KD, GW])
        rows = ph.sb("rows", [SEQS, 2, GW])
        pm = ph.ps("pm", [P, 2, BANK])
        pt = ph.ps("pt", [P, 2, BANK])
        w_in0, w_in1, slot_free, pm_free, pt_free, rows_out, rows_T, waited = ph.sems(
            "w_in0 w_in1 slot_free pm_free pt_free rows_out rows_T waited")
        w_in = (w_in0, w_in1)
        block = ph.block()
        src = A["ada_w"].rearrange("l (k p) n -> p l k n", p=P)

        @block.sync
        def _(sp):
            for layer in range(DEPTH):
                with sp.Fori(0, NG // 2) as i:
                    for u in range(2):
                        at = sp.snap((2 * i + u) * GW)
                        turn = sp.snap(2 * i + (u + layer * NG + 1))
                        sp.wait_ge(slot_free, turn)
                        sp.dma_start(w[:, u, :, :], src[:, layer, :, ds(at, GW)]).then_inc(w_in[u], 16)

        @block.tensor
        def _(pe):
            pe.sem_inc(slot_free, 2)
            for layer in range(DEPTH):
                with pe.Fori(0, NG // 2) as i:
                    for u in range(2):
                        turn = pe.snap(2 * i + (u + layer * NG + 1))
                        pe.wait_ge(w_in[u], i * 16 + (layer * NG // 2 + 1) * 16)
                        pe.wait_ge(pm_free, turn)
                        for k in range(KD):
                            ins = nc.tensor.matmul(pm[0:SEQS, u, :], g.scT[:, k, :], w[:, u, k, :],
                                                   start=(k == 0), stop=(k == KD - 1))
                        ins.then_inc(slot_free, 1)
                        pe.wait_ge(rows_out, turn)
                        pe.wait_ge(pt_free, turn)
                        pe.sem_inc(waited, 1)
                        for q in range(GW // P):
                            ins = nc.tensor.transpose(pt[:, u, q * SEQS:(q + 1) * SEQS],
                                                      rows[:, u, q * P:(q + 1) * P], g.ident[0:SEQS, 0:SEQS])
                        ins.then_inc(rows_T, 1)

        @block.scalar
        def _(act):
            act.sem_inc(pm_free, 2)
            for layer in range(DEPTH):
                with act.Fori(0, NG // 2) as i:
                    for u in range(2):
                        act.wait_ge(slot_free, 2 * i + (u + layer * NG + 3))
                        nc.scalar.copy(rows[:, u, :], pm[0:SEQS, u, :]).then_inc(rows_out, 1)
                        act.wait_ge(rows_out, 2 * i + (u + layer * NG + 1))
                        act.sem_inc(pm_free, 1)

        @block.vector
        def _(dve):
            dve.sem_inc(pt_free, 2)
            for layer in range(DEPTH):
                with dve.Fori(0, NG // 2) as i:
                    for u in range(2):
                        at = dve.snap((2 * i + u) * (GW // P) + layer * 6 * KD)
                        dve.wait_ge(rows_T, 2 * i + (u + layer * NG + 1))
                        nc.vector.tensor_tensor(
                            g.mod[:, ds(at, GW // P), :],
                            pt[:, u, 0:GW // P * SEQS].rearrange("p (q s) -> p q s", s=SEQS),
                            bc(g.colA[:, ds(at, GW // P)], 2, SEQS), ALU.add).then_inc(pt_free, 1)
            dve.wait_ge(pt_free, 2 + DEPTH * NG)
            for layer in range(DEPTH):
                for which, name in enumerate(("norm_mix_w", "norm_ffn_w")):
                    at = ROW_A[name] + layer * KD
                    nc.vector.scalar_tensor_tensor(g.scale[:, layer, which, :, :],
                                                   g.modcol(layer, 3 * which + 1), 1.0,
                                                   bc(g.colA[:, at:at + KD], 2, SEQS), ALU.add, ALU.mult)


def mean_square_steps(nc, g, block, ss, rstd, sems):
    squared, summed, mean_done, inv_done, rstd_done = sems

    @block.tensor
    def _(pe):
        for k in range(KD):
            pe.wait_ge(squared, k + 1)
            for c in range(NCH):
                ins = nc.tensor.matmul(ss[:, c, 0:CH], g.ones[:, :], g.hT[:, k, c * CH:(c + 1) * CH],
                                       start=(k == 0), stop=(k == KD - 1))
        ins.then_inc(summed, 1)

    def scalar_steps(act):
        for k in range(KD):
            nc.scalar.activation(g.hT[:, k, :], g.xT[:, k, :], ACT.Square).then_inc(squared, 1)
        act.wait_ge(inv_done, 1)
        nc.scalar.activation(rstd[:, :], rstd[:, :], ACT.Sqrt).then_inc(rstd_done, 1)

    def vector_steps(dve):
        dve.wait_ge(summed, 1)
        nc.vector.tensor_scalar(rstd[:, :].rearrange("p (c n) -> p c n", n=CH), ss[:, :, 0:CH],
                                1.0 / D, 1e-6, ALU.mult, ALU.add).then_inc(mean_done, 1)
        dve.wait_ge(mean_done, 1)
        nc.vector.reciprocal(rstd[:, :], rstd[:, :]).then_inc(inv_done, 1)
        dve.wait_ge(rstd_done, 1)

    return scalar_steps, vector_steps


def norm(nc, g, layer, which):
    with Phase(nc, f"norm{layer}{which}") as ph:
        rstd = ph.sb("rstd", [P, T])
        ss = ph.ps("ss", [P, NCH, BANK])
        sems = ph.sems("squared summed mean_done inv_done rstd_done")
        scaled, sample_mul = ph.sems("scaled sample_mul")
        block = ph.block()
        sc, sh = g.scale[:, layer, which, :, :], g.modcol(layer, 3 * which)
        scalar_steps, vector_steps = mean_square_steps(nc, g, block, ss, rstd, sems)

        @block.scalar
        def _(act):
            scalar_steps(act)
            for k in range(KD):
                act.wait_ge(scaled, k + 1)
                nc.scalar.activation(g.hT[:, k, 0:TP], g.hT[:, k, 0:TP], ACT.Identity,
                                     bias=sh[:, k, 0:1], scale=sc[:, k, 0:1])

        @block.vector
        def _(dve):
            vector_steps(dve)
            for k in range(KD):
                nc.vector.tensor_tensor(g.hT[:, k, :], g.xT[:, k, :], rstd[:, :], ALU.mult).then_inc(scaled, 1)

        @block.gpsimd
        def _(pool):
            for k in range(KD):
                pool.wait_ge(scaled, k + 1)
                v = g.hT[:, k, TP:T].rearrange("p (s t) -> p s t", t=LS)
                nc.gpsimd.tensor_tensor(v, v, bc(sc[:, k, 1:SEQS], 2, LS), ALU.mult).then_inc(sample_mul, 1)
                pool.wait_ge(sample_mul, k + 1)
                nc.gpsimd.tensor_tensor(v, v, bc(sh[:, k, 1:SEQS], 2, LS), ALU.add)


def project_to_dram(nc, g, weights, n_cols, name, tails):
    n_slabs, rest = n_cols // SLAB, n_cols % SLAB
    with Phase(nc, name) as ph:
        w = ph.sb("w", [P, 2, KD, SLAB])
        out = ph.sb("out", [P, 2, T])
        acc = ph.ps("acc", [P, 2, 4, BANK])
        slab_free, w_in0, w_in1, rest_in, mm_done, acc_free, copied, stored0, stored1, tail_done = ph.sems(
            "slab_free w_in0 w_in1 rest_in mm_done acc_free copied stored0 stored1 tail_done")
        w_in, stored = (w_in0, w_in1), (stored0, stored1)
        block = ph.block()
        src = weights.rearrange("(k p) n -> p k n", p=P)

        def each_slab(eng, body):
            with eng.Fori(0, n_slabs // 2) as i:
                for u in range(2):
                    body(u, eng.snap(2 * i + (u + 1)), i)
            if n_slabs % 2:
                body(0, n_slabs, n_slabs // 2)

        @block.sync
        def _(sp):
            def load(u, turn, pair):
                at = (pair * 2 + u) * SLAB
                if not isinstance(pair, int):
                    at = sp.snap(at)
                sp.wait_ge(slab_free, turn)
                sp.dma_start(w[:, u, :, :], src[:, :, ds(at, SLAB)]).then_inc(w_in[u], 16)
            each_slab(sp, load)
            if rest:
                sp.wait_ge(slab_free, n_slabs + 1)
                sp.dma_start(w[:, n_slabs % 2, :, 0:rest], src[:, :, n_slabs * SLAB:n_cols]).then_inc(rest_in, 16)

        @block.tensor
        def _(pe):
            pe.sem_inc(slab_free, 2)

            def multiply(u, turn, pair):
                pe.wait_ge(w_in[u], pair * 16 + 16)
                for n in range(2):
                    pe.wait_ge(acc_free, turn * 2 + (n - 1))
                    for k in range(KD):
                        for c in range(NCH):
                            ins = nc.tensor.matmul(acc[:, n, c, 0:CH], w[:, u, k, n * P:(n + 1) * P],
                                                   g.hT[:, k, c * CH:(c + 1) * CH],
                                                   start=(k == 0), stop=(k == KD - 1))
                    ins.then_inc(mm_done, 1)
                    if n == 1:
                        pe.wait_ge(mm_done, turn * 2)
                        pe.sem_inc(slab_free, 1)
            each_slab(pe, multiply)
            if rest:
                pe.wait_ge(rest_in, 16)
                pe.wait_ge(acc_free, 2 * n_slabs + 1)
                for k in range(KD):
                    for c in range(NCH):
                        ins = nc.tensor.matmul(acc[0:rest, 0, c, 0:CH], w[:, n_slabs % 2, k, 0:rest],
                                               g.hT[:, k, c * CH:(c + 1) * CH], start=(k == 0), stop=(k == KD - 1))
                ins.then_inc(mm_done, 1)

        @block.scalar
        def _(act):
            act.sem_inc(acc_free, 2)
            act.sem_inc(stored0, 16)
            act.sem_inc(stored1, 16)

            def store(u, turn, pair):
                for n in range(2):
                    tile, row = turn * 2 + (n - 1), (pair * 4 + (2 * u + n)) * P
                    if not isinstance(pair, int):
                        tile, row = act.snap(tile), act.snap(row)
                    act.wait_ge(mm_done, tile)
                    act.wait_ge(stored[n], turn * 16)
                    if tails:
                        act.wait_ge(tail_done, tile)
                    nc.scalar.copy(out[:, n, :].rearrange("p (c n) -> p c n", n=CH),
                                   acc[:, n, 0:NCH, 0:CH]).then_inc(copied, 1)
                    act.wait_ge(copied, tile)
                    act.sem_inc(acc_free, 1)
                    act.dma_start(g.pT[ds(row, P), HALO:HALO + T], out[:, n, :]).then_inc(stored[n], 16)
            each_slab(act, store)
            if rest:
                act.wait_ge(mm_done, 2 * n_slabs + 1)
                act.wait_ge(stored0, 16 * n_slabs + 16)
                if tails:
                    act.wait_ge(tail_done, 2 * n_slabs + 1)
                nc.scalar.copy(out[0:rest, 0, :].rearrange("p (c n) -> p c n", n=CH),
                               acc[0:rest, 0, 0:NCH, 0:CH]).then_inc(copied, 1)
                act.wait_ge(copied, 2 * n_slabs + 1)
                act.dma_start(g.pT[n_slabs * SLAB:n_cols, HALO:HALO + T], out[0:rest, 0, :]).then_inc(stored0, 16)
            act.wait_ge(stored0, 16 * (n_slabs + 1 + (rest > 0)))
            act.wait_ge(stored1, 16 * (n_slabs + 1))

        if tails:
            @block.vector
            def _(dve):
                dve.sem_inc(tail_done, 2)

                def tail(u, turn, pair):
                    for n in range(2):
                        tile = pair * 4 + (2 * u + n)
                        if not isinstance(pair, int):
                            tile = dve.snap(tile)
                        dve.wait_ge(copied, turn * 2 + (n - 1))
                        nc.vector.tensor_copy(g.tails[:, ds(tile, 1), 0:TAIL].rearrange("p o c -> p (o c)"),
                                              out[:, n, TP - TAIL:TP])
                        nc.vector.tensor_copy(
                            g.tails[:, ds(tile, 1), TAIL:SEQS * TAIL].rearrange("p o (s c) -> p (o s) c", c=TAIL),
                            out[:, n, TP:T].rearrange("p (s t) -> p s t", t=LS)[:, :, LS - TAIL:LS]
                        ).then_inc(tail_done, 1)
                each_slab(dve, tail)


def multiply_down(nc, g, weights, kt, gate, name):
    with Phase(nc, name) as ph:
        w = ph.sb("w", [P, 2, KACT, P])
        tmp = ph.sb("tmp", [P, 2, NS * LS])
        acc = ph.ps("acc", [P, 2, 4, BANK])
        slab_free, w_in0, w_in1, acc_free, gated, added = ph.sems("slab_free w_in0 w_in1 acc_free gated added")
        w_in = (w_in0, w_in1)
        block = ph.block()
        src = weights.rearrange("(k p) n -> p k n", p=P)

        @block.sync
        def _(sp):
            with sp.Fori(0, KD // 2) as i:
                for u in range(2):
                    at, turn = sp.snap((2 * i + u) * P), sp.snap(2 * i + (u + 1))
                    sp.wait_ge(slab_free, turn)
                    sp.dma_start(w[:, u, 0:kt, :], src[:, :, ds(at, P)]).then_inc(w_in[u], 16)

        @block.tensor
        def _(pe):
            pe.sem_inc(slab_free, 2)
            with pe.Fori(0, KD // 2) as i:
                for u in range(2):
                    pe.wait_ge(w_in[u], i * 16 + 16)
                    pe.wait_ge(acc_free, 2 * i + (u + 1))
                    for k in range(kt):
                        for c in range(NCH):
                            ins = nc.tensor.matmul(acc[:, u, c, 0:CH], w[:, u, k, :],
                                                   g.act[:, k, c * CH:(c + 1) * CH],
                                                   start=(k == 0), stop=(k == kt - 1))
                    ins.then_inc(slab_free, 1)

        @block.vector
        def _(dve):
            dve.sem_inc(acc_free, 2)
            with dve.Fori(0, KD // 2) as i:
                for u in range(2):
                    n, turn = dve.snap(2 * i + u), dve.snap(2 * i + (u + 1))
                    dve.wait_ge(slab_free, 2 * i + (u + 3))
                    two = 2 * CH
                    for lo, hi, part, m in ((0, two, acc[:, u, 0:2, 0:CH], CH),
                                            (two, TP, acc[:, u, 2:3, 0:TP - two], TP - two)):
                        xs = g.xT[:, ds(n, 1), lo:hi].rearrange("p o (c n) -> p (o c) n", n=m)
                        nc.vector.scalar_tensor_tensor(xs, part, gate[:, ds(n, 1), 0:1].rearrange("p o s -> p (o s)"),
                                                       xs, ALU.mult, ALU.add)
                    gs = bc(gate[:, ds(n, 1), 1:SEQS].rearrange("p o s -> p (o s)"), 2, LS)
                    nc.vector.tensor_tensor(tmp[:, u, :].rearrange("p (s t) -> p s t", t=LS),
                                            acc[:, u, 2, TP - two:CH].rearrange("p (s t) -> p s t", t=LS),
                                            gs, ALU.mult).then_inc(gated, 1)
                    dve.wait_ge(gated, turn)
                    xs = g.xT[:, ds(n, 1), TP:T].rearrange("p o c -> p (o c)")
                    nc.vector.tensor_tensor(xs, xs, tmp[:, u, :], ALU.add).then_inc(added, 1)
                    dve.sem_inc(acc_free, 1)


def gate_up(nc, g, w_gate, w_up, first, n_slabs, name):
    with Phase(nc, name) as ph:
        w = ph.sb("w", [P, 2, KD, SLAB])
        sil = ph.sb("sil", [P, 2, T])
        acc = ph.ps("acc", [P, 2, 4, BANK])
        gate_free, up_free, gate_in, up_in, gate_done, up_done, sil_done, mul_done = ph.sems(
            "gate_free up_free gate_in up_in gate_done up_done sil_done mul_done")
        block = ph.block()
        kinds = ((gate_free, gate_in, gate_done, sil_done, w_gate), (up_free, up_in, up_done, mul_done, w_up))

        @block.sync
        def _(sp):
            with sp.Fori(0, n_slabs) as i:
                at, turn = sp.snap(i * SLAB + first * SLAB), sp.snap(i + 1)
                for kind, (free, w_in, _, _, src) in enumerate(kinds):
                    sp.wait_ge(free, turn)
                    sp.dma_start(w[:, kind, :, :], src.rearrange("(k p) n -> p k n", p=P)[:, :, ds(at, SLAB)]
                                 ).then_inc(w_in, 16)

        @block.tensor
        def _(pe):
            pe.sem_inc(gate_free, 1)
            pe.sem_inc(up_free, 1)
            with pe.Fori(0, n_slabs) as i:
                for n in range(2):
                    tile = pe.snap(2 * i + (n + 1))
                    for kind, (free, w_in, done, used, _) in enumerate(kinds):
                        if n == 0:
                            pe.wait_ge(w_in, i * 16 + 16)
                        pe.wait_ge(used, tile)
                        for k in range(KD):
                            for c in range(NCH):
                                ins = nc.tensor.matmul(acc[:, kind, c, 0:CH], w[:, kind, k, n * P:(n + 1) * P],
                                                       g.hT[:, k, c * CH:(c + 1) * CH],
                                                       start=(k == 0), stop=(k == KD - 1))
                        ins.then_inc(done, 1)
                        if n == 1:
                            pe.wait_ge(done, tile)
                            pe.sem_inc(free, 1)

        @block.scalar
        def _(act):
            act.sem_inc(sil_done, 1)
            with act.Fori(0, n_slabs) as i:
                for n in range(2):
                    act.wait_ge(gate_done, 2 * i + (n + 1))
                    act.wait_ge(mul_done, 2 * i + n)
                    nc.scalar.activation(sil[:, n, :].rearrange("p (c n) -> p c n", n=CH),
                                         acc[:, 0, 0:NCH, 0:CH], ACT.Silu).then_inc(sil_done, 1)

        @block.vector
        def _(dve):
            dve.sem_inc(mul_done, 1)
            with dve.Fori(0, n_slabs) as i:
                for n in range(2):
                    tile = dve.snap(2 * i + n)
                    dve.wait_ge(up_done, 2 * i + (n + 1))
                    dve.wait_ge(sil_done, 2 * i + (n + 2))
                    nc.vector.tensor_tensor(
                        g.act[:, ds(tile, 1), :].rearrange("p o (c n) -> p (o c) n", n=CH),
                        acc[:, 1, 0:NCH, 0:CH], sil[:, n, :].rearrange("p (c n) -> p c n", n=CH),
                        ALU.mult).then_inc(mul_done, 1)


def write_y(nc, g, y_prompt, y_sample):
    with Phase(nc, "out") as ph:
        rstd = ph.sb("rstd", [P, T])
        rows = ph.sb("rows", [P, 2, D])
        ss = ph.ps("ss", [P, NCH, BANK])
        pt = ph.ps("pt", [P, 2, 2, BANK])
        sems = ph.sems("squared summed mean_done inv_done rstd_done")
        scaled, turned, copied_a, copied_v, out0, out1 = ph.sems("scaled turned copied_a copied_v out0 out1")
        outs = (out0, out1)
        block = ph.block()
        scalar_steps, vector_steps = mean_square_steps(nc, g, block, ss, rstd, sems)
        yp = y_prompt.rearrange("o (t p) d -> (o t) p d", p=P)
        ys = y_sample.rearrange("b s d -> (b s) d")

        @block.scalar
        def _(act):
            scalar_steps(act)
            for t in range(NT):
                act.wait_ge(turned, t + 1)
                if t >= 2:
                    act.wait_ge(outs[t % 2], 16 * (t // 2))
                nc.scalar.copy(rows[:, t % 2, 0:512], pt[:, t % 2, 0, :]).then_inc(copied_a, 1)

        @block.tensor
        def _(pe):
            pe.wait_ge(scaled, KD)
            for t in range(NT):
                if t >= 2:
                    pe.wait_ge(copied_a, t - 1)
                    pe.wait_ge(copied_v, t - 1)
                for k in range(KD):
                    ins = nc.tensor.transpose(pt[:, t % 2, k // 4, (k % 4) * P:(k % 4 + 1) * P],
                                              g.hT[:, k, t * P:(t + 1) * P], g.ident[:, :])
                ins.then_inc(turned, 1)

        @block.vector
        def _(dve):
            vector_steps(dve)
            for k in range(KD):
                at = ROW_B["norm_out_w"] + k
                nc.vector.scalar_tensor_tensor(g.hT[:, k, :], g.xT[:, k, :], g.colB[:, at:at + 1], rstd[:, :],
                                               ALU.mult, ALU.mult).then_inc(scaled, 1)
            for t in range(NT):
                dve.wait_ge(turned, t + 1)
                if t >= 2:
                    dve.wait_ge(outs[t % 2], 16 * (t // 2))
                nc.vector.tensor_copy(rows[:, t % 2, 512:D], pt[:, t % 2, 1, :]).then_inc(copied_v, 1)

        @block.sync
        def _(sp):
            for t in range(NT):
                sp.wait_ge(copied_a, t + 1)
                sp.wait_ge(copied_v, t + 1)
                sp.dma_start(yp[t] if t < NTP else ys, rows[:, t % 2, :]).then_inc(outs[t % 2], 16)
            sp.wait_ge(out0, 16 * 5)
            sp.wait_ge(out1, 16 * 4)


def new_shift_conv(nc, g, shift_p, conv_p, shift_s, conv_s):
    with Phase(nc, "tails") as ph:
        shift_rows = ph.sb("shift_rows", [SEQS, A_COLS])
        conv_rows = ph.sb("conv_rows", [SEQS * TAIL, XBC])
        pt = ph.ps("pt", [P, 8, BANK])
        turned, copied, stored = ph.sems("turned copied stored")
        block = ph.block()

        @block.tensor
        def _(pe):
            for j in range(NA):
                last = g.tails[:, j, :].rearrange("p (s c) -> p s c", c=TAIL)[:, :, TAIL - 1]
                nc.tensor.transpose(pt[0:SEQS, j // 4, (j % 4) * P:(j % 4 + 1) * P], last, g.ident[:, :])
            for j in range(NXBC):
                ins = nc.tensor.transpose(pt[0:SEQS * TAIL, 4 + j // 4, (j % 4) * P:(j % 4 + 1) * P],
                                          g.tails[:, JX + j, :], g.ident[:, :])
            ins.then_inc(turned, 1)

        @block.vector
        def _(dve):
            dve.wait_ge(turned, 1)
            for b in range(4):
                n = min(BANK, A_COLS - b * BANK)
                nc.vector.tensor_copy(shift_rows[:, b * BANK:b * BANK + n], pt[0:SEQS, b, 0:n])
            for b in range(3):
                ins = nc.vector.tensor_copy(conv_rows[:, b * BANK:(b + 1) * BANK], pt[0:SEQS * TAIL, 4 + b, :])
            ins.then_inc(copied, 1)

        @block.sync
        def _(sp):
            sp.wait_ge(copied, 1)
            sp.dma_start(shift_p[0], shift_rows[0:1, :]).then_inc(stored, 16)
            sp.dma_start(shift_s.rearrange("b l n -> (b l) n"), shift_rows[1:SEQS, :]).then_inc(stored, 16)
            sp.dma_start(conv_p.rearrange("b l w n -> (b l w) n"), conv_rows[0:TAIL, :]).then_inc(stored, 16)
            sp.dma_start(conv_s.rearrange("b l w n -> (b l w) n"), conv_rows[TAIL:SEQS * TAIL, :]).then_inc(stored, 16)
            sp.wait_ge(stored, 64)


class Turn:

    def __init__(self, eng, t):
        self.eng, self.t, self.kept = eng, t, {}

    def at(self, n, k=None):
        k = n if k is None else k
        if isinstance(self.t, int):
            return self.t * n + k
        if n > 8:
            return self.t * n + k
        if (n, k) not in self.kept:
            self.kept[n, k] = self.eng.snap(self.t * n + k)
        return self.kept[n, k]

    def wait(self, sem, n=1, k=None):
        self.eng.wait_ge(sem, self.at(n, k))

    def col(self, width, base=0):
        v = self.t * width + base
        return v if isinstance(v, int) else self.eng.snap(v)


def each_tile(eng, body):
    with eng.Fori(0, NTP) as t:
        body(Turn(eng, t), False)
    body(Turn(eng, NTP), True)


def held(tn, waited, sem, n=1, k=None):
    tn.wait(sem, n, k)
    tn.eng.sem_inc(waited, 1)


HA, HDA = 8, 64
PAIRS = HA // 2
GRP = 2
HG = HA // GRP
JG_ = PAIRS // GRP


def rwkv_states_in(nc, g, A, S):
    with Phase(nc, "rw_in") as ph:
        rows = ph.sb("rows", [HDA, NS, HA * HDA])
        pt = ph.ps("pt", [P, 8, BANK])
        loaded, turned = ph.sems("loaded turned")
        block = ph.block()

        @block.sync
        def _(sp):
            for b in range(NS):
                sp.dma_start(rows[:, b, :].rearrange("v (h k) -> v h k", k=HDA),
                             A["state_rwkv"][b, 0].rearrange("h v k -> v h k")).then_inc(loaded, 16)

        @block.tensor
        def _(pe):
            pe.wait_ge(loaded, 16 * NS)
            for b in range(NS):
                for j in range(PAIRS):
                    ins = nc.tensor.transpose(pt[:, b, j * HDA:(j + 1) * HDA], rows[:, b, j * P:(j + 1) * P],
                                              g.ident[0:HDA, 0:HDA])
            ins.then_inc(turned, 1)

        @block.vector
        def _(dve):
            dve.wait_ge(turned, 1)
            nc.vector.tensor_copy(S[:, 0:NS, :, :].rearrange("p b j v -> p b (j v)"), pt[:, :, 0:PAIRS * HDA])


def rwkv_states_out(nc, g, S, dsts, name):
    n = len(dsts)
    with Phase(nc, name) as ph:
        rows = ph.sb("rows", [HDA, n, HA * HDA])
        pt = ph.ps("pt", [HDA, n, BANK])
        turned, copied, stored = ph.sems("turned copied stored")
        block = ph.block()

        @block.tensor
        def _(pe):
            for b in range(n):
                for j in range(PAIRS):
                    ins = nc.tensor.transpose(pt[:, b, j * P:(j + 1) * P], S[:, b, j, :], g.ident[:, :])
            ins.then_inc(turned, 1)

        @block.vector
        def _(dve):
            dve.wait_ge(turned, 1)
            nc.vector.tensor_copy(rows[:, :, :], pt[:, :, :]).then_inc(copied, 1)

        @block.sync
        def _(sp):
            sp.wait_ge(copied, 1)
            for b, dst in enumerate(dsts):
                sp.dma_start(dst.rearrange("h v k -> v h k"),
                             rows[:, b, :].rearrange("v (h k) -> v h k", k=HDA)).then_inc(stored, 16)
            sp.wait_ge(stored, 16 * n)


def rwkv(nc, g, A, out_p, out_s):
    with ExitStack() as outer:
        S = outer.enter_context(nc.sbuf_tensor("rw_S", [P, NB + 1, PAIRS, HDA], F32))
        S_samples = outer.enter_context(nc.sbuf_tensor("rw_S_samples", [P, NS, PAIRS, HDA], F32))
        rwkv_states_in(nc, g, A, S_samples)
        rwkv_tiles(nc, g, A, S, S_samples)
        rwkv_states_out(nc, g, S[:, NB:NB + 1, :, :], [out_p[0, 0]], "rw_outp")
        rwkv_states_out(nc, g, S_samples, [out_s[b, 0] for b in range(NS)], "rw_outs")


def rwkv_tiles(nc, g, A, S, S_samples):
    with Phase(nc, "rwkv") as ph:
        W4 = PAIRS * P

        def arr(name):
            return ph.sb(name, [P, PAIRS, P])
        raw = ph.sb("raw", [P, NA, 1 + P])
        diff = ph.sb("diff", [P, NA, P])
        mixed = ph.sb("mixed", [P, NA, P])
        w2 = ph.sb("w2", [P, WA])
        g2 = ph.sb("g2", [P, WA])
        one_minus_ka = ph.sb("one_minus_ka", [P, PAIRS])
        sig, a_, gl, c_, cprev, dinv, dcum = map(arr, "sig a gl c cprev dinv dcum".split())
        kmod, ba, bt, kt, kend, rk = map(arr, "kmod ba bt kt kend rk".split())
        crem = arr("crem")
        AR = ph.sb("AR", [P, PAIRS, 2, P])
        kk, kinv, kk2 = diff[:, 0:4, :], diff[:, 4:8, :], diff[:, 8:12, :]
        tanh_in = ph.sb("tanh_in", [HDA, P])
        sig_in = ph.sb("sig_in", [P, P])
        X = ph.sb("X", [P, HA, P])
        v_tok, b_tok, k_tok = (ph.sb(n, [P, HA, HDA]) for n in ("v_tok", "b_tok", "k_tok"))
        MT = arr("MT")
        Sd = ph.sb("Sd", [P, 2, JG_, HDA])
        room = g.act[:, PAIRS:KACT, :].rearrange("p a b -> p (a b)")
        used = [0]

        def carve(*shape):
            n = math.prod(shape)
            v = room[:, used[0]:used[0] + n]
            used[0] += n
            names = " ".join(f"d{i}" for i in range(len(shape)))
            return v.rearrange(f"p ({names}) -> p {names}", **{f"d{i}": s for i, s in enumerate(shape)})
        b_msk, k_msk = carve(HG, NB, HDA), carve(HG, NB, HDA)
        GM = carve(HG, 4, P)
        AM = carve(HG, P)
        pw = carve(HG, 4, P)
        GT = ph.sb("GT", [P, JG_, NB, HDA])
        bank = [ph.ps(f"bank{i}", [P, BANK]) for i in range(8)]
        (loaded, weights_in, raw_free, diff_done, mixed_done, lora_in, lora_done, sig_done, gates_done, kk_done,
         kk2_done, ss_done, ssinv1, ssinv2, kinv_done, kkn_done, c_done, cprev_done, crem_done, exps_done, am1, am2,
         kmod_done, ba_done, rk1, rk_done, tilde_done, kend_done, T_done, tok_done, msk_done, msk_b) = ph.sems(
            "loaded weights_in raw_free diff_done mixed_done lora_in lora_done sig_done gates_done kk_done "
            "kk2_done ss_done ssinv1 ssinv2 kinv_done kkn_done c_done cprev_done crem_done exps_done am1 am2 "
            "kmod_done ba_done rk1 rk_done tilde_done kend_done T_done tok_done msk_done msk_b")
        (gram_done, gm_done, S1_done, S2_done, S3_done, S4_done, S5_done, pw1, pw2, pw3, x1, x2, x3, x4, x5,
         M_done, MT_done, GT_mm, GT_done, state_in, chain_mm, decayed, chained, O_done, o_done, mean_done, oc_done,
         sq_done, var_done, var1, var2, rs_done, normed, affine_done, bonus_done, bonus_mul, summed_, out_done,
         saved, waited) = ph.sems(
            "gram_done gm_done S1_done S2_done S3_done S4_done S5_done pw1 pw2 pw3 x1 x2 x3 x4 x5 "
            "M_done MT_done GT_mm GT_done state_in chain_mm decayed chained O_done o_done mean_done oc_done "
            "sq_done var_done var1 var2 rs_done normed affine_done bonus_done bonus_mul summed out_done "
            "saved waited")
        block = ph.block()
        r_, k_, v_ = mixed[:, JR:JR + 4, :], mixed[:, JK:JK + 4, :], mixed[:, JV:JV + 4, :]
        col = lambda name, n=PAIRS: g.colB[:, ROW_B[name]:ROW_B[name] + n]
        flat = lambda ap: ap.rearrange("p j c -> p (j c)")
        blocks = lambda ap: ap.rearrange("p j (b c) -> p (j b) c", c=BLK)
        o_, oc, sq = bt, kt, ba

        @block.sync
        def _(sp):
            sp.dma_start(w2[0:64, :], A["w2"][0]).then_inc(weights_in, 16)
            sp.dma_start(w2[64:128, :], A["a2"][0]).then_inc(weights_in, 16)
            sp.dma_start(g2[:, :], A["g2"][0]).then_inc(weights_in, 16)
            src = g.pT[0:NA * P, :].rearrange("(j p) c -> p j c", p=P)

            def load(tn, sample):
                at = tn.col(P, HALO - 1)
                tn.wait(raw_free)
                sp.dma_start(raw[:, :, :], src[:, :, ds(at, P + 1)]).then_inc(loaded, 16)
            each_tile(sp, load)

        @block.scalar
        def _(act):
            def tile(tn, sample):
                at = tn.col(P)
                tn.wait(mixed_done)
                nc.scalar.activation(tanh_in[:, :], mixed[0:64, JWA, :], ACT.Tanh)
                nc.scalar.activation(sig_in[:, :], mixed[:, JG, :], ACT.Sigmoid).then_inc(lora_in, 1)
                tn.wait(lora_done)
                for j in range(PAIRS):
                    ins = nc.scalar.activation(sig[:, j, :], bank[0][:, j * P:(j + 1) * P], ACT.Sigmoid,
                                               bias=col("w0")[:, j:j + 1])
                ins.then_inc(sig_done, 1)
                for j in range(PAIRS):
                    nc.scalar.activation(a_[:, j, :], bank[1][:, j * P:(j + 1) * P], ACT.Sigmoid,
                                         bias=col("a0")[:, j:j + 1])
                nc.scalar.copy(flat(gl[:, :, :]), bank[2][:, :]).then_inc(gates_done, 1)
                tn.wait(ssinv2)
                nc.scalar.activation(kinv, kinv, ACT.Sqrt).then_inc(kinv_done, 1)
                tn.wait(crem_done)
                tn.wait(cprev_done)
                nc.scalar.activation(dcum[:, :, :], c_[:, :, :], ACT.Exp, scale=-KAPPA)
                nc.scalar.activation(dinv[:, :, :], c_[:, :, :], ACT.Exp, scale=KAPPA)
                nc.scalar.activation(cprev[:, :, :], cprev[:, :, :], ACT.Exp, scale=-KAPPA)
                nc.scalar.activation(crem[:, :, :], crem[:, :, :], ACT.Exp, scale=-KAPPA).then_inc(exps_done, 1)
                tn.wait(T_done)
                nc.scalar.copy(X[:, :, 0:HDA], bank[4][:, :].rearrange("p (h k) -> p h k", k=HDA))
                nc.scalar.copy(v_tok[:, :, :].rearrange("p h k -> p (h k)"), bank[5][:, :])
                nc.scalar.copy(b_tok[:, :, :].rearrange("p h k -> p (h k)"), bank[6][:, :])
                nc.scalar.copy(k_tok[:, :, :].rearrange("p h k -> p (h k)"), bank[7][:, :]).then_inc(tok_done, 1)
                for q in range(GRP):
                    for stage, (mm, out, dst) in enumerate(((S1_done, pw1, (0, 2)), (S2_done, pw2, (2, 4)),
                                                            (S3_done, pw3, (1, 2)))):
                        for hh in range(HG):
                            h = q * HG + hh
                            tn.wait(mm, 8, h + 1)
                            n = (dst[1] - dst[0]) * P
                            nc.scalar.copy(pw[:, hh, dst[0]:dst[1], :].rearrange("p a c -> p (a c)"),
                                           bank[4 + h % 2][:, 0:n]).then_inc(out, 1)
                    for jj in range(JG_):
                        tn.wait(GT_mm, 4, q * JG_ + jj + 1)
                        nc.scalar.copy(GT[:, jj, :, :].rearrange("p b k -> p (b k)"),
                                       bank[1 + jj][:, :]).then_inc(GT_done, 1)
                tn.wait(O_done, 2)
                nc.scalar.copy(flat(o_[:, :, :]), bank[3][:, :]).then_inc(o_done, 1)
                tn.wait(var2)
                nc.scalar.activation(sq[:, :, :], sq[:, :, :], ACT.Sqrt).then_inc(rs_done, 1)
                tn.wait(normed)
                for j in range(PAIRS):
                    ins = nc.scalar.activation(oc[:, j, :], oc[:, j, :], ACT.Identity,
                                               bias=col("lnx_b")[:, j:j + 1], scale=col("lnx_w")[:, j:j + 1])
                ins.then_inc(affine_done, 1)
            each_tile(act, tile)

        @block.gpsimd
        def _(pool):
            tt = nc.gpsimd.tensor_tensor
            nc.gpsimd.tensor_scalar(one_minus_ka[:, :], col("k_a"), -1.0, 1.0, ALU.mult, ALU.add).then_inc(am1, 1)
            pool.wait_ge(am1, 1)
            pool.sem_inc(am2, 1)

            def tile(tn, sample):
                tn.wait(sig_done)
                tn.wait(c_done)
                tt(cprev[:, :, :], c_[:, :, :], sig[:, :, :], ALU.subtract).then_inc(cprev_done, 1)
                tt(blocks(crem[:, :, :]), blocks(c_[:, :, :])[:, :, BLK - 1:BLK].to_broadcast([P, PAIRS * NB, BLK]),
                   blocks(c_[:, :, :]), ALU.subtract).then_inc(crem_done, 1)
                tn.wait(gates_done)
                tt(kmod[:, :, :], a_[:, :, :], bc(col("k_a"), 2, P), ALU.mult).then_inc(am1, 1)
                tn.wait(am1, 1, 2)
                tt(kmod[:, :, :], kmod[:, :, :], bc(one_minus_ka[:, :], 2, P), ALU.add).then_inc(am2, 1)
                tn.wait(am2, 1, 2)
                tt(kmod[:, :, :], kmod[:, :, :], k_, ALU.mult).then_inc(kmod_done, 1)
                tn.wait(kkn_done)
                tt(ba[:, :, :], kk, a_[:, :, :], ALU.mult).then_inc(ba_done, 1)
                tn.wait(exps_done)
                tn.wait(ba_done)
                tn.wait(kmod_done)
                tt(kend[:, :, :], kmod[:, :, :], crem[:, :, :], ALU.mult).then_inc(kend_done, 1)
                tn.wait(kend_done, 2, 1)
                tt(crem[:, :, :], ba[:, :, :], crem[:, :, :], ALU.mult).then_inc(kend_done, 1)
                tt(rk[:, :, :], r_, bc(col("r_k"), 2, P), ALU.mult).then_inc(rk1, 1)
                tn.wait(rk1)
                tt(rk[:, :, :], rk[:, :, :], kmod[:, :, :], ALU.mult).then_inc(rk_done, 1)
                tn.wait(tok_done)
                for q in range(GRP):
                    if q:
                        tn.wait(O_done, 2, 1)
                    for dst, tok in ((b_msk, b_tok), (k_msk, k_tok)):
                        ins = tt(dst, bc(tok[:, q * HG:(q + 1) * HG, :], 2, NB),
                                 bc(bc(g.blockmask[:, :], 1, HG), 3, HDA), ALU.mult)
                    ins.then_inc(msk_done, 1)
            each_tile(pool, tile)

        @block.vector
        def _(dve):
            tt, stt = nc.vector.tensor_tensor, nc.vector.scalar_tensor_tensor
            dve.sem_inc(raw_free, 1)
            nc.vector.memset(S[:, NB, :, :], 0.0).then_inc(saved, 1)

            def tile(tn, sample):
                at = tn.col(P)
                dve.wait_ge(loaded, tn.t * 16 + 16)
                now, before = raw[:, :, 1:1 + P], raw[:, :, 0:P]
                tt(diff[:, :, :], before, now, ALU.subtract).then_inc(diff_done, 1)
                tn.wait(diff_done)
                if sample:
                    first = lambda ap: ap.rearrange("p j (b c) -> p j b c", c=BLK)[:, :, :, 0]
                    tt(first(diff[:, :, :]), g.shiftT[:, :, :], first(now), ALU.subtract).then_inc(diff_done, 1)
                    dve.wait_ge(diff_done, NT + 1)
                for j in range(NA):
                    mu = g.colB[:, ROW_B["mu_a"] + j:ROW_B["mu_a"] + j + 1]
                    ins = stt(mixed[:, j, :], diff[:, j, :], mu, now[:, j, :], ALU.mult, ALU.add)
                ins.then_inc(mixed_done, 1)
                tn.wait(mixed_done)
                dve.sem_inc(raw_free, 1)
                tt(kk, k_, bc(col("k_k"), 2, P), ALU.mult).then_inc(kk_done, 1)
                tn.wait(kk_done)
                tt(kk2, kk, kk, ALU.mult).then_inc(kk2_done, 1)
                tn.wait(ss_done)
                nc.vector.tensor_scalar(flat(kinv), bank[3][:, :], 1e-24, None, ALU.max).then_inc(ssinv1, 1)
                tn.wait(ssinv1)
                nc.vector.reciprocal(kinv, kinv).then_inc(ssinv2, 1)
                tn.wait(sig_done)
                nc.vector.tensor_tensor_scan(flat(c_[:, :, :]), g.reset[:, :], flat(sig[:, :, :]), 0.0,
                                             ALU.mult, ALU.add).then_inc(c_done, 1)
                tn.wait(kinv_done)
                tt(kk, kk, kinv, ALU.mult).then_inc(kkn_done, 1)
                tn.wait(kkn_done)
                tn.wait(exps_done)
                stt(AR[:, :, 0, :], kk, -1.0, cprev[:, :, :], ALU.mult, ALU.mult)
                tt(AR[:, :, 1, :], r_, dcum[:, :, :], ALU.mult)
                tn.wait(ba_done)
                tt(bt[:, :, :], ba[:, :, :], dinv[:, :, :], ALU.mult)
                tn.wait(kmod_done)
                tt(kt[:, :, :], kmod[:, :, :], dinv[:, :, :], ALU.mult).then_inc(tilde_done, 1)
                if sample:
                    nc.vector.tensor_copy(S[:, 0:NS, :, :].rearrange("p b j v -> p (b j v)"),
                                          S_samples[:, :, :, :].rearrange("p b j v -> p (b j v)")).then_inc(state_in, 1)
                else:
                    tn.wait(saved)
                    nc.vector.tensor_copy(S[:, 0, :, :], S[:, NB, :, :]).then_inc(state_in, 1)
                tn.wait(state_in)
                for q in range(GRP):
                    for hh in range(HG):
                        h = q * HG + hh
                        tn.wait(gram_done, 8, h + 1)
                        tt(GM[:, hh, :, :].rearrange("p a c -> p (a c)"), bank[h % 2][:, :],
                           g.gram_mask[:, :, :, :].rearrange("p a b c -> p (a b c)"), ALU.mult)
                        tt(AM[:, hh, :], bank[2 + h % 2][:, 2 * P:3 * P], g.after[:, :], ALU.mult).then_inc(gm_done, 1)
                    for stage, (mm, out) in enumerate(((S1_done, x1), (S2_done, x2), (S3_done, x3), (S4_done, x4),
                                                       (S5_done, x5))):
                        for hh in range(HG):
                            h = q * HG + hh
                            tn.wait(mm, 8, h + 1)
                            if stage == 0:
                                nc.vector.tensor_copy(X[:, h, HDA:P], bank[6 + h % 2][:, 0:HDA]).then_inc(out, 1)
                            else:
                                tt(X[:, h, :], X[:, h, :], bank[6 + h % 2][:, 0:P], ALU.add).then_inc(out, 1)
                    js = slice(q * JG_, (q + 1) * JG_)
                    tn.wait(M_done, 2, q + 1)
                    tt(MT[:, js, :], bank[0][:, 0:JG_ * P].rearrange("p (j c) -> p j c", c=P), AR[:, js, 1, :],
                       ALU.add).then_inc(MT_done, 1)
                    dend = dcum[:, js, :].rearrange("p j (b c) -> p j b c", c=BLK)
                    for b in range(NB):
                        tt(Sd[:, b % 2, :, :], S[:, b, js, :], bc(dend[:, :, b, BLK - 1], 2, HDA),
                           ALU.mult).then_inc(decayed, 1)
                        tn.wait(decayed, 16, q * NB + b + 1)
                        tn.wait(chain_mm, 16, q * NB + b + 1)
                        dst = S_samples[:, b, js, :] if sample else S[:, b + 1, js, :]
                        tt(dst, Sd[:, b % 2, :, :],
                           bank[6 + b % 2][:, 0:JG_ * HDA].rearrange("p (j v) -> p j v", v=HDA),
                           ALU.add).then_inc(chained, 1)
                        if not sample:
                            tn.wait(chained, 16, q * NB + b + 1)
                if not sample:
                    dve.sem_inc(saved, 1)
                tn.wait(mean_done)
                stt(flat(oc[:, :, :]), bank[5][:, :], -1.0 / HDA, flat(o_[:, :, :]), ALU.mult, ALU.add
                    ).then_inc(oc_done, 1)
                tn.wait(oc_done)
                tt(sq[:, :, :], oc[:, :, :], oc[:, :, :], ALU.mult).then_inc(sq_done, 1)
                tn.wait(var_done)
                nc.vector.tensor_scalar(flat(sq[:, :, :]), bank[0][:, :], 1.0 / HDA, LNX_EPS, ALU.mult, ALU.add
                                        ).then_inc(var1, 1)
                tn.wait(var1)
                nc.vector.reciprocal(sq[:, :, :], sq[:, :, :]).then_inc(var2, 1)
                tn.wait(rs_done)
                tt(oc[:, :, :], oc[:, :, :], sq[:, :, :], ALU.mult).then_inc(normed, 1)
                tt(flat(o_[:, :, :]), bank[4][:, :], flat(v_), ALU.mult).then_inc(bonus_mul, 1)
                tn.wait(bonus_mul)
                tn.wait(affine_done)
                tt(oc[:, :, :], oc[:, :, :], o_[:, :, :], ALU.add).then_inc(summed_, 1)
                tn.wait(summed_)
                tt(g.act[:, 0:PAIRS, ds(at, P)], oc[:, :, :], gl[:, :, :], ALU.mult).then_inc(out_done, 1)
                tn.wait(out_done)
            each_tile(dve, tile)

        @block.tensor
        def _(pe):
            mm = nc.tensor.matmul
            pe.wait_ge(weights_in, 48)

            def tile(tn, sample):
                tn.wait(lora_in)
                for j in range(PAIRS):
                    js = slice(j * P, (j + 1) * P)
                    mm(bank[0][:, js], w2[0:64, js], tanh_in[:, :], start=True, stop=True)
                    mm(bank[1][:, js], w2[64:128, js], mixed[64:128, JWA, :], start=True, stop=True)
                    ins = mm(bank[2][:, js], g2[:, js], sig_in[:, :], start=True, stop=True)
                ins.then_inc(lora_done, 1)
                tn.wait(kk2_done)
                mm(bank[3][:, :], g.ones64[:, :], flat(kk2), start=True, stop=True).then_inc(ss_done, 1)
                tn.wait(tilde_done)
                tn.wait(kend_done, 2)
                for j in range(PAIRS):
                    js = slice(j * P, (j + 1) * P)
                    for i, x in enumerate((AR[:, j, 0, :], v_[:, j, :], crem[:, j, :], kend[:, j, :])):
                        ins = nc.tensor.transpose(bank[4 + i][:, js], x, g.ident[:, :])
                ins.then_inc(T_done, 1)
                for q in range(GRP):
                    for hh in range(HG):
                        h = q * HG + hh
                        j, part = h // 2, slice(64 * (h % 2), 64 * (h % 2) + 64)
                        if hh >= 2:
                            tn.wait(gm_done, 8, h - 1)
                        rhs = AR[part, j, :, :].rearrange("p a c -> p (a c)")
                        mm(bank[h % 2][:, 0:2 * P], bt[part, j, :], rhs, start=True, stop=True)
                        mm(bank[h % 2][:, 2 * P:4 * P], kt[part, j, :], rhs, start=True, stop=True)
                        mm(bank[2 + h % 2][:, 2 * P:3 * P], AR[part, j, 0, :], bt[part, j, :], start=True, stop=True
                           ).then_inc(gram_done, 1)
                    if q == 0:
                        tn.wait(tok_done)
                    stages = ((S1_done, None, gm_done), (S2_done, pw1, x1), (S3_done, pw2, x2),
                              (S4_done, pw3, x3), (S5_done, None, x4))
                    for stage, (done, powers, xs) in enumerate(stages):
                        for hh in range(HG):
                            h = q * HG + hh
                            if hh < 2 and stage:
                                tn.wait(xs, 8, (q + 1) * HG)
                                if stage < 4:
                                    tn.wait((None, pw1, pw2, pw3)[stage], 8, (q + 1) * HG)
                            else:
                                tn.wait(xs, 8, h + 1)
                                if powers is not None:
                                    tn.wait(powers, 8, h + 1)
                            if hh >= 2:
                                tn.wait((x1, x2, x3, x4, x5)[stage], 8, h - 1)
                                if stage < 3:
                                    tn.wait((pw1, pw2, pw3)[stage], 8, h - 1)
                            bp, bx = bank[4 + h % 2], bank[6 + h % 2]
                            AT, AakT, A_ = GM[:, hh, 0, :], GM[:, hh, 2, :], AM[:, hh, :]
                            A2T, A2, A4T, A4 = (pw[:, hh, i, :] for i in range(4))
                            A8T = A2
                            if stage == 0:
                                mm(bp[:, 0:P], A_, AT, start=True, stop=True)
                                mm(bp[:, P:2 * P], AT, A_, start=True, stop=True)
                                ins = mm(bx[:, 0:HDA], AakT, v_tok[:, h, :], start=True, stop=True)
                            else:
                                if stage == 1:
                                    mm(bp[:, 0:P], A2, A2T, start=True, stop=True)
                                    mm(bp[:, P:2 * P], A2T, A2, start=True, stop=True)
                                if stage == 2:
                                    mm(bp[:, 0:P], A4, A4T, start=True, stop=True)
                                ins = mm(bx[:, 0:P], (None, AT, A2T, A4T, A8T)[stage], X[:, h, :],
                                         start=True, stop=True)
                            ins.then_inc(done, 1)
                    tn.wait(x5, 8, (q + 1) * HG)
                    tn.wait(msk_done, 2, q + 1)
                    for hh in range(HG):
                        h = q * HG + hh
                        jj, part = hh // 2, slice(64 * (h % 2), 64 * (h % 2) + 64)
                        ins = mm(bank[0][part, jj * P:(jj + 1) * P], X[:, h, 0:HDA], GM[:, hh, 1, :],
                                 start=True, stop=True)
                    ins.then_inc(M_done, 1)
                    for hh in range(HG):
                        h = q * HG + hh
                        jj, part = hh // 2, slice(64 * (h % 2), 64 * (h % 2) + 64)
                        ins = mm(bank[1 + jj][part, :], X[:, h, 0:HDA],
                                 b_msk[:, hh, :, :].rearrange("p b k -> p (b k)"), start=True, stop=True)
                        if hh % 2:
                            ins.then_inc(GT_mm, 1)
                    if q == 0:
                        tn.wait(state_in)
                    tn.wait(GT_done, 4, (q + 1) * JG_)
                    for b in range(NB):
                        if b:
                            if sample:
                                if b >= 2:
                                    tn.wait(chained, 16, q * NB + b - 1)
                            else:
                                held(tn, waited, chained, 16, q * NB + b)
                        for hh in range(HG):
                            h = q * HG + hh
                            jj, part = hh // 2, slice(64 * (h % 2), 64 * (h % 2) + 64)
                            out = bank[6 + b % 2][part, jj * HDA:(jj + 1) * HDA]
                            mm(out, k_msk[:, hh, b, :], v_tok[:, h, :], start=True, stop=False)
                            mm(out, b_msk[:, hh, b, :], X[:, h, HDA:P], start=False, stop=False)
                            ins = mm(out, GT[part, jj, b, :], S[part, b, h // 2, :], start=False, stop=True)
                        ins.then_inc(chain_mm, 1)
                    tn.wait(MT_done, 2, q + 1)
                    for hh in range(HG):
                        h = q * HG + hh
                        j, part = h // 2, slice(64 * (h % 2), 64 * (h % 2) + 64)
                        out = bank[3][part, j * P:(j + 1) * P]
                        mm(out, X[:, h, HDA:P], GM[:, hh, 1, :], start=True, stop=False)
                        mm(out, v_tok[:, h, :], GM[:, hh, 3, :], start=False, stop=False)
                        for b in range(NB):
                            ins = mm(out[:, b * BLK:(b + 1) * BLK], S[part, b, j, :],
                                     MT[part, j, b * BLK:(b + 1) * BLK], start=False, stop=(b == NB - 1))
                    ins.then_inc(O_done, 1)
                tn.wait(rk_done)
                mm(bank[4][:, :], g.ones64[:, :], flat(rk[:, :, :]), start=True, stop=True).then_inc(bonus_done, 1)
                tn.wait(o_done)
                mm(bank[5][:, :], g.ones64[:, :], flat(o_[:, :, :]), start=True, stop=True).then_inc(mean_done, 1)
                tn.wait(sq_done)
                mm(bank[0][:, :], g.ones64[:, :], flat(sq[:, :, :]), start=True, stop=True).then_inc(var_done, 1)
            each_tile(pe, tile)


HDB, NBS = 64, 128
WB = HB * HDB
KB = WB // P
GH = HB // 2


def ssm_states_in(nc, g, A, S):
    with Phase(nc, "ssm_in") as ph:
        rows = ph.sb("rows", [P, 2, KB, NBS])
        pt = ph.ps("pt", [P, 2, 2, BANK])
        in0, in1, turned, copied = ph.sems("in0 in1 turned copied")
        loaded = (in0, in1)
        block = ph.block()

        @block.sync
        def _(sp):
            for b in range(NS):
                if b >= 2:
                    sp.wait_ge(turned, b - 1)
                sp.dma_start(rows[:, b % 2, :, :], A["state_ssm"][b, 0].rearrange("(j h) p n -> (h p) j n", h=2)
                             ).then_inc(loaded[b % 2], 16)

        @block.tensor
        def _(pe):
            for b in range(NS):
                pe.wait_ge(loaded[b % 2], 16 * (b // 2 + 1))
                if b >= 2:
                    pe.wait_ge(copied, b - 1)
                for j in range(KB):
                    ins = nc.tensor.transpose(pt[:, b % 2, j // 4, (j % 4) * P:(j % 4 + 1) * P],
                                              rows[:, b % 2, j, :], g.ident[:, :])
                ins.then_inc(turned, 1)

        @block.vector
        def _(dve):
            for b in range(NS):
                dve.wait_ge(turned, b + 1)
                nc.vector.tensor_copy(S[:, b, :].rearrange("p (a c) -> p a c", c=BANK), pt[:, b % 2, :, :]
                                      ).then_inc(copied, 1)


def ssm_states_out(nc, g, S, dsts, name):
    with Phase(nc, name) as ph:
        rows = ph.sb("rows", [P, 2, KB, NBS])
        pt = ph.ps("pt", [P, 2, 2, BANK])
        turned, copied, out0, out1 = ph.sems("turned copied out0 out1")
        stored = (out0, out1)
        block = ph.block()

        @block.tensor
        def _(pe):
            for b in range(len(dsts)):
                if b >= 2:
                    pe.wait_ge(copied, b - 1)
                for j in range(KB):
                    ins = nc.tensor.transpose(pt[:, b % 2, j // 4, (j % 4) * P:(j % 4 + 1) * P],
                                              S[:, b, j * P:(j + 1) * P], g.ident[:, :])
                ins.then_inc(turned, 1)

        @block.vector
        def _(dve):
            for b in range(len(dsts)):
                dve.wait_ge(turned, b + 1)
                if b >= 2:
                    dve.wait_ge(stored[b % 2], 16 * (b // 2))
                nc.vector.tensor_copy(rows[:, b % 2, :, :].rearrange("p (a j) n -> p a (j n)", a=2),
                                      pt[:, b % 2, :, :]).then_inc(copied, 1)

        @block.sync
        def _(sp):
            for b, dst in enumerate(dsts):
                sp.wait_ge(copied, b + 1)
                sp.dma_start(dst.rearrange("(j h) p n -> (h p) j n", h=2), rows[:, b % 2, :, :]
                             ).then_inc(stored[b % 2], 16)
            for u in range(min(2, len(dsts))):
                sp.wait_ge(stored[u], 16 * ((len(dsts) + 1 - u) // 2))


def mamba(nc, g, A, out_p, out_s):
    with ExitStack() as outer:
        S = outer.enter_context(nc.sbuf_tensor("mb_S", [P, 1, WB], F32))
        S_samples = outer.enter_context(nc.sbuf_tensor("mb_S_samples", [P, NS, WB], F32))
        ssm_states_in(nc, g, A, S_samples)
        mamba_tiles(nc, g, A, S, S_samples)
        ssm_states_out(nc, g, S, [out_p[0, 0]], "ssm_outp")
        ssm_states_out(nc, g, S_samples, [out_s[b, 0] for b in range(NS)], "ssm_outs")


def mamba_tiles(nc, g, A, S, S_samples):
    with Phase(nc, "mamba") as ph:
        raw = ph.sb("raw", [P, NXBC, NB * (BLK + 3)])
        zt = ph.sb("zt", [P, KB, P])
        xc = ph.sb("xc", [P, NXBC, P])
        dt_raw = ph.sb("dt_raw", [HB, P])
        dt_y, dt_e = ph.sb("dt_y", [HB, P]), ph.sb("dt_e", [HB, P])
        dtla = ph.sb("dtla", [HB, 2, P])
        exp_a = ph.sb("exp_a", [HB, 1])
        dtla_tok = ph.sb("dtla_tok", [P, 2, HB])
        RL = ph.sb("RL", [P, HB, P])
        att = ph.sb("att", [P, HB, P])
        CE = ph.sb("CE", [P, HB, P])
        dec = ph.sb("dec", [P, HB, NB])
        xd = ph.sb("xd", [P, HB, HDB])
        xde = ph.sb("xde", [P, HB, HDB])
        to_end = ph.sb("to_end", [P, HB])
        CBm = ph.sb("CBm", [P, 2, P])
        B_tok = ph.sb("B_tok", [P, 2, NBS])
        y = ph.sb("y", [P, KB, P])
        rs = ph.sb("rs", [P, 2, P])
        bank = [ph.ps(f"bank{i}", [P, BANK]) for i in range(8)]
        rl_flat = RL[:, :, :].rearrange("p h l -> p (h l)")
        tap0, tap1 = xc, att[:, 0:NXBC, :]
        tap2, tap3 = RL[:, 0:NXBC, :], CE[:, 0:NXBC, :]
        B_blk = RL[:, :, :].rearrange("p (b u) l -> p b (u l)", u=2)
        squares = xde[:, :, :].rearrange("p h q -> p (h q)").rearrange("p (j c) -> p j c", c=P)
        (xbc_in, z_in, dt_in, raw_free, unfolded, dt_y_done, dt_abs, dt_exp, dt_ln, dt_done, ea, la_done, dtT, dt_tok,
         RL_done, t0, t1, t2, t3, t01, t23, conv_done, silu_done, z_done, seg_mm, seg_done, cum_mm, cum_done,
         CB_mm, CB_done, att_done, dec_done, CE_done, xT_done, xd_done, end_mm, end_done, xde_done, B_T, B_done,
         Bblk_done, y_mm, skip_done, y_done, yz_done, sq_done, ss_mm, var1, var2, rs_done, rms_done, out_done,
         st_mm, st_dec, st_done, waited, yz_free, y_mm_credit, out_credit, st_mm_all) = ph.sems(
            "xbc_in z_in dt_in raw_free unfolded dt_y_done dt_abs dt_exp dt_ln dt_done ea la_done dtT dt_tok "
            "RL_done t0 t1 t2 t3 t01 t23 conv_done silu_done z_done seg_mm seg_done cum_mm cum_done "
            "CB_mm CB_done att_done dec_done CE_done xT_done xd_done end_mm end_done xde_done B_T B_done "
            "Bblk_done y_mm skip_done y_done yz_done sq_done ss_mm var1 var2 rs_done rms_done out_done "
            "st_mm st_dec st_done waited "
            "yz_free y_mm_credit out_credit st_mm_all")
        block = ph.block()
        QH = BANK // P

        def window(w, sample):
            if sample:
                v = raw[:, :, :].rearrange("p j (b c) -> p j b c", c=BLK + 3)
                return v[:, :, :, w:w + BLK]
            return raw[:, :, w:w + P]

        def fold(ap, sample):
            return ap.rearrange("p j (b c) -> p j b c", c=BLK) if sample else ap

        def tap_w(w, sample):
            at = ROW_B["conv_w"] + w * NXBC
            v = bc(g.colB[:, at:at + NXBC], 2, P)
            return fold(v, True) if sample else v

        @block.sync
        def _(sp):
            def load(tn, sample):
                xbc = g.pT[JX * P:NAB * P, :].rearrange("(j p) c -> p j c", p=P)
                z = g.pT[JZ * P:JX * P, :].rearrange("(j p) c -> p j c", p=P)
                at = tn.col(P, HALO)
                tn.wait(raw_free)
                if sample:
                    sp.wait_ge(out_done, NT - 1)
                    sp.dma_start(y[:, :, :], xbc[:, 0:KB, ds(at, P)]).then_inc(xbc_in, 16)
                    sp.dma_start(xd[:, 0:(NXBC - KB) * 2, :].rearrange("p (j u) c -> p j (u c)", u=2),
                                 xbc[:, KB:NXBC, ds(at, P)]).then_inc(xbc_in, 16)
                else:
                    at3 = tn.col(P, 0)
                    sp.dma_start(raw[:, :, 0:3 + P], xbc[:, :, ds(at3, 3 + P)]).then_inc(xbc_in, 16)
                sp.dma_start(dt_raw[:, :], g.pT[NAB * P:NAB * P + HB, ds(at, P)]).then_inc(dt_in, 16)
                tn.wait(yz_free)
                sp.dma_start(zt[:, :, :], z[:, :, ds(at, P)]).then_inc(z_in, 16)
            each_tile(sp, load)

        @block.vector
        def _(dve):
            tt, stt = nc.vector.tensor_tensor, nc.vector.scalar_tensor_tensor
            dve.sem_inc(raw_free, 1)
            dve.sem_inc(yz_free, 1)
            dve.sem_inc(out_credit, 1)
            dve.wait_ge(ea, 1)
            nc.vector.memset(S[:, :, :], 0.0).then_inc(st_done, 1)

            def tile(tn, sample):
                at = tn.col(P)
                after, notafter = (g.after, g.notafter) if sample else (g.after128, g.notafter128)
                if sample:
                    dve.wait_ge(xbc_in, NTP * 16 + 32)
                    v = raw[:, :, :].rearrange("p j (b c) -> p j b c", c=BLK + 3)
                    nc.vector.tensor_copy(v[:, 0:KB, :, 3:], fold(y[:, :, :], True))
                    nc.vector.tensor_copy(v[:, KB:, :, 3:], fold(
                        xd[:, 0:(NXBC - KB) * 2, :].rearrange("p (j u) c -> p j (u c)", u=2), True))
                    nc.vector.tensor_copy(v[:, :, :, 0:3], g.convT[:, :, :].rearrange("p j (b c) -> p j b c", c=3)
                                          ).then_inc(unfolded, 1)
                    dve.wait_ge(unfolded, 1)
                else:
                    dve.wait_ge(xbc_in, tn.t * 16 + 16)
                dve.wait_ge(dt_in, tn.t * 16 + 16)
                nc.vector.tensor_scalar(dt_y[:, :], dt_raw[:, :], g.dt_bias[:, 0:1], None, ALU.add
                                        ).then_inc(dt_y_done, 1)
                tn.wait(dt_y_done)
                stt(dt_e[:, :], dt_y[:, :], -1.0, dt_y[:, :], ALU.mult, ALU.max).then_inc(dt_abs, 1)
                tn.wait(y_mm_credit)
                tt(fold(tap0[:, :, :], sample), window(0, sample), tap_w(0, sample), ALU.mult).then_inc(t0, 1)
                tt(fold(tap1, sample), window(1, sample), tap_w(1, sample), ALU.mult).then_inc(t1, 1)
                tn.wait(t1)
                tt(tap0[:, :, :], tap0[:, :, :], tap1, ALU.add).then_inc(t01, 1)
                tn.wait(t01)
                tn.wait(t23)
                tt(xc[:, :, :], tap0[:, :, :], tap2, ALU.add).then_inc(conv_done, 1)
                tn.wait(conv_done)
                dve.sem_inc(raw_free, 1)
                tn.wait(dt_ln)
                stt(dtla[:, 0, :], dt_y[:, :], 0.0, dt_e[:, :], ALU.max, ALU.add).then_inc(dt_done, 1)
                tn.wait(dt_done)
                nc.vector.tensor_scalar(dtla[:, 1, :], dtla[:, 0, :], exp_a[:, 0:1], None, ALU.mult
                                        ).then_inc(la_done, 1)
                tn.wait(dtT)
                nc.vector.tensor_copy(dtla_tok[:, :, :].rearrange("p a h -> p (a h)"), bank[6][:, 0:2 * HB]
                                      ).then_inc(dt_tok, 1)
                tn.wait(dt_tok)
                tt(RL[:, :, :], bc(dtla_tok[:, 1, :], 2, P), bc(notafter[:, :], 1, HB), ALU.mult).then_inc(RL_done, 1)
                tn.wait(xT_done)
                for i in range(2):
                    ins = tt(xd[:, i * GH:(i + 1) * GH, :], bank[4 + i][:, :].rearrange("p (h q) -> p h q", q=HDB),
                             bc(dtla_tok[:, 0, i * GH:(i + 1) * GH], 2, HDB), ALU.mult)
                ins.then_inc(xd_done, 1)
                tn.wait(B_T)
                nc.vector.tensor_copy(B_tok[:, :, :].rearrange("p g n -> p (g n)"), bank[7][:, 256:512]
                                      ).then_inc(B_done, 1)
                tt(CBm[:, :, :], bank[7][:, 0:256].rearrange("p (g c) -> p g c", c=P), bc(notafter[:, :], 1, 2),
                   ALU.mult).then_inc(CB_done, 1)
                tn.wait(CB_done)
                tn.wait(seg_done, 4)
                for i in range(2):
                    hs = slice(i * GH, (i + 1) * GH)
                    ins = tt(att[:, hs, :], att[:, hs, :], bc(CBm[:, i, :], 1, GH), ALU.mult)
                ins.then_inc(att_done, 1)
                tn.wait(skip_done)
                tn.wait(y_mm)
                for i in range(2):
                    ins = tt(y[:, 4 * i:4 * i + 4, :], y[:, 4 * i:4 * i + 4, :],
                             bank[4 + i][:, :].rearrange("p (j c) -> p j c", c=P), ALU.add)
                ins.then_inc(y_done, 1)
                if not sample:
                    tn.wait(dec_done)
                    tt(S[:, 0, :].rearrange("p (h q) -> p h q", q=HDB), S[:, 0, :].rearrange("p (h q) -> p h q", q=HDB),
                       bc(dec[:, :, 0], 2, HDB), ALU.mult).then_inc(st_dec, 1)
                    tn.wait(st_dec)
                    dve.wait_ge(st_mm, tn.t + 1)
                    for i in range(2):
                        ins = tt(S[:, 0, i * BANK:(i + 1) * BANK], S[:, 0, i * BANK:(i + 1) * BANK], bank[i][:, :],
                                 ALU.add)
                    ins.then_inc(st_done, 1)
                else:
                    for b in range(NB):
                        v = S_samples[:, b, :].rearrange("p (h q) -> p h q", q=HDB)
                        tt(v, v, bc(dec[:, :, b], 2, HDB), ALU.mult).then_inc(st_dec, 1)
                        dve.wait_ge(st_dec, NTP + b + 1)
                        dve.wait_ge(st_mm, NTP + b + 1)
                        for i in range(2):
                            ins = tt(S_samples[:, b, i * BANK:(i + 1) * BANK], S_samples[:, b, i * BANK:(i + 1) * BANK],
                                     bank[2 * (b % 2) + i][:, :], ALU.add)
                        ins.then_inc(st_done, 1)
                tn.wait(z_done)
                tn.wait(y_done)
                tt(y[:, :, :], y[:, :, :], zt[:, :, :], ALU.mult).then_inc(yz_done, 1)
                tn.wait(yz_done)
                dve.sem_inc(yz_free, 1)
                tn.wait(ss_mm)
                nc.vector.tensor_scalar(rs[:, :, :].rearrange("p g c -> p (g c)"), bank[6][:, 256:512],
                                        1.0 / (WB // 2), 1e-5, ALU.mult, ALU.add).then_inc(var1, 1)
                tn.wait(var1)
                nc.vector.reciprocal(rs[:, :, :], rs[:, :, :]).then_inc(var2, 1)
                tn.wait(rs_done)
                for i in range(2):
                    ins = tt(y[:, 4 * i:4 * i + 4, :], y[:, 4 * i:4 * i + 4, :], bc(rs[:, i, :], 1, 4), ALU.mult)
                ins.then_inc(rms_done, 1)
                tn.wait(rms_done)
                at_w = ROW_B["norm_b_w"]
                tt(g.act[:, PAIRS:KACT, ds(at, P)], y[:, :, :], bc(g.colB[:, at_w:at_w + KB], 2, P), ALU.mult
                   ).then_inc(out_done, 1)
                tn.wait(out_done)
                dve.sem_inc(out_credit, 1)
            each_tile(dve, tile)

        @block.gpsimd
        def _(pool):
            tt = nc.gpsimd.tensor_tensor

            def tile(tn, sample):
                if sample:
                    pool.wait_ge(unfolded, 1)
                else:
                    pool.wait_ge(xbc_in, tn.t * 16 + 16)
                tn.wait(y_mm_credit)
                tt(fold(tap2, sample), window(2, sample), tap_w(2, sample), ALU.mult).then_inc(t2, 1)
                tt(fold(tap3, sample), window(3, sample), tap_w(3, sample), ALU.mult).then_inc(t3, 1)
                tn.wait(t2)
                tn.wait(t3)
                tt(tap2, tap2, tap3, ALU.add).then_inc(t23, 1)
                tn.wait(t23)
                tn.wait(silu_done)
                held(tn, waited, cum_done, 4)
                if sample:
                    nc.gpsimd.tensor_copy(dec[:, :, :], CE[:, :, :].rearrange("p h (b c) -> p h b c", c=BLK)[:, :, :, BLK - 1]
                                          ).then_inc(dec_done, 1)
                else:
                    nc.gpsimd.tensor_copy(dec[:, :, 0], CE[:, :, P - 1]).then_inc(dec_done, 1)
                tn.wait(dec_done)
                for i in range(2):
                    hs = slice(i * GH, (i + 1) * GH)
                    ins = tt(CE[:, hs, :], CE[:, hs, :], bc(xc[:, KB + 2 + i, :], 1, GH), ALU.mult)
                ins.then_inc(CE_done, 1)
                tn.wait(end_done)
                tn.wait(xd_done)
                tt(xde[:, :, :], xd[:, :, :], bc(to_end[:, :], 2, HDB), ALU.mult).then_inc(xde_done, 1)
                if sample:
                    tn.wait(B_done)
                    pool.wait_ge(seg_done, 4 * NT)
                    ins = tt(B_blk, bc(B_tok[:, :, :].rearrange("p g n -> p (g n)"), 1, NB),
                             bc(g.blockmask[:, :], 2, 2 * NBS), ALU.mult)
                    ins.then_inc(Bblk_done, 1)
                tn.wait(out_credit)
                tt(y[:, :, :], xc[:, 0:KB, :], bc(g.dskip[:, :], 2, P), ALU.mult).then_inc(skip_done, 1)
            each_tile(pool, tile)

        @block.scalar
        def _(act):
            nc.scalar.activation(exp_a[:, :], g.a_log[:, :], ACT.Exp).then_inc(ea, 1)

            def tile(tn, sample):
                tn.wait(dt_abs)
                nc.scalar.activation(dt_e[:, :], dt_e[:, :], ACT.Exp, scale=-1.0).then_inc(dt_exp, 1)
                tn.wait(dt_exp)
                nc.scalar.activation(dt_e[:, :], dt_e[:, :], ACT.Ln, bias=1.0).then_inc(dt_ln, 1)
                tn.wait(conv_done)
                for j in range(NXBC):
                    at = ROW_B["conv_b"] + j
                    ins = nc.scalar.activation(xc[:, j, :], xc[:, j, :], ACT.Silu, bias=g.colB[:, at:at + 1])
                ins.then_inc(silu_done, 1)
                act.wait_ge(z_in, tn.t * 16 + 16)
                nc.scalar.activation(zt[:, :, :], zt[:, :, :], ACT.Silu).then_inc(z_done, 1)
                for i in range(HB // QH):
                    tn.wait(seg_mm, 4, i + 1)
                    nc.scalar.activation(att[:, i * QH:(i + 1) * QH, :].rearrange("p h l -> p (h l)"),
                                         bank[i % 2][:, :], ACT.Exp, scale=-1.0).then_inc(seg_done, 1)
                    tn.wait(cum_mm, 4, i + 1)
                    nc.scalar.activation(CE[:, i * QH:(i + 1) * QH, :].rearrange("p h l -> p (h l)"),
                                         bank[2 + i % 2][:, :], ACT.Exp, scale=-1.0).then_inc(cum_done, 1)
                tn.wait(end_mm)
                nc.scalar.activation(to_end[:, :], bank[6][:, 32:32 + HB], ACT.Exp, scale=-1.0).then_inc(end_done, 1)
                tn.wait(yz_done)
                tn.wait(st_mm_all)
                nc.scalar.activation(squares, y[:, :, :], ACT.Square).then_inc(sq_done, 1)
                tn.wait(var2)
                nc.scalar.activation(rs[:, :, :], rs[:, :, :], ACT.Sqrt).then_inc(rs_done, 1)
            each_tile(act, tile)

        @block.tensor
        def _(pe):
            mm = nc.tensor.matmul

            def tile(tn, sample):
                after = g.after if sample else g.after128
                held(tn, waited, la_done)
                nc.tensor.transpose(bank[6][:, 0:HB], dtla[:, 0, :], g.ident[0:HB, 0:HB])
                nc.tensor.transpose(bank[6][:, HB:2 * HB], dtla[:, 1, :], g.ident[0:HB, 0:HB]).then_inc(dtT, 1)
                tn.wait(silu_done)
                for j in range(KB):
                    ins = nc.tensor.transpose(bank[4 + j // 4][:, (j % 4) * P:(j % 4 + 1) * P], xc[:, j, :], g.ident[:, :])
                ins.then_inc(xT_done, 1)
                for i in range(2):
                    mm(bank[7][:, i * P:(i + 1) * P], xc[:, KB + i, :], xc[:, KB + 2 + i, :], start=True, stop=True)
                for i in range(2):
                    ins = nc.tensor.transpose(bank[7][:, 256 + i * P:256 + (i + 1) * P], xc[:, KB + i, :], g.ident[:, :])
                ins.then_inc(B_T, 1)
                tn.wait(RL_done)
                if not sample:
                    tn.wait(st_done)
                for i in range(HB // QH):
                    if i >= 2:
                        tn.wait(seg_done, 4, i - 1)
                        tn.wait(cum_done, 4, i - 1)
                    rhs = rl_flat[:, i * BANK:(i + 1) * BANK]
                    mm(bank[i % 2][:, :], after[:, :], rhs, start=True, stop=True).then_inc(seg_mm, 1)
                    mm(bank[2 + i % 2][:, :], g.ones[:, :], rhs, start=True, stop=True).then_inc(cum_mm, 1)
                mm(bank[6][:, 32:32 + HB], after[:, :], dtla_tok[:, 1, :], start=True, stop=True).then_inc(end_mm, 1)
                tn.wait(att_done)
                tn.wait(CE_done)
                for h in range(HB):
                    part, j = slice(64 * (h % 2), 64 * (h % 2) + 64), h // 2
                    out = bank[4 + j // 4][part, (j % 4) * P:(j % 4 + 1) * P]
                    mm(out, xd[:, h, :], att[:, h, :], start=True, stop=False)
                    if sample:
                        for b in range(NB):
                            ins = mm(out[:, b * BLK:(b + 1) * BLK], S_samples[:, b, h * HDB:(h + 1) * HDB],
                                     CE[:, h, b * BLK:(b + 1) * BLK], start=False, stop=(b == NB - 1))
                    else:
                        ins = mm(out, S[:, 0, h * HDB:(h + 1) * HDB], CE[:, h, :], start=False, stop=True)
                ins.then_inc(y_mm, 1)
                pe.wait_ge(y_mm, tn.t + 1)
                pe.sem_inc(y_mm_credit, 1)
                tn.wait(xde_done)
                if sample:
                    tn.wait(seg_done, 4)
                    pe.wait_ge(Bblk_done, 1)
                    for b in range(NB):
                        if b >= 2:
                            pe.wait_ge(st_done, 1 + NTP + b - 1)
                        for i in range(2):
                            ins = mm(bank[2 * (b % 2) + i][:, :], B_blk[:, b, i * NBS:(i + 1) * NBS],
                                     xde[:, i * GH:(i + 1) * GH, :].rearrange("p h q -> p (h q)"), start=True, stop=True)
                        ins.then_inc(st_mm, 1)
                    pe.wait_ge(st_mm, NTP + NB)
                else:
                    for i in range(2):
                        ins = mm(bank[i][:, :], B_tok[:, i, :], xde[:, i * GH:(i + 1) * GH, :].rearrange("p h q -> p (h q)"),
                                 start=True, stop=True)
                    ins.then_inc(st_mm, 1)
                    pe.wait_ge(st_mm, tn.t + 1)
                pe.sem_inc(st_mm_all, 1)
                tn.wait(sq_done)
                for i in range(2):
                    for j in range(4):
                        ins = mm(bank[6][:, 256 + i * P:256 + (i + 1) * P], g.ones[:, :], squares[:, 4 * i + j, :],
                                 start=(j == 0), stop=(j == 3))
                ins.then_inc(ss_mm, 1)
            pe.sem_inc(y_mm_credit, 1)
            each_tile(pe, tile)


HC = 8
LEVELS = (8, 4, 2, 1)


def hgrn(nc, g, A, out_p, out_s):
    with Phase(nc, "hgrn") as ph:
        def arr(name):
            return ph.sb(name, [P, HC, P])
        raw = ph.sb("raw", [P, 4 * HC, P])
        q_, f_, i_, gg = (raw[:, n * HC:(n + 1) * HC, :] for n in range(4))
        sq_ = arr("sq")
        lf, b_, k_ = arr("lf"), arr("b"), arr("k")
        E = [arr("E0"), arr("E1")]
        QL, KL = [arr("QL0"), arr("QL1")], [arr("KL0"), arr("KL1")]
        Qe, rem = arr("Qe"), arr("rem")
        v_tok, k_tok = arr("v_tok"), lf
        sig_g = arr("sig_g")
        dend = ph.sb("dend", [P, HC, NB])
        Vm = ph.sb("Vm", [P, 2, NB, P])
        room = g.act[:, HC:KACT, :].rearrange("p a b -> p (a b)")
        S = room[:, 0:HC * P].rearrange("p (h v) -> p h v", v=P)
        Sb = ph.sb("Sb", [P, 3, NB + 1, P])
        S_new = room[:, HC * P:HC * P + 2 * NB * P].rearrange("p (a b v) -> p a b v", a=2, b=NB)
        att = room[:, (HC + 2 * NB) * P:(2 * HC + 2 * NB) * P].rearrange("p (h c) -> p h c", c=P)
        o_, osq = QL[0], KL[0]
        rs = QL[1]
        bank = [ph.ps(f"bank{i}", [P, BANK]) for i in range(8)]
        (loaded, raw_free, absf, e1, l1, lf_done, b_done, kx, k_done, sig_q, sig_g_done, q_done, rem_sub, exps, Qe_done,
         kend_done, D_done, E_done, QK_done, gram, att_out, T_done, tok_v, tok_k, Vm_done, H_mm, chained, state_in,
         o_mm, o_done, osq_done, ss_mm, var1, var2, rs_done, normed, gm, out_done, samples_in, S_out, S_kept, waited,
         dend_done, level_used) = ph.sems(
            "loaded raw_free absf e1 l1 lf_done b_done kx k_done sig_q sig_g_done q_done rem_sub exps Qe_done "
            "kend_done D_done E_done QK_done gram att_out T_done tok_v tok_k Vm_done H_mm chained state_in "
            "o_mm o_done osq_done ss_mm var1 var2 rs_done normed gm out_done samples_in S_out S_kept waited "
            "dend_done level_used")
        in0, in1, in2, so0, so1, tile_free = ph.sems("in0 in1 in2 so0 so1 tile_free")
        ins_, outs_ = (in0, in1, in2), (so0, so1)
        block = ph.block()
        flat = lambda ap: ap.rearrange("p h c -> p (h c)")
        two = lambda ap, i: ap[:, 4 * i:4 * i + 4, :].rearrange("p h c -> p (h c)")
        blocks = lambda ap: ap.rearrange("p h (b c) -> p (h b) c", c=BLK)

        @block.sync
        def _(sp):
            src = g.pT[0:NC_ * P, :].rearrange("(j p) c -> p j c", p=P)

            def load(tn, sample):
                at = tn.col(P, HALO)
                tn.wait(raw_free)
                sp.dma_start(raw[:, :, :], src[:, :, ds(at, P)]).then_inc(loaded, 16)
                if sample:
                    def load_states(h):
                        sp.dma_start(Sb[:, h % 3, 0:NB, :], A["state_hgrn"][:, 0, h].rearrange("b k v -> k b v")
                                     ).then_inc(ins_[h % 3], 16)
                    sp.wait_ge(o_mm, NTP * HC)
                    sp.wait_ge(S_kept, NTP * HC)
                    for h in range(3):
                        load_states(h)
                    for h in range(HC):
                        sp.wait_ge(chained, NTP * HC * NB + (h + 1) * NB)
                        sp.dma_start(out_s[:, 0, h].rearrange("b k v -> k b v"), S_new[:, h % 2, :, :]
                                     ).then_inc(outs_[h % 2], 16)
                        if h + 3 < HC:
                            sp.wait_ge(o_mm, NTP * HC + h + 1)
                            load_states(h + 3)
            each_tile(sp, load)
            sp.wait_ge(S_kept, NTP * HC)
            sp.dma_start(out_p[0, 0].rearrange("h k v -> k h v"), S).then_inc(S_out, 16)
            sp.wait_ge(so0, 64)
            sp.wait_ge(so1, 64)
            sp.wait_ge(S_out, 16)

        @block.scalar
        def _(act):
            def tile(tn, sample):
                tn.wait(absf)
                nc.scalar.activation(lf[:, :, :], lf[:, :, :], ACT.Exp, scale=-1.0).then_inc(e1, 1)
                tn.wait(e1)
                nc.scalar.activation(lf[:, :, :], lf[:, :, :], ACT.Ln, bias=1.0).then_inc(l1, 1)
                nc.scalar.activation(sq_[:, :, :], q_, ACT.Sigmoid).then_inc(sig_q, 1)
                nc.scalar.activation(k_[:, :, :], f_, ACT.Sigmoid, scale=-1.0).then_inc(k_done, 1)
                nc.scalar.activation(sig_g[:, :, :], gg, ACT.Sigmoid).then_inc(sig_g_done, 1)
                tn.wait(T_done, 2, 1)
                for i in range(2):
                    ins = nc.scalar.copy(two(v_tok, i), bank[4 + i][:, :])
                ins.then_inc(tok_v, 1)
                tn.wait(b_done)
                nc.scalar.activation(Qe[:, :, :], b_[:, :, :], ACT.Exp)
                tn.wait(rem_sub)
                nc.scalar.activation(rem[:, :, :], rem[:, :, :], ACT.Exp).then_inc(exps, 1)
                for L, h_ in enumerate(LEVELS):
                    tn.wait(D_done, 4, L + 1)
                    v = E[L % 2][:, :, :].rearrange("p h (m u c) -> p (h m) u c", u=2, c=h_)
                    nc.scalar.activation(v[:, :, 0, :], v[:, :, 0, :], ACT.Exp, scale=-1.0)
                    nc.scalar.activation(v[:, :, 1, :], v[:, :, 1, :], ACT.Exp).then_inc(E_done, 1)
                tn.wait(T_done, 2, 2)
                for i in range(2):
                    ins = nc.scalar.copy(two(k_tok, i), bank[6 + i][:, :])
                ins.then_inc(tok_k, 1)
                tn.wait(o_mm, HC)
                for i in range(2):
                    ins = nc.scalar.copy(two(o_, i), bank[i][:, :])
                ins.then_inc(o_done, 1)
                tn.wait(o_done)
                nc.scalar.activation(osq[:, :, :], o_[:, :, :], ACT.Square).then_inc(osq_done, 1)
                tn.wait(var2)
                nc.scalar.activation(rs[:, :, :], rs[:, :, :], ACT.Sqrt).then_inc(rs_done, 1)
            each_tile(act, tile)

        @block.gpsimd
        def _(pool):
            tt = nc.gpsimd.tensor_tensor
            def tile(tn, sample):
                tn.wait(b_done)
                tt(blocks(rem[:, :, :]), blocks(b_[:, :, :])[:, :, BLK - 1:BLK].to_broadcast([P, HC * NB, BLK]),
                   blocks(b_[:, :, :]), ALU.subtract).then_inc(rem_sub, 1)
                for L, h_ in enumerate(LEVELS):
                    if L >= 2:
                        tn.wait(QK_done, 4, L - 1)
                    v = b_[:, :, :].rearrange("p h (m c) -> p (h m) c", c=2 * h_)
                    d = E[L % 2][:, :, :].rearrange("p h (m c) -> p (h m) c", c=2 * h_)
                    n = HC * P // (2 * h_)
                    tt(d, v, v[:, :, h_ - 1:h_].to_broadcast([P, n, 2 * h_]), ALU.subtract).then_inc(D_done, 1)
                tn.wait(exps)
                tn.wait(q_done)
                tt(dend[:, :, :], Qe[:, :, :].rearrange("p h (b c) -> p h b c", c=BLK)[:, :, :, BLK - 1],
                   bc(g.ones[:, 0:NB], 1, HC), ALU.mult).then_inc(dend_done, 1)
                tn.wait(k_done)
                tt(rem[:, :, :], rem[:, :, :], k_[:, :, :], ALU.mult).then_inc(kend_done, 1)
                tn.wait(dend_done)
                tt(Qe[:, :, :], Qe[:, :, :], sq_[:, :, :], ALU.mult).then_inc(Qe_done, 1)
                tn.wait(tok_v)
                for h in range(HC):
                    if h >= 2:
                        tn.wait(H_mm, 8, h - 1)
                    tt(Vm[:, h % 2, :, :], bc(v_tok[:, h, :], 1, NB), bc(g.blockmask[:, :], 2, P), ALU.mult
                       ).then_inc(Vm_done, 1)
            each_tile(pool, tile)

        @block.vector
        def _(dve):
            tt, stt = nc.vector.tensor_tensor, nc.vector.scalar_tensor_tensor
            dve.sem_inc(raw_free, 1)
            nc.vector.memset(S, 0.0).then_inc(state_in, 1)
            dve.wait_ge(state_in, 1)
            dve.sem_inc(tile_free, 1)

            def tile(tn, sample):
                at = tn.col(P)
                dve.wait_ge(loaded, tn.t * 16 + 16)
                stt(lf[:, :, :], f_, -1.0, f_, ALU.mult, ALU.max).then_inc(absf, 1)
                tn.wait(l1)
                stt(lf[:, :, :], f_, 0.0, lf[:, :, :], ALU.min, ALU.subtract).then_inc(lf_done, 1)
                tn.wait(lf_done)
                for i in range(2):
                    ins = nc.vector.tensor_tensor_scan(two(b_, i), g.reset[:, :], two(lf, i), 0.0, ALU.mult, ALU.add)
                ins.then_inc(b_done, 1)
                tn.wait(sig_q)
                tt(sq_[:, :, :], sq_[:, :, :], q_, ALU.mult).then_inc(q_done, 1)
                tn.wait(sig_g_done)
                tt(sig_g[:, :, :], sig_g[:, :, :], gg, ALU.mult).then_inc(gm, 1)
                tn.wait(k_done)
                tn.wait(q_done)
                tn.wait(T_done, 2, 1)
                tn.wait(gm)
                dve.sem_inc(raw_free, 1)

                def take(L):
                    for i in range(2):
                        src = bank[2 * (L % 2) + i][:, :].rearrange("p (h c) -> p h c", c=P)
                        dst = att[:, 4 * i:4 * i + 4, :]
                        if L == 0:
                            ins = tt(dst, src, bc(g.level_mask[:, 4, :], 1, 4), ALU.mult)
                        else:
                            ins = nc.vector.copy_predicated(
                                dst, bc(g.level_mask[:, L - 1, :], 1, 4).bitcast(mybir.dt.uint32), src)
                    ins.then_inc(att_out, 1)

                for L in range(4):
                    tn.wait(E_done, 4, L + 1)
                    if L >= 2:
                        tn.wait(gram, 5, L)
                    e, u = E[L % 2], L % 2
                    tt(QL[u][:, :, :], sq_[:, :, :], e[:, :, :], ALU.mult)
                    tt(KL[u][:, :, :], k_[:, :, :], e[:, :, :], ALU.mult).then_inc(QK_done, 1)
                    held(tn, waited, gram, 5, L + 1)
                    take(L)
                    tn.wait(att_out, 5, L + 1)
                held(tn, waited, gram, 5, 5)
                take(4)
                tn.wait(dend_done)
                for h in range(HC):
                    u = h % 3
                    if sample:
                        dve.wait_ge(ins_[u], 16 * (h // 3 + 1))
                        if h >= 2:
                            dve.wait_ge(outs_[h % 2], 16 * (h // 2))
                    else:
                        if h >= 3:
                            tn.wait(o_mm, 8, h - 2)
                        nc.vector.tensor_copy(Sb[:, u, 0, :], S[:, h, :]).then_inc(state_in, 1)
                        dve.wait_ge(state_in, tn.t * HC + (h + 2))
                    tn.wait(H_mm, 8, h + 1)
                    for b in range(NB):
                        src = bank[4 + 2 * (h % 2) + b // 4][:, (b % 4) * P:(b % 4 + 1) * P]
                        dst = S_new[:, h % 2, b, :] if sample else Sb[:, u, b + 1, :]
                        stt(dst, Sb[:, u, b, :], dend[:, h, b:b + 1], src, ALU.mult, ALU.add).then_inc(chained, 1)
                        if not sample:
                            dve.wait_ge(chained, tn.t * (HC * NB) + (h * NB + b + 1))
                    if not sample:
                        nc.vector.tensor_copy(S[:, h, :], Sb[:, u, NB, :]).then_inc(S_kept, 1)
                if not sample:
                    tn.wait(S_kept, 8)
                tn.wait(ss_mm)
                for i in range(2):
                    ins = nc.vector.tensor_scalar(two(rs, i), bank[2 + i][:, :], 1.0 / P, 1e-5, ALU.mult, ALU.add)
                ins.then_inc(var1, 1)
                tn.wait(var1)
                nc.vector.reciprocal(rs[:, :, :], rs[:, :, :]).then_inc(var2, 1)
                tn.wait(rs_done)
                for h in range(HC):
                    w = g.colB[:, ROW_B["norm_c_w"] + h:ROW_B["norm_c_w"] + h + 1]
                    ins = stt(o_[:, h, :], o_[:, h, :], w, rs[:, h, :], ALU.mult, ALU.mult)
                ins.then_inc(normed, 1)
                tn.wait(normed)
                tt(g.act[:, 0:HC, ds(at, P)], o_[:, :, :], sig_g[:, :, :], ALU.mult).then_inc(out_done, 1)
                tn.wait(out_done)
                dve.sem_inc(tile_free, 1)
            each_tile(dve, tile)

        @block.tensor
        def _(pe):
            mm = nc.tensor.matmul

            def tile(tn, sample):
                pe.wait_ge(loaded, tn.t * 16 + 16)
                tn.wait(tile_free)
                for h in range(HC):
                    ins = nc.tensor.transpose(bank[4 + h // 4][:, (h % 4) * P:(h % 4 + 1) * P], i_[:, h, :], g.ident[:, :])
                ins.then_inc(T_done, 1)

                def gram_level(L):
                    K, Q = (k_, sq_) if L == 0 else (KL[(L - 1) % 2], QL[(L - 1) % 2])
                    for h in range(HC):
                        ins = mm(bank[2 * (L % 2) + h // 4][:, (h % 4) * P:(h % 4 + 1) * P], K[:, h, :], Q[:, h, :],
                                 start=True, stop=True)
                    ins.then_inc(gram, 1)
                tn.wait(k_done)
                tn.wait(q_done)
                gram_level(0)
                for L in range(1, 5):
                    tn.wait(QK_done, 4, L)
                    if L >= 2:
                        tn.wait(att_out, 5, L - 1)
                    gram_level(L)
                    if L == 1:
                        tn.wait(kend_done)
                        for h in range(HC):
                            ins = nc.tensor.transpose(bank[6 + h // 4][:, (h % 4) * P:(h % 4 + 1) * P], rem[:, h, :],
                                                      g.ident[:, :])
                        ins.then_inc(T_done, 1)

                def states(h):
                    if h == 0:
                        tn.wait(tok_k)
                    tn.wait(Vm_done, 8, h + 1)
                    if h >= 2:
                        tn.wait(chained, HC * NB, (h - 1) * NB)
                    for i in range(2):
                        ins = mm(bank[4 + 2 * (h % 2) + i][:, :], k_tok[:, h, :],
                                 Vm[:, h % 2, 4 * i:4 * i + 4, :].rearrange("p b v -> p (b v)"), start=True, stop=True)
                    ins.then_inc(H_mm, 1)
                states(0)
                states(1)
                tn.wait(att_out, 5, 5)
                tn.wait(Qe_done)
                for h in range(HC):
                    if sample:
                        pe.wait_ge(ins_[h % 3], 16 * (h // 3 + 1))
                    else:
                        tn.wait(chained, HC * NB, (h + 1) * NB - 1)
                    out = bank[h // 4][:, (h % 4) * P:(h % 4 + 1) * P]
                    mm(out, v_tok[:, h, :], att[:, h, :], start=True, stop=False)
                    for b in range(NB):
                        ins = mm(out[:, b * BLK:(b + 1) * BLK], Sb[:, h % 3, b, :], Qe[:, h, b * BLK:(b + 1) * BLK],
                                 start=False, stop=(b == NB - 1))
                    ins.then_inc(o_mm, 1)
                    if h + 2 < HC:
                        states(h + 2)
                tn.wait(osq_done)
                for i in range(2):
                    ins = mm(bank[2 + i][:, :], g.ones[:, :], two(osq, i), start=True, stop=True)
                ins.then_inc(ss_mm, 1)
                tn.wait(ss_mm)
            each_tile(pe, tile)


def allocate(nc, g, ctx):
    def sb(name, shape):
        return ctx.enter_context(nc.sbuf_tensor(name, shape, F32))
    g.xT = sb("xT", [P, KD, T])
    g.act = sb("act", [P, KACT, T])
    g.ident = sb("ident", [P, P])
    g.ones = sb("ones", [P, P])
    g.ones64 = sb("ones64", [P, P])
    g.blockmask = sb("blockmask", [P, NB])
    g.reset = sb("reset", [P, 4 * P])
    g.before = sb("before", [P, P])
    g.notafter = sb("notafter", [P, P])
    g.after = sb("after", [P, P])
    g.notafter128 = sb("notafter128", [P, P])
    g.after128 = sb("after128", [P, P])
    g.gram_mask = sb("gram_mask", [P, 2, 2, P])
    g.level_mask = sb("level_mask", [P, 5, P])
    g.colA = sb("colA", [P, P])
    g.colB = sb("colB", [P, NROW_B])
    g.scT = sb("scT", [P, KD, SEQS])
    g.mod = sb("mod", [P, DEPTH * 6 * KD, SEQS])
    g.scale = sb("scale", [P, DEPTH, 2, KD, SEQS])
    g.shiftT = sb("shiftT", [P, NA, NS])
    g.convT = sb("convT", [P, NXBC, NS * 3])
    g.tails = sb("tails", [P, NAB, SEQS * TAIL])
    g.dskip = sb("dskip", [P, KD])
    g.dt_bias = sb("dt_bias", [HB, 1])
    g.a_log = sb("a_log", [HB, 1])
    g.modcol = lambda layer, j: g.mod[:, (layer * 6 + j) * KD:(layer * 6 + j + 1) * KD, :]


def build(nc, A, outs):
    g = Core()
    (y_prompt, y_sample, rwkv_p, shift_p, ssm_p, conv_p, hgrn_p,
     rwkv_s, shift_s, ssm_s, conv_s, hgrn_s) = outs
    with ExitStack() as ctx:
        g.pT = nc.dram_tensor("pT", [NAB * P + HB, HALO + T], F32).ap()
        allocate(nc, g, ctx)
        constants(nc, g)
        load_inputs(nc, g, A)
        modulation(nc, g, A)
        with normed_x(nc, g):
            norm(nc, g, 0, 0)
            project_to_dram(nc, g, A["w_in_ab"][0], IN_AB, "in_ab", True)
        new_shift_conv(nc, g, shift_p, conv_p, shift_s, conv_s)
        rwkv(nc, g, A, rwkv_p, rwkv_s)
        mamba(nc, g, A, ssm_p, ssm_s)
        multiply_down(nc, g, A["w_out_ab"][0], 12, g.modcol(0, 2), "out_ab")
        ffn(nc, g, A, 0)
        with normed_x(nc, g):
            norm(nc, g, 1, 0)
            project_to_dram(nc, g, A["w_in_c"][0], IN_C, "in_c", False)
        hgrn(nc, g, A, hgrn_p, hgrn_s)
        multiply_down(nc, g, A["w_out_c"][0], 8, g.modcol(1, 2), "out_c")
        ffn(nc, g, A, 1)
        with normed_x(nc, g):
            write_y(nc, g, y_prompt, y_sample)


@contextmanager
def normed_x(nc, g):
    with nc.sbuf_tensor(f"hT{nc.next_id()}", [P, KD, T], F32) as g.hT:
        yield


def ffn(nc, g, A, layer):
    with normed_x(nc, g):
        norm(nc, g, layer, 1)
        for part, (first, n_slabs) in enumerate(((0, 6), (6, 5))):
            gate_up(nc, g, A["w_gate"][layer], A["w_up"][layer], first, n_slabs, f"up{layer}{part}")
            multiply_down(nc, g, A["w_down"][layer, first * SLAB:(first + n_slabs) * SLAB, :], 2 * n_slabs,
                          g.modcol(layer, 5), f"down{layer}{part}")


_OUTS = [(1, 1024, 1024), (8, 16, 1024), (1, 1, 8, 64, 64), (1, 1, 1792), (1, 1, 16, 64, 128), (1, 1, 3, 1536),
         (1, 1, 8, 128, 128), (8, 1, 8, 64, 64), (8, 1, 1792), (8, 1, 16, 64, 128), (8, 1, 3, 1536),
         (8, 1, 8, 128, 128)]


def kernel(**inputs):
    import numpy as _np
    import concourse.bacc as _bacc
    from concourse import mybir as _mybir
    from concourse.bass_utils import run_bass_kernel_spmd as _run

    nc = _bacc.Bacc("TRN2", target_bir_lowering=False, num_devices=1)
    arrays, aps = {}, {}
    for name in inputs:
        a = _np.ascontiguousarray(inputs[name])
        arrays[f"in_{name}"] = a
        aps[name] = nc.dram_tensor(f"in_{name}", a.shape, _mybir.dt.from_np(a.dtype), kind="ExternalInput").ap()
    outs = [nc.dram_tensor(f"out_{i}", shape, _mybir.dt.float32, kind="ExternalOutput").ap()
            for i, shape in enumerate(_OUTS)]
    build(nc, aps, outs)
    r = _run(nc, [arrays], core_ids=[0])
    return tuple(r.results[0][f"out_{i}"] for i in range(len(_OUTS)))
```

```python
import math
from contextlib import ExitStack, contextmanager

import concourse.bass as bass
from concourse import mybir

F32 = mybir.dt.float32
F32R = mybir.dt.float32r
ACT = mybir.ActivationFunctionType
ALU = mybir.AluOpType
ds = bass.ds

P = 128
D = 1024
KD = D // P
TP = 1024
NS, LS = 8, 16
T = TP + NS * LS
NT = T // P
NTP = TP // P
CH = 384
NCH = T // CH
SEQS = 1 + NS
BLK = 16
NB = P // BLK
DEPTH = 2
FF = 2816
KF = FF // P
KACT = 12
BANK = 512

WA = 512
A_COLS = 1792
NA = A_COLS // P
JR, JK, JV, JWA, JG = 0, 4, 8, 12, 13
JZ, JX, JB, JC = 14, 22, 30, 32
XBC = 1536
NXBC = XBC // P
HB = 16
IN_AB = 4368
NAB = IN_AB // P
IN_C = 4096
NC_ = IN_C // P
HALO = 3
TAIL = 3
LNX_EPS = 64e-5
KAPPA = math.exp(-0.5)

ROW_A = {"ada_b": 0, "norm_mix_w": 96, "norm_ffn_w": 112}
ROW_B = {"norm_out_w": 0, "mu_a": 8, "w0": 22, "a0": 26, "k_k": 30, "k_a": 34, "r_k": 38, "lnx_w": 42,
         "lnx_b": 46, "conv_b": 50, "norm_b_w": 62, "norm_c_w": 70, "conv_w": 78}
NROW_B = 126


class Core:
    pass


def bc(ap, axis, n):
    ap = ap.unsqueeze(axis)
    shape = list(ap.shape)
    shape[axis] = n
    return ap.to_broadcast(shape)


class Phase:

    def __init__(self, nc, name):
        self.nc, self.name, self.ctx, self.own_sems = nc, name, ExitStack(), []

    def __enter__(self):
        return self

    def __exit__(self, *a):
        self.ctx.__exit__(*a)
        self.nc.clear_and_free_semaphores(self.own_sems)
        self.nc.all_engine_barrier(sem_only=True)

    def sb(self, name, shape, dt=F32):
        return self.ctx.enter_context(self.nc.sbuf_tensor(f"{self.name}_{name}", shape, dt))

    def ps(self, name, shape):
        return self.ctx.enter_context(self.nc.psum_tensor(f"{self.name}_{name}", shape, F32))

    def sems(self, names):
        new = [self.nc.alloc_semaphore(f"{self.name}_{n}") for n in names.split()]
        self.own_sems += new
        return new

    def block(self):
        return self.ctx.enter_context(self.nc.Block())


def constants(nc, g):
    with Phase(nc, "const") as ph:
        step, = ph.sems("step")
        block = ph.block()

        @block.gpsimd
        def _(pool):
            n = [0]

            def then(ins):
                ins.then_inc(step, 1)
                n[0] += 1
                pool.wait_ge(step, n[0])

            def keep(view, base, mult, pattern, op=ALU.is_ge, fill=0.0):
                then(nc.gpsimd.affine_select(out=view, in_=view, compare_op=op, fill=fill, base=base,
                                             pattern=pattern, channel_multiplier=mult))

            def blocks(ap, size):
                return ap.rearrange("p (b j) -> p b j", j=size)

            then(nc.gpsimd.memset(g.ident[:, :], 0.0))
            keep(g.ident[:, :], 0, 1, [[-1, P]], ALU.not_equal, 1.0)
            then(nc.gpsimd.memset(g.ones[:, :], 1.0))
            for i, eps in enumerate((1e-6, 1e-5, LNX_EPS)):
                then(nc.gpsimd.memset(g.eps[:, i:i + 1], eps))
            then(nc.gpsimd.memset(g.sumsq[:, :], 0.0))
            then(nc.gpsimd.memset(g.ones64[:, :], 1.0))
            v = blocks(g.ones64[:, :], 64)
            keep(v, 0, 1, [[-64, 2], [0, 64]])
            keep(v, 63, -1, [[64, 2], [0, 64]])
            then(nc.gpsimd.memset(g.blockmask[:, :], 1.0))
            keep(g.blockmask[:, :], 0, 1, [[-BLK, NB]])
            keep(g.blockmask[:, :], BLK - 1, -1, [[BLK, NB]])
            then(nc.gpsimd.memset(g.reset[:, :], 1.0))
            then(nc.gpsimd.memset(blocks(g.reset[:, :], BLK)[:, :, 0:1], 0.0))
            for m, strict in ((g.before, 1), (g.notafter, 0)):
                then(nc.gpsimd.memset(m[:, :], 1.0))
                v = blocks(m[:, :], BLK)
                keep(v, -strict, -1, [[BLK, NB], [1, BLK]])
                keep(v, 0, 1, [[-BLK, NB], [0, BLK]])
            then(nc.gpsimd.memset(g.after[:, :], 1.0))
            v = blocks(g.after[:, :], BLK)
            keep(v, -1, 1, [[-BLK, NB], [-1, BLK]])
            keep(v, BLK - 1, -1, [[BLK, NB], [0, BLK]])
            for i in range(2):
                then(nc.gpsimd.tensor_copy(g.gram_mask[:, i, 0, :], g.before[:, :]))
                then(nc.gpsimd.tensor_copy(g.gram_mask[:, i, 1, :], g.notafter[:, :]))
            then(nc.gpsimd.memset(g.notafter128[:, :], 1.0))
            keep(g.notafter128[:, :], 0, -1, [[1, P]])
            then(nc.gpsimd.memset(g.after128[:, :], 1.0))
            keep(g.after128[:, :], -1, 1, [[-1, P]])
            then(nc.gpsimd.memset(g.level_mask[:, :, :], 0.0))
            for i, h in enumerate((8, 4, 2, 1)):
                v = g.level_mask[:, i, :].rearrange("p (m u j) -> p m u j", u=2, j=h)[:, :, 1, :]
                then(nc.gpsimd.memset(v, 1.0))
                keep(v, 0, 1, [[-2 * h, P // (2 * h)], [0, h]])
                keep(v, h - 1, -1, [[2 * h, P // (2 * h)], [0, h]])
            then(nc.gpsimd.tensor_copy(g.level_mask[:, 4, :], g.ident[:, :]))


def load_inputs(nc, g, A):
    with Phase(nc, "load") as ph:
        rows_a = ph.sb("rows_a", [P, P])
        rows_b = ph.sb("rows_b", [NROW_B, P])
        c_rows = ph.sb("c_rows", [SEQS, D])
        sc_rows = ph.sb("sc_rows", [SEQS, D])
        shift_rows = ph.sb("shift_rows", [NS, A_COLS])
        conv_rows = ph.sb("conv_rows", [NS * 3, XBC])
        x_rows = ph.sb("x_rows", [P, 2, D])
        zeros = ph.sb("zeros", [P, NAB + 1, HALO])
        pt = ph.ps("pt", [P, 2, 2, BANK])
        pq = ph.ps("pq", [P, 3, BANK])
        (params_in, cond_in, states_in, silu_done, params_T, shift_T, conv_T,
         halo_zero, halo_out, x_in0, x_in1, x_T, x_out_a, x_out_v, small_in) = ph.sems(
            "params_in cond_in states_in silu_done params_T shift_T conv_T "
            "halo_zero halo_out x_in0 x_in1 x_T x_out_a x_out_v small_in")
        x_in = (x_in0, x_in1)
        block = ph.block()

        def rows(eng, dst, at, src, n):
            eng.dma_start(dst[at:at + n, :], src).then_inc(params_in, 16)

        n_params = 3 + len(ROW_B)

        @block.sync
        def _(sp):
            sp.dma_start(c_rows[0:1, :], A["c_prompt"]).then_inc(cond_in, 16)
            sp.dma_start(c_rows[1:SEQS, :], A["c_sample"]).then_inc(cond_in, 16)
            for name, at in ROW_A.items():
                src = A[name].rearrange("l (t p) -> (l t) p", p=P)
                rows(sp, rows_a, at, src, src.shape[0])
            for name, at in ROW_B.items():
                src = A[name]
                if name == "norm_out_w":
                    src = src.rearrange("(t p) -> t p", p=P)
                elif name == "r_k":
                    src = src.rearrange("l (t h) k -> (l t) (h k)", h=2)
                elif name == "conv_w":
                    src = src.rearrange("l w (t p) -> (l w t) p", p=P)
                else:
                    src = src.rearrange("l (t p) -> (l t) p", p=P)
                rows(sp, rows_b, at, src, src.shape[0])
            sp.dma_start(shift_rows[:, :], A["state_rwkv_shift"].rearrange("b l n -> (b l) n")).then_inc(states_in, 16)
            sp.dma_start(conv_rows[:, :], A["state_conv"].rearrange("b l w n -> (b l w) n")).then_inc(states_in, 16)
            xp = A["x_prompt"].rearrange("o (t p) d -> (o t) p d", p=P)

            def load_x(t, u, src, turn):
                if turn is not None:
                    sp.wait_ge(x_T, turn)
                sp.dma_start(x_rows[:, u, :], src).then_inc(x_in[u], 16)
            load_x(0, 0, xp[0], None)
            load_x(1, 1, xp[1], None)
            for t in range(2, NTP):
                load_x(t, t % 2, xp[t], t - 1)
            load_x(NTP, NTP % 2, A["x_sample"].rearrange("b s d -> (b s) d"), NTP - 1)
            sp.wait_ge(halo_zero, 1)
            sp.dma_start(g.pT[0:NAB * P, 0:HALO].rearrange("(j p) c -> p j c", p=P),
                         zeros[:, 0:NAB, :]).then_inc(halo_out, 16)
            sp.wait_ge(halo_out, 16)

        @block.gpsimd
        def _(pool):
            nc.gpsimd.memset(zeros[:, :, :], 0.0).then_inc(halo_zero, 1)
            for h in range(2):
                src = A["d_skip"].rearrange("o (t h) -> (o h) t", h=2)[h:h + 1, :]
                pool.dma_start(g.dskip[64 * h:64 * h + 64, :], src.to_broadcast([64, 8]),
                               allow_slow_non_contiguous=True).then_inc(small_in, 16)
            pool.dma_start(g.dt_bias[:, :], A["dt_bias"].rearrange("o h -> h o"), allow_slow_non_contiguous=True).then_inc(small_in, 16)
            pool.dma_start(g.a_log[:, :], A["a_log"].rearrange("o h -> h o"), allow_slow_non_contiguous=True).then_inc(small_in, 16)
            pool.wait_ge(small_in, 64)

        @block.scalar
        def _(act):
            act.wait_ge(cond_in, 32)
            nc.scalar.activation(sc_rows[:, :], c_rows[:, :], ACT.Silu).then_inc(silu_done, 1)
            for t in range(NT):
                act.wait_ge(x_T, t + 1)
                nc.scalar.copy(g.xT[:, 0:4, t * P:(t + 1) * P],
                               pt[:, t % 2, 0, :].rearrange("p (k c) -> p k c", c=P)).then_inc(x_out_a, 1)

        @block.vector
        def _(dve):
            dve.wait_ge(params_T, 1)
            nc.vector.tensor_copy(g.colA[:, :], pq[:, 0, 0:P])
            nc.vector.tensor_copy(g.colB[:, :], pq[:, 0, P:P + NROW_B])
            dve.wait_ge(shift_T, 1)
            nc.vector.tensor_copy(g.scT[:, :, :], pq[:, 1, 0:KD * SEQS].rearrange("p (k s) -> p k s", s=SEQS))
            nc.vector.tensor_copy(g.shiftT[:, :, :], pq[:, 1, P:P + NA * NS].rearrange("p (k s) -> p k s", s=NS))
            dve.wait_ge(conv_T, 1)
            nc.vector.tensor_copy(g.convT[:, :, :], pq[:, 2, 0:NXBC * NS * 3].rearrange("p (k s) -> p k s", s=NS * 3))
            for t in range(NT):
                dve.wait_ge(x_T, t + 1)
                nc.vector.tensor_copy(g.xT[:, 4:8, t * P:(t + 1) * P],
                                      pt[:, t % 2, 1, :].rearrange("p (k c) -> p k c", c=P)).then_inc(x_out_v, 1)

        @block.tensor
        def _(pe):
            pe.wait_ge(params_in, 16 * n_params)
            nc.tensor.transpose(pq[:, 0, 0:P], rows_a[:, :], g.ident[:, :])
            nc.tensor.transpose(pq[:, 0, P:P + NROW_B], rows_b[:, :], g.ident[0:NROW_B, 0:NROW_B]).then_inc(params_T, 1)
            pe.wait_ge(silu_done, 1)
            for k in range(KD):
                ins = nc.tensor.transpose(pq[:, 1, k * SEQS:(k + 1) * SEQS], sc_rows[:, k * P:(k + 1) * P],
                                          g.ident[0:SEQS, 0:SEQS])
            pe.wait_ge(states_in, 32)
            for j in range(NA):
                ins = nc.tensor.transpose(pq[:, 1, P + j * NS:P + (j + 1) * NS], shift_rows[:, j * P:(j + 1) * P],
                                          g.ident[0:NS, 0:NS])
            ins.then_inc(shift_T, 1)
            for j in range(NXBC):
                ins = nc.tensor.transpose(pq[:, 2, j * 24:(j + 1) * 24], conv_rows[:, j * P:(j + 1) * P],
                                          g.ident[0:24, 0:24])
            ins.then_inc(conv_T, 1)
            for t in range(NT):
                pe.wait_ge(x_in[t % 2], 16 * (t // 2 + 1))
                if t >= 2:
                    pe.wait_ge(x_out_a, t - 1)
                    pe.wait_ge(x_out_v, t - 1)
                for k in range(KD):
                    ins = nc.tensor.transpose(pt[:, t % 2, k // 4, (k % 4) * P:(k % 4 + 1) * P],
                                              x_rows[:, t % 2, k * P:(k + 1) * P], g.ident[:, :])
                ins.then_inc(x_T, 1)


def modulation(nc, g, A):
    GW = 512
    NG = 6 * D // GW
    with Phase(nc, "ada") as ph:
        w = ph.sb("w", [P, 2, KD, GW])
        rows = ph.sb("rows", [SEQS, 2, GW])
        pm = ph.ps("pm", [P, 2, BANK])
        pt = ph.ps("pt", [P, 2, BANK])
        w_in0, w_in1, slot_free, pm_free, pt_free, rows_out, rows_T, waited = ph.sems(
            "w_in0 w_in1 slot_free pm_free pt_free rows_out rows_T waited")
        w_in = (w_in0, w_in1)
        sq = ph.sb("sq", [P, T])
        sq_done, sum_done = ph.sems("sq_done sum_done")
        block = ph.block()
        src = A["ada_w"].rearrange("l (k p) n -> p l k n", p=P)

        @block.gpsimd
        def _(pool):
            for k in range(KD):
                if k:
                    pool.wait_ge(sum_done, k)
                nc.gpsimd.tensor_tensor(sq[:, :], g.xT[:, k, :], g.xT[:, k, :], ALU.mult).then_inc(sq_done, 1)
                pool.wait_ge(sq_done, k + 1)
                nc.gpsimd.tensor_tensor(g.sumsq[:, :], g.sumsq[:, :], sq[:, :], ALU.add).then_inc(sum_done, 1)

        @block.sync
        def _(sp):
            for layer in range(DEPTH):
                with sp.Fori(0, NG // 2) as i:
                    for u in range(2):
                        at = sp.snap((2 * i + u) * GW)
                        turn = sp.snap(2 * i + (u + layer * NG + 1))
                        sp.wait_ge(slot_free, turn)
                        sp.dma_start(w[:, u, :, :], src[:, layer, :, ds(at, GW)]).then_inc(w_in[u], 16)

        @block.tensor
        def _(pe):
            pe.sem_inc(slot_free, 2)
            for layer in range(DEPTH):
                with pe.Fori(0, NG // 2) as i:
                    for u in range(2):
                        turn = pe.snap(2 * i + (u + layer * NG + 1))
                        pe.wait_ge(w_in[u], i * 16 + (layer * NG // 2 + 1) * 16)
                        pe.wait_ge(pm_free, turn)
                        for k in range(KD):
                            ins = nc.tensor.matmul(pm[0:SEQS, u, :], g.scT[:, k, :], w[:, u, k, :],
                                                   start=(k == 0), stop=(k == KD - 1))
                        ins.then_inc(slot_free, 1)
                        pe.wait_ge(rows_out, turn)
                        pe.wait_ge(pt_free, turn)
                        pe.sem_inc(waited, 1)
                        for q in range(GW // P):
                            ins = nc.tensor.transpose(pt[:, u, q * SEQS:(q + 1) * SEQS],
                                                      rows[:, u, q * P:(q + 1) * P], g.ident[0:SEQS, 0:SEQS])
                        ins.then_inc(rows_T, 1)

        @block.scalar
        def _(act):
            act.sem_inc(pm_free, 2)
            for layer in range(DEPTH):
                with act.Fori(0, NG // 2) as i:
                    for u in range(2):
                        act.wait_ge(slot_free, 2 * i + (u + layer * NG + 3))
                        nc.scalar.copy(rows[:, u, :], pm[0:SEQS, u, :]).then_inc(rows_out, 1)
                        act.wait_ge(rows_out, 2 * i + (u + layer * NG + 1))
                        act.sem_inc(pm_free, 1)

        @block.vector
        def _(dve):
            dve.sem_inc(pt_free, 2)
            for layer in range(DEPTH):
                with dve.Fori(0, NG // 2) as i:
                    for u in range(2):
                        at = dve.snap((2 * i + u) * (GW // P) + layer * 6 * KD)
                        dve.wait_ge(rows_T, 2 * i + (u + layer * NG + 1))
                        nc.vector.tensor_tensor(
                            g.mod[:, ds(at, GW // P), :],
                            pt[:, u, 0:GW // P * SEQS].rearrange("p (q s) -> p q s", s=SEQS),
                            bc(g.colA[:, ds(at, GW // P)], 2, SEQS), ALU.add).then_inc(pt_free, 1)
            dve.wait_ge(pt_free, 2 + DEPTH * NG)
            for layer in range(DEPTH):
                for which, name in enumerate(("norm_mix_w", "norm_ffn_w")):
                    at = ROW_A[name] + layer * KD
                    nc.vector.scalar_tensor_tensor(g.scale[:, layer, which, :, :],
                                                   g.modcol(layer, 3 * which + 1), 1.0,
                                                   bc(g.colA[:, at:at + KD], 2, SEQS), ALU.add, ALU.mult)


def rstd_steps(nc, g, block_pe, ss, sems):
    summed, ln_done, rstd_done = sems
    if block_pe is not None:
        for c in range(NCH):
            ins = nc.tensor.matmul(ss[:, c, 0:CH], g.ones[:, :], g.sumsq[:, c * CH:(c + 1) * CH], start=True, stop=True)
        ins.then_inc(summed, 1)
        return

    def scalar_part(act):
        act.wait_ge(summed, 1)
        nc.scalar.activation(ss[:, 0:NCH, 0:CH], ss[:, 0:NCH, 0:CH], ACT.Ln, bias=g.eps[:, 0:1], scale=1.0 / D).then_inc(ln_done, 1)
        act.wait_ge(ln_done, 1)
        nc.scalar.activation(ss[:, 0:NCH, 0:CH], ss[:, 0:NCH, 0:CH], ACT.Exp, scale=-0.5).then_inc(rstd_done, 1)
    return scalar_part


class Norm:

    def __init__(self, nc, g, ph, layer, which, ss):
        self.nc, self.g, self.ss = nc, g, ss
        self.sc, self.sh = g.scale[:, layer, which, :, :], g.modcol(layer, 3 * which)
        self.m = ph.sb("norm_m", [P, 2, TP])
        self.ms = ph.sb("norm_ms", [P, KD, NS * LS])
        (self.summed, self.ln_done, self.rstd_done, self.m_done, self.hi_done, self.ready, self.ms_done,
         self.ms_step, self.samples_ready) = ph.sems(
            "summed ln_done rstd_done m_done hi_done ready ms_done ms_step samples_ready")

    def tensor(self):
        rstd_steps(self.nc, self.g, True, self.ss, (self.summed, None, None))

    def scalar(self, act):
        nc, g = self.nc, self.g
        rstd_steps(nc, g, None, self.ss, (self.summed, self.ln_done, self.rstd_done))(act)
        for k in range(KD):
            act.wait_ge(self.m_done, k + 1)
            nc.scalar.activation(g.hH[:, k, 0:TP], self.m[:, k % 2, :], ACT.Identity, bias=self.sh[:, k, 0:1]
                                 ).then_inc(self.hi_done, 1)

    def vector(self, dve):
        nc, g = self.nc, self.g
        dve.wait_ge(self.rstd_done, 1)
        two = 2 * CH

        def scaled(k):
            if k >= 2:
                dve.wait_ge(self.ready, k - 1)
            for lo, hi, part in ((0, two, self.ss[:, 0:2, 0:CH]), (two, TP, self.ss[:, 2:3, 0:TP - two])):
                n = part.shape[2]
                ins = nc.vector.scalar_tensor_tensor(
                    self.m[:, k % 2, lo:hi].rearrange("p (c n) -> p c n", n=n),
                    g.xT[:, k, lo:hi].rearrange("p (c n) -> p c n", n=n), self.sc[:, k, 0:1], part, ALU.mult, ALU.mult)
            ins.then_inc(self.m_done, 1)

        def low(k):
            dve.wait_ge(self.hi_done, k + 1)
            nc.vector.scalar_tensor_tensor(g.hL[:, k, 0:TP], self.m[:, k % 2, :], self.sh[:, k, 0:1],
                                           g.hH[:, k, 0:TP].bitcast(F32), ALU.add, ALU.subtract
                                           ).then_inc(self.ready, 1)
        scaled(0)
        nc.vector.tensor_tensor(self.ms[:, :, :], g.xT[:, :, TP:T],
                                bc(self.ss[:, 2, TP - two:CH], 1, KD), ALU.mult).then_inc(self.ms_done, 1)
        for k in range(KD):
            if k + 1 < KD:
                scaled(k + 1)
            low(k)

    def pool(self, pool):
        nc, g = self.nc, self.g
        v = self.ms[:, :, :].rearrange("p k (s t) -> p k s t", t=LS)
        pool.wait_ge(self.ms_done, 1)
        for i, (col, op) in enumerate(((self.sc, ALU.mult), (self.sh, ALU.add))):
            for k in range(KD):
                ins = nc.gpsimd.tensor_tensor(v[:, k], v[:, k], bc(col[:, k, 1:SEQS], 2, LS), op)
            ins.then_inc(self.ms_step, 1)
            pool.wait_ge(self.ms_step, i + 1)
        nc.gpsimd.tensor_copy(g.hH[:, :, TP:T], self.ms[:, :, :]).then_inc(self.ms_step, 1)
        pool.wait_ge(self.ms_step, 3)
        nc.gpsimd.tensor_tensor(g.hL[:, :, TP:T], self.ms[:, :, :], g.hH[:, :, TP:T].bitcast(F32),
                                ALU.subtract).then_inc(self.samples_ready, 1)


class Ring:
    def __init__(self, nc, ph, kt):
        self.nc = nc
        self.raw = ph.sb("raw", [P, 2, kt, P])
        self.wH = ph.sb("wH", [P, 2, kt, P], F32R)
        self.wL = ph.sb("wL", [P, 2, kt, P], F32R)
        self.acc = ph.ps("acc", [P, 2, 4, BANK])
        names = ph.sems("raw_in0 raw_in1 hi_half0 hi_half1 split0 split1 mult0 mult1 used0 used1 held")
        self.raw_in, self.hi_half, self.split, self.mult, self.used = (names[i:i + 2] for i in range(0, 10, 2))
        self.held = names[10]

    def load(self, sp, s, u, kt, src, at, cols=P):
        at = reg(sp, at)
        if not is_zero(s):
            sp.wait_ge(self.split[u], s)
        sp.dma_start(self.raw[:, u, 0:kt, 0:cols], src[:, :, ds(at, cols)]).then_inc(self.raw_in[u], 16)

    def split_step(self, pool, s, u, kt, cols=P):
        nc = self.nc
        raw, wH, wL = (t[:, u, 0:kt, 0:cols] for t in (self.raw, self.wH, self.wL))
        pool.wait_ge(self.raw_in[u], s * 16 + 16)
        pool.sem_inc(self.held, 1)
        if not is_zero(s):
            pool.wait_ge(self.mult[u], s)
            pool.sem_inc(self.held, 1)
        nc.gpsimd.tensor_copy(wH, raw).then_inc(self.hi_half[u], 1)
        pool.wait_ge(self.hi_half[u], s + 1)
        nc.gpsimd.tensor_tensor(wL, raw, wH.bitcast(F32), ALU.subtract).then_inc(self.split[u], 1)

    def multiply(self, pe, s, u, kt, xH, xL, before=None, groups=((0, 1, 2),), rows=P):
        nc = self.nc
        pe.wait_ge(self.split[u], s + 1)
        if not is_zero(s):
            pe.wait_ge(self.used[u], s)
        for chunks in groups:
            for k in range(kt):
                if before:
                    before(chunks, k)
                for w, xs in ((self.wH, (xH, xL)), (self.wL, (xH,))):
                    for c in chunks:
                        for x in xs:
                            ins = nc.tensor.matmul(self.acc[0:rows, u, c, 0:CH], w[:, u, k, 0:rows],
                                                   x[:, k, c * CH:(c + 1) * CH],
                                                   start=(k == 0 and w is self.wH and x is xH),
                                                   stop=(k == kt - 1 and w is self.wL))
        ins.then_inc(self.mult[u], 1)


def is_zero(s):
    return isinstance(s, int) and s == 0


def reg(eng, value):
    return value if isinstance(value, int) else eng.snap(value)


def steps(eng, first, n, body):
    if first == 0 or n == 1:
        body(first)
        if n > 1:
            steps(eng, first + 1, n - 1, body)
    elif n > 1:
        with eng.Fori(first, first + n) as s:
            body(s)


def wait_for_norm(pe, norm):
    def before(chunks, k):
        pe.wait_ge(norm.ready, k + 1)
        if chunks == (2,) and k == 0:
            pe.wait_ge(norm.samples_ready, 1)
    return dict(before=before, groups=((0, 1), (2,)))


def project_to_dram(nc, g, weights, n_cols, layer, name, tails):
    n_steps, rest = n_cols // (2 * P), n_cols % (2 * P)
    with Phase(nc, name) as ph:
        ring = Ring(nc, ph, KD)
        acc, mult, used = ring.acc, ring.mult, ring.used
        norm = Norm(nc, g, ph, layer, 0, acc[:, 1])
        out = ph.sb("out", [P, 2, T])
        stored0, stored1, tail_done = ph.sems("stored0 stored1 tail_done")
        stored = (stored0, stored1)
        block = ph.block()
        src = weights.rearrange("(k p) n -> p k n", p=P)

        @block.sync
        def _(sp):
            def load(s):
                for u in range(2):
                    ring.load(sp, s, u, KD, src, (s * 2 + u) * P)
            steps(sp, 0, n_steps, load)
            if rest:
                ring.load(sp, n_steps, 0, KD, src, n_steps * 2 * P, rest)

        @block.gpsimd
        def _(pool):
            ring.split_step(pool, 0, 0, KD)
            norm.pool(pool)
            ring.split_step(pool, 0, 1, KD)

            def split(s):
                for u in range(2):
                    ring.split_step(pool, s, u, KD)
            steps(pool, 1, n_steps - 1, split)
            if rest:
                ring.split_step(pool, n_steps, 0, KD, rest)

        @block.tensor
        def _(pe):
            norm.tensor()
            ring.multiply(pe, 0, 0, KD, g.hH, g.hL, **wait_for_norm(pe, norm))
            ring.multiply(pe, 0, 1, KD, g.hH, g.hL)

            def multiply(s):
                for u in range(2):
                    ring.multiply(pe, s, u, KD, g.hH, g.hL)
            steps(pe, 1, n_steps - 1, multiply)
            if rest:
                ring.multiply(pe, n_steps, 0, KD, g.hH, g.hL, rows=rest)

        @block.scalar
        def _(act):
            norm.scalar(act)

            def store(s):
                for u in range(2):
                    row = reg(act, (s * 2 + u) * P)
                    act.wait_ge(mult[u], s + 1)
                    if not is_zero(s):
                        act.wait_ge(stored[u], s * 16)
                    if tails and not is_zero(s):
                        act.wait_ge(tail_done, s * 2 + (u - 1))
                    nc.scalar.copy(out[:, u, :].rearrange("p (c n) -> p c n", n=CH),
                                   acc[:, u, 0:NCH, 0:CH]).then_inc(used[u], 1)
                    act.wait_ge(used[u], s + 1)
                    act.dma_start(g.pT[ds(row, P), HALO:HALO + T], out[:, u, :]).then_inc(stored[u], 16)
            store(0)
            steps(act, 1, n_steps - 1, store)
            if rest:
                act.wait_ge(mult[0], n_steps + 1)
                act.wait_ge(stored0, 16 * n_steps)
                if tails:
                    act.wait_ge(tail_done, 2 * n_steps - 1)
                nc.scalar.copy(out[0:rest, 0, :].rearrange("p (c n) -> p c n", n=CH),
                               acc[0:rest, 0, 0:NCH, 0:CH]).then_inc(used[0], 1)
                act.wait_ge(used[0], n_steps + 1)
                act.dma_start(g.pT[n_steps * 2 * P:n_cols, HALO:HALO + T], out[0:rest, 0, :]).then_inc(stored0, 16)
            act.wait_ge(stored0, 16 * (n_steps + (rest > 0)))
            act.wait_ge(stored1, 16 * n_steps)

        @block.vector
        def _(dve):
            norm.vector(dve)
            if not tails:
                return

            def tail(s):
                for u in range(2):
                    tile = reg(dve, s * 2 + u)
                    dve.wait_ge(used[u], s + 1)
                    nc.vector.tensor_copy(g.tails[:, ds(tile, 1), 0:TAIL].rearrange("p o c -> p (o c)"),
                                          out[:, u, TP - TAIL:TP])
                    nc.vector.tensor_copy(
                        g.tails[:, ds(tile, 1), TAIL:SEQS * TAIL].rearrange("p o (s c) -> p (o s) c", c=TAIL),
                        out[:, u, TP:T].rearrange("p (s t) -> p s t", t=LS)[:, :, LS - TAIL:LS]
                    ).then_inc(tail_done, 1)
            steps(dve, 0, n_steps, tail)


class GatedAdd:

    def __init__(self, nc, g, ph, ring, gate, sq):
        self.nc, self.g, self.ring, self.gate, self.sq = nc, g, ring, gate, sq
        self.tmp = ph.sb("tmp", [P, 2, NS * LS])
        self.added, self.sq_done, self.sum_done = ph.sems("added sq_done sum_done")

    def vector(self, dve, s, u, first, before, last):
        nc, g, acc, gate = self.nc, self.g, self.ring.acc, self.gate
        n = reg(dve, (s + (-first)) * 2 + u)
        dve.wait_ge(self.ring.mult[u], s + 1)
        two = 2 * CH
        for lo, hi, part, m in ((0, two, acc[:, u, 0:2, 0:CH], CH),
                                (two, TP, acc[:, u, 2:3, 0:TP - two], TP - two)):
            xs = g.xT[:, ds(n, 1), lo:hi].rearrange("p o (c n) -> p (o c) n", n=m)
            nc.vector.scalar_tensor_tensor(xs, part, gate[:, ds(n, 1), 0:1].rearrange("p o s -> p (o s)"),
                                           xs, ALU.mult, ALU.add)
        turn = (s + (-first)) * 2 + u
        if not (isinstance(turn, int) and before + turn < 2):
            dve.wait_ge(self.added, turn + (before - 1))
        gs = bc(gate[:, ds(n, 1), 1:SEQS].rearrange("p o s -> p (o s)"), 2, LS)
        nc.vector.tensor_tensor(self.tmp[:, u, :].rearrange("p (s t) -> p s t", t=LS),
                                acc[:, u, 2, TP - two:CH].rearrange("p (s t) -> p s t", t=LS),
                                gs, ALU.mult).then_inc(self.ring.used[u], 1)
        dve.wait_ge(self.ring.used[u], s + 1)
        xs = g.xT[:, ds(n, 1), TP:T].rearrange("p o c -> p (o c)")
        nc.vector.tensor_tensor(xs, xs, self.tmp[:, u, :], ALU.add).then_inc(self.added, 1)
        if last:
            x = g.xT[:, ds(n, 1), :].rearrange("p o c -> p (o c)")
            dve.wait_ge(self.added, turn + (before + 1))
            if not is_zero(turn):
                dve.wait_ge(self.sum_done, turn)
            nc.vector.tensor_tensor(self.sq, x, x, ALU.mult).then_inc(self.sq_done, 1)
            dve.wait_ge(self.sq_done, turn + 1)
            nc.vector.tensor_tensor(g.sumsq[:, :], g.sumsq[:, :], self.sq, ALU.add).then_inc(self.sum_done, 1)


def mixer_out(nc, g, weights, parts, gate, name):
    kt = max(parts)
    with Phase(nc, name) as ph:
        ring = Ring(nc, ph, kt)
        aH, aL = ph.sb("aH", [P, kt, T], F32R), ph.sb("aL", [P, kt, T], F32R)
        sq = ph.sb("sq", [P, T])
        add = GatedAdd(nc, g, ph, ring, gate, sq[:, :])
        hi_done, lo_done = ph.sems("hi_done lo_done")
        block = ph.block()
        half = KD // 2
        table = []
        for i, n in enumerate(parts):
            table.append((sum(parts[:i]), n, i * half))

        @block.sync
        def _(sp):
            for k0, n, first in table:
                src = weights[k0 * P:(k0 + n) * P, :].rearrange("(k p) n -> p k n", p=P)

                def load(s):
                    for u in range(2):
                        ring.load(sp, s, u, n, src, ((s + (-first)) * 2 + u) * P)
                steps(sp, first, half, load)

        @block.gpsimd
        def _(pool):
            for k0, n, first in table:
                def split(s):
                    for u in range(2):
                        ring.split_step(pool, s, u, n)
                steps(pool, first, half, split)

        @block.tensor
        def _(pe):
            for k0, n, first in table:
                def before(chunks, k):
                    pe.wait_ge(lo_done, k0 + k + 1)

                def multiply(s):
                    for u in range(2):
                        ring.multiply(pe, s, u, n, aH, aL)
                ring.multiply(pe, first, 0, n, aH, aL, before)
                ring.multiply(pe, first, 1, n, aH, aL)
                steps(pe, first + 1, half - 1, multiply)

        @block.scalar
        def _(act):
            for k0, n, first in table:
                if first:
                    act.wait_ge(ring.mult[1], first)
                for k in range(n):
                    nc.scalar.copy(aH[:, k, :], g.act[:, k0 + k, :]).then_inc(hi_done, 1)

        @block.vector
        def _(dve):
            nc.vector.memset(g.sumsq[:, :], 0.0)
            for k0, n, first in table:
                for k in range(n):
                    dve.wait_ge(hi_done, k0 + k + 1)
                    nc.vector.tensor_tensor(aL[:, k, :], g.act[:, k0 + k, :], aH[:, k, :].bitcast(F32),
                                            ALU.subtract).then_inc(lo_done, 1)
                last = first == table[-1][2]

                def add_tiles(s):
                    for u in range(2):
                        add.vector(dve, s, u, first, first * 2, last)
                add_tiles(first)
                steps(dve, first + 1, half - 1, add_tiles)


def ffn(nc, g, A, layer):
    parts = (5, 5, 4, 4, 4)
    kt, half = max(parts), KD // 2
    table = []
    for n in parts:
        k0 = sum(r[1] for r in table)
        table.append((k0, n, k0 + half * len(table), k0 + half * len(table) + n))
    with normed_x(nc, g), Phase(nc, f"ffn{layer}") as ph:
        ring = Ring(nc, ph, KD)
        acc, mult, used = ring.acc, ring.mult, ring.used
        norm = Norm(nc, g, ph, layer, 1, acc[:, 1])
        uH, uL = ph.sb("uH", [P, kt, T], F32R), ph.sb("uL", [P, kt, T], F32R)
        sil = norm_m_as_tile(norm)
        add = GatedAdd(nc, g, ph, ring, g.modcol(layer, 5), sil)
        rounded, hidden = ph.sems("rounded hidden")
        block = ph.block()
        sil3 = sil.rearrange("p (c n) -> p c n", n=CH)

        @block.sync
        def _(sp):
            for k0, n, up, down in table:
                def load_up(s):
                    for u, name in enumerate(("w_gate", "w_up")):
                        ring.load(sp, s, u, KD, A[name][layer].rearrange("(k p) n -> p k n", p=P),
                                  (s + (k0 - up)) * P)
                steps(sp, up, n, load_up)
                src = A["w_down"][layer, k0 * P:(k0 + n) * P, :].rearrange("(k p) n -> p k n", p=P)

                def load_down(s):
                    for u in range(2):
                        ring.load(sp, s, u, n, src, ((s + (-down)) * 2 + u) * P)
                steps(sp, down, half, load_down)

        @block.gpsimd
        def _(pool):
            for k0, n, up, down in table:
                def split_up(s):
                    for u in range(2):
                        ring.split_step(pool, s, u, KD)

                def split_down(s):
                    for u in range(2):
                        ring.split_step(pool, s, u, n)
                if up == 0:
                    ring.split_step(pool, 0, 0, KD)
                    norm.pool(pool)
                    ring.split_step(pool, 0, 1, KD)
                    steps(pool, 1, n - 1, split_up)
                else:
                    steps(pool, up, n, split_up)
                steps(pool, down, half, split_down)

        @block.tensor
        def _(pe):
            norm.tensor()
            for k0, n, up, down in table:
                def multiply_up(s):
                    for u in range(2):
                        ring.multiply(pe, s, u, KD, g.hH, g.hL)

                def before(chunks, k):
                    if k == 0:
                        pe.wait_ge(hidden, k0 + n - 1)
                    if k == n - 1:
                        pe.wait_ge(hidden, k0 + n)

                def multiply_down(s):
                    for u in range(2):
                        ring.multiply(pe, s, u, n, uH, uL)
                if up == 0:
                    ring.multiply(pe, 0, 0, KD, g.hH, g.hL, **wait_for_norm(pe, norm))
                    ring.multiply(pe, 0, 1, KD, g.hH, g.hL)
                    steps(pe, 1, n - 1, multiply_up)
                else:
                    steps(pe, up, n, multiply_up)
                ring.multiply(pe, down, 0, n, uH, uL, before)
                ring.multiply(pe, down, 1, n, uH, uL)
                steps(pe, down + 1, half - 1, multiply_down)

        @block.scalar
        def _(act):
            norm.scalar(act)
            act.wait_ge(norm.ready, KD)
            for k0, n, up, down in table:
                def silu(s):
                    act.wait_ge(mult[0], s + 1)
                    if not is_zero(s):
                        act.wait_ge(hidden, s + (k0 - up))
                    nc.scalar.activation(sil3, acc[:, 0, 0:NCH, 0:CH], ACT.Silu).then_inc(used[0], 1)
                steps(act, up, n, silu)

        @block.vector
        def _(dve):
            norm.vector(dve)
            nc.vector.memset(g.sumsq[:, :], 0.0)
            for k0, n, up, down in table:
                def hidden_tile(s):
                    at = reg(dve, s + (-up))
                    dve.wait_ge(mult[1], s + 1)
                    dve.wait_ge(used[0], s + 1)
                    nc.vector.tensor_tensor(sil3, acc[:, 1, 0:NCH, 0:CH], sil3, ALU.mult).then_inc(used[1], 1)
                    dve.wait_ge(used[1], s + 1)
                    hi = uH[:, ds(at, 1), :].rearrange("p o c -> p (o c)")
                    nc.vector.tensor_copy(hi, sil).then_inc(rounded, 1)
                    dve.wait_ge(rounded, s + (k0 - up + 1))
                    nc.vector.tensor_tensor(uL[:, ds(at, 1), :].rearrange("p o c -> p (o c)"), sil,
                                            hi.bitcast(F32), ALU.subtract).then_inc(hidden, 1)
                steps(dve, up, n, hidden_tile)
                last = k0 == table[-1][0]
                before = (up - k0) * 2

                def add_tiles(s):
                    for u in range(2):
                        add.vector(dve, s, u, down, before, last)
                add_tiles(down)
                steps(dve, down + 1, half - 1, add_tiles)


def norm_m_as_tile(norm):
    return norm.m[:, :, :].rearrange("p a b -> p (a b)")[:, 0:T]


def write_y(nc, g, y_prompt, y_sample):
    with Phase(nc, "out") as ph:
        h = ph.sb("h", [P, KD, T])
        rows = ph.sb("rows", [P, 2, D])
        ss = ph.ps("ss", [P, 4, BANK])
        pt = ph.ps("pt", [P, 2, 2, BANK])
        rstd_sems = ph.sems("summed ln_done rstd_done")
        scaled, turned, copied_a, copied_v, out0, out1 = ph.sems("scaled turned copied_a copied_v out0 out1")
        outs = (out0, out1)
        block = ph.block()
        yp = y_prompt.rearrange("o (t p) d -> (o t) p d", p=P)
        ys = y_sample.rearrange("b s d -> (b s) d")

        @block.scalar
        def _(act):
            rstd_steps(nc, g, None, ss, rstd_sems)(act)
            for t in range(NT):
                act.wait_ge(turned, t + 1)
                if t >= 2:
                    act.wait_ge(outs[t % 2], 16 * (t // 2))
                nc.scalar.copy(rows[:, t % 2, 0:512], pt[:, t % 2, 0, :]).then_inc(copied_a, 1)

        @block.tensor
        def _(pe):
            rstd_steps(nc, g, True, ss, rstd_sems)
            for t in range(NT):
                pe.wait_ge(scaled, KD * (t // 3 + 1))
                if t >= 2:
                    pe.wait_ge(copied_a, t - 1)
                    pe.wait_ge(copied_v, t - 1)
                for k in range(KD):
                    ins = nc.tensor.transpose(pt[:, t % 2, k // 4, (k % 4) * P:(k % 4 + 1) * P],
                                              h[:, k, t * P:(t + 1) * P], g.ident[:, :])
                ins.then_inc(turned, 1)

        @block.vector
        def _(dve):
            dve.wait_ge(rstd_sems[2], 1)

            def scale_chunk(c):
                for k in range(KD):
                    at = ROW_B["norm_out_w"] + k
                    nc.vector.scalar_tensor_tensor(h[:, k, c * CH:(c + 1) * CH], g.xT[:, k, c * CH:(c + 1) * CH],
                                                   g.colB[:, at:at + 1], ss[:, c, 0:CH],
                                                   ALU.mult, ALU.mult).then_inc(scaled, 1)
            scale_chunk(0)
            for c in range(NCH):
                if c + 1 < NCH:
                    scale_chunk(c + 1)
                for t in range(3 * c, 3 * c + 3):
                    dve.wait_ge(turned, t + 1)
                    if t >= 2:
                        dve.wait_ge(outs[t % 2], 16 * (t // 2))
                    nc.vector.tensor_copy(rows[:, t % 2, 512:D], pt[:, t % 2, 1, :]).then_inc(copied_v, 1)

        @block.sync
        def _(sp):
            for t in range(NT):
                sp.wait_ge(copied_a, t + 1)
                sp.wait_ge(copied_v, t + 1)
                sp.dma_start(yp[t] if t < NTP else ys, rows[:, t % 2, :]).then_inc(outs[t % 2], 16)
            sp.wait_ge(out0, 16 * 5)
            sp.wait_ge(out1, 16 * 4)


def new_shift_conv(nc, g, shift_p, conv_p, shift_s, conv_s):
    with Phase(nc, "tails") as ph:
        shift_rows = ph.sb("shift_rows", [SEQS, A_COLS])
        conv_rows = ph.sb("conv_rows", [SEQS * TAIL, XBC])
        pt = ph.ps("pt", [P, 8, BANK])
        turned, copied, stored = ph.sems("turned copied stored")
        block = ph.block()

        @block.tensor
        def _(pe):
            for j in range(NA):
                last = g.tails[:, j, :].rearrange("p (s c) -> p s c", c=TAIL)[:, :, TAIL - 1]
                nc.tensor.transpose(pt[0:SEQS, j // 4, (j % 4) * P:(j % 4 + 1) * P], last, g.ident[:, :])
            for j in range(NXBC):
                ins = nc.tensor.transpose(pt[0:SEQS * TAIL, 4 + j // 4, (j % 4) * P:(j % 4 + 1) * P],
                                          g.tails[:, JX + j, :], g.ident[:, :])
            ins.then_inc(turned, 1)

        @block.vector
        def _(dve):
            dve.wait_ge(turned, 1)
            for b in range(4):
                n = min(BANK, A_COLS - b * BANK)
                nc.vector.tensor_copy(shift_rows[:, b * BANK:b * BANK + n], pt[0:SEQS, b, 0:n])
            for b in range(3):
                ins = nc.vector.tensor_copy(conv_rows[:, b * BANK:(b + 1) * BANK], pt[0:SEQS * TAIL, 4 + b, :])
            ins.then_inc(copied, 1)

        @block.sync
        def _(sp):
            sp.wait_ge(copied, 1)
            sp.dma_start(shift_p[0], shift_rows[0:1, :]).then_inc(stored, 16)
            sp.dma_start(shift_s.rearrange("b l n -> (b l) n"), shift_rows[1:SEQS, :]).then_inc(stored, 16)
            sp.dma_start(conv_p.rearrange("b l w n -> (b l w) n"), conv_rows[0:TAIL, :]).then_inc(stored, 16)
            sp.dma_start(conv_s.rearrange("b l w n -> (b l w) n"), conv_rows[TAIL:SEQS * TAIL, :]).then_inc(stored, 16)
            sp.wait_ge(stored, 64)


class Turn:

    def __init__(self, eng, t):
        self.eng, self.t, self.kept = eng, t, {}

    def at(self, n, k=None):
        k = n if k is None else k
        if isinstance(self.t, int):
            return self.t * n + k
        if n > 8:
            return self.t * n + k
        if (n, k) not in self.kept:
            self.kept[n, k] = self.eng.snap(self.t * n + k)
        return self.kept[n, k]

    def wait(self, sem, n=1, k=None):
        self.eng.wait_ge(sem, self.at(n, k))

    def col(self, width, base=0):
        v = self.t * width + base
        return v if isinstance(v, int) else self.eng.snap(v)


def each_tile(eng, body):
    with eng.Fori(0, NTP) as t:
        body(Turn(eng, t), False)
    body(Turn(eng, NTP), True)


def held(tn, waited, sem, n=1, k=None):
    tn.wait(sem, n, k)
    tn.eng.sem_inc(waited, 1)


HA, HDA = 8, 64
PAIRS = HA // 2
GRP = 2
HG = HA // GRP
JG_ = PAIRS // GRP


def rwkv_states_in(nc, g, A, S):
    with Phase(nc, "rw_in") as ph:
        rows = ph.sb("rows", [HDA, NS, HA * HDA])
        pt = ph.ps("pt", [P, 8, BANK])
        loaded, turned = ph.sems("loaded turned")
        block = ph.block()

        @block.sync
        def _(sp):
            for b in range(NS):
                sp.dma_start(rows[:, b, :].rearrange("v (h k) -> v h k", k=HDA),
                             A["state_rwkv"][b, 0].rearrange("h v k -> v h k")).then_inc(loaded, 16)

        @block.tensor
        def _(pe):
            pe.wait_ge(loaded, 16 * NS)
            for b in range(NS):
                for j in range(PAIRS):
                    ins = nc.tensor.transpose(pt[:, b, j * HDA:(j + 1) * HDA], rows[:, b, j * P:(j + 1) * P],
                                              g.ident[0:HDA, 0:HDA])
            ins.then_inc(turned, 1)

        @block.vector
        def _(dve):
            dve.wait_ge(turned, 1)
            nc.vector.tensor_copy(S[:, 0:NS, :, :].rearrange("p b j v -> p b (j v)"), pt[:, :, 0:PAIRS * HDA])


def rwkv_states_out(nc, g, S, dsts, name):
    n = len(dsts)
    with Phase(nc, name) as ph:
        rows = ph.sb("rows", [HDA, n, HA * HDA])
        pt = ph.ps("pt", [HDA, n, BANK])
        turned, copied, stored = ph.sems("turned copied stored")
        block = ph.block()

        @block.tensor
        def _(pe):
            for b in range(n):
                for j in range(PAIRS):
                    ins = nc.tensor.transpose(pt[:, b, j * P:(j + 1) * P], S[:, b, j, :], g.ident[:, :])
            ins.then_inc(turned, 1)

        @block.vector
        def _(dve):
            dve.wait_ge(turned, 1)
            nc.vector.tensor_copy(rows[:, :, :], pt[:, :, :]).then_inc(copied, 1)

        @block.sync
        def _(sp):
            sp.wait_ge(copied, 1)
            for b, dst in enumerate(dsts):
                sp.dma_start(dst.rearrange("h v k -> v h k"),
                             rows[:, b, :].rearrange("v (h k) -> v h k", k=HDA)).then_inc(stored, 16)
            sp.wait_ge(stored, 16 * n)


def rwkv(nc, g, A, out_p, out_s):
    with ExitStack() as outer:
        S = outer.enter_context(nc.sbuf_tensor("rw_S", [P, NB + 1, PAIRS, HDA], F32))
        S_samples = outer.enter_context(nc.sbuf_tensor("rw_S_samples", [P, NS, PAIRS, HDA], F32))
        rwkv_states_in(nc, g, A, S_samples)
        rwkv_tiles(nc, g, A, S, S_samples)
        rwkv_states_out(nc, g, S[:, NB:NB + 1, :, :], [out_p[0, 0]], "rw_outp")
        rwkv_states_out(nc, g, S_samples, [out_s[b, 0] for b in range(NS)], "rw_outs")


def rwkv_tiles(nc, g, A, S, S_samples):
    with Phase(nc, "rwkv") as ph:
        W4 = PAIRS * P

        def arr(name):
            return ph.sb(name, [P, PAIRS, P])
        raw = ph.sb("raw", [P, NA, 1 + P])
        diff = ph.sb("diff", [P, NA, P])
        mixed = ph.sb("mixed", [P, NA, P])
        w2 = ph.sb("w2", [P, WA])
        g2 = ph.sb("g2", [P, WA])
        one_minus_ka = ph.sb("one_minus_ka", [P, PAIRS])
        sig, a_, gl, c_, cprev, dinv, dcum = map(arr, "sig a gl c cprev dinv dcum".split())
        kmod, ba, bt, kt, kend, rk = map(arr, "kmod ba bt kt kend rk".split())
        crem = arr("crem")
        AR = ph.sb("AR", [P, PAIRS, 2, P])
        kk, kinv, kk2 = diff[:, 0:4, :], diff[:, 4:8, :], diff[:, 8:12, :]
        tanh_in = ph.sb("tanh_in", [HDA, P])
        sig_in = ph.sb("sig_in", [P, P])
        X = ph.sb("X", [P, HA, P])
        v_tok, b_tok, k_tok = (ph.sb(n, [P, HA, HDA]) for n in ("v_tok", "b_tok", "k_tok"))
        MT = arr("MT")
        eye = ph.sb("eye", [P, HDA])
        Dg = ph.sb("Dg", [P, JG_, NB, HDA])
        room = g.act[:, PAIRS:KACT, :].rearrange("p a b -> p (a b)")
        used = [0]

        def carve(*shape):
            n = math.prod(shape)
            v = room[:, used[0]:used[0] + n]
            used[0] += n
            names = " ".join(f"d{i}" for i in range(len(shape)))
            return v.rearrange(f"p ({names}) -> p {names}", **{f"d{i}": s for i, s in enumerate(shape)})
        b_msk, k_msk = carve(HG, NB, HDA), carve(HG, NB, HDA)
        GM = carve(HG, 4, P)
        AM = carve(HG, P)
        pw = carve(HG, 4, P)
        GT = g.sumsq[:, 0:JG_ * NB * HDA].rearrange("p (a b c) -> p a b c", b=NB, c=HDA)
        bank = [ph.ps(f"bank{i}", [P, BANK]) for i in range(8)]
        (loaded, weights_in, raw_free, diff_done, mixed_done, lora_in, lora_done, sig_done, gates_done, kk_done,
         kk2_done, ss_done, ssinv1, ssinv2, kinv_done, kkn_done, c_done, cprev_done, crem_done, exps_done, am1, am2,
         kmod_done, ba_done, rk1, rk_done, tilde_done, kend_done, T_done, tok_done, msk_done, msk_b) = ph.sems(
            "loaded weights_in raw_free diff_done mixed_done lora_in lora_done sig_done gates_done kk_done "
            "kk2_done ss_done ssinv1 ssinv2 kinv_done kkn_done c_done cprev_done crem_done exps_done am1 am2 "
            "kmod_done ba_done rk1 rk_done tilde_done kend_done T_done tok_done msk_done msk_b")
        (gram_done, gm_done, S1_done, S2_done, S3_done, S4_done, S5_done, pw1, pw2, pw3, x1, x2, x3, x4, x5,
         M_done, MT_done, GT_mm, GT_done, state_in, chain_mm, chained, O_done, o_done, mean_done, oc_done,
         sq_done, var_done, var1, rs_done, normed, affine_done, bonus_done, bonus_mul, summed_, out_done,
         saved, waited, eye_done, Dg_done) = ph.sems(
            "gram_done gm_done S1_done S2_done S3_done S4_done S5_done pw1 pw2 pw3 x1 x2 x3 x4 x5 "
            "M_done MT_done GT_mm GT_done state_in chain_mm chained O_done o_done mean_done oc_done "
            "sq_done var_done var1 rs_done normed affine_done bonus_done bonus_mul summed out_done "
            "saved waited eye_done Dg_done")
        block = ph.block()
        r_, k_, v_ = mixed[:, JR:JR + 4, :], mixed[:, JK:JK + 4, :], mixed[:, JV:JV + 4, :]
        col = lambda name, n=PAIRS: g.colB[:, ROW_B[name]:ROW_B[name] + n]
        flat = lambda ap: ap.rearrange("p j c -> p (j c)")
        blocks = lambda ap: ap.rearrange("p j (b c) -> p (j b) c", c=BLK)
        o_, oc, sq = bt, kt, ba

        @block.sync
        def _(sp):
            sp.dma_start(w2[0:64, :], A["w2"][0]).then_inc(weights_in, 16)
            sp.dma_start(w2[64:128, :], A["a2"][0]).then_inc(weights_in, 16)
            sp.dma_start(g2[:, :], A["g2"][0]).then_inc(weights_in, 16)
            src = g.pT[0:NA * P, :].rearrange("(j p) c -> p j c", p=P)

            def load(tn, sample):
                at = tn.col(P, HALO - 1)
                tn.wait(raw_free)
                sp.dma_start(raw[:, :, :], src[:, :, ds(at, P + 1)]).then_inc(loaded, 16)
            each_tile(sp, load)

        @block.scalar
        def _(act):
            def tile(tn, sample):
                at = tn.col(P)
                tn.wait(mixed_done)
                nc.scalar.activation(tanh_in[:, :], mixed[0:64, JWA, :], ACT.Tanh)
                nc.scalar.activation(sig_in[:, :], mixed[:, JG, :], ACT.Sigmoid).then_inc(lora_in, 1)
                tn.wait(lora_done)
                for j in range(PAIRS):
                    ins = nc.scalar.activation(sig[:, j, :], bank[0][:, j * P:(j + 1) * P], ACT.Sigmoid,
                                               bias=col("w0")[:, j:j + 1])
                ins.then_inc(sig_done, 1)
                for j in range(PAIRS):
                    nc.scalar.activation(a_[:, j, :], bank[1][:, j * P:(j + 1) * P], ACT.Sigmoid,
                                         bias=col("a0")[:, j:j + 1])
                nc.scalar.copy(flat(gl[:, :, :]), bank[2][:, :]).then_inc(gates_done, 1)
                tn.wait(ssinv1)
                nc.scalar.activation(kinv, kinv, ACT.Ln).then_inc(ssinv2, 1)
                tn.wait(ssinv2)
                nc.scalar.activation(kinv, kinv, ACT.Exp, scale=-0.5).then_inc(kinv_done, 1)
                tn.wait(crem_done)
                tn.wait(cprev_done)
                nc.scalar.activation(dcum[:, :, :], c_[:, :, :], ACT.Exp, scale=-KAPPA)
                nc.scalar.activation(dinv[:, :, :], c_[:, :, :], ACT.Exp, scale=KAPPA)
                nc.scalar.activation(cprev[:, :, :], cprev[:, :, :], ACT.Exp, scale=-KAPPA)
                nc.scalar.activation(crem[:, :, :], crem[:, :, :], ACT.Exp, scale=-KAPPA).then_inc(exps_done, 1)
                tn.wait(T_done)
                nc.scalar.copy(X[:, :, 0:HDA], bank[4][:, :].rearrange("p (h k) -> p h k", k=HDA))
                nc.scalar.copy(v_tok[:, :, :].rearrange("p h k -> p (h k)"), bank[5][:, :])
                nc.scalar.copy(b_tok[:, :, :].rearrange("p h k -> p (h k)"), bank[6][:, :])
                nc.scalar.copy(k_tok[:, :, :].rearrange("p h k -> p (h k)"), bank[7][:, :]).then_inc(tok_done, 1)
                for q in range(GRP):
                    for stage, (mm, out, dst) in enumerate(((S1_done, pw1, (0, 2)), (S2_done, pw2, (2, 4)),
                                                            (S3_done, pw3, (1, 2)))):
                        for hh in range(HG):
                            h = q * HG + hh
                            tn.wait(mm, 8, h + 1)
                            n = (dst[1] - dst[0]) * P
                            nc.scalar.copy(pw[:, hh, dst[0]:dst[1], :].rearrange("p a c -> p (a c)"),
                                           bank[4 + h % 2][:, 0:n]).then_inc(out, 1)
                tn.wait(O_done, 2)
                nc.scalar.copy(flat(o_[:, :, :]), bank[3][:, :]).then_inc(o_done, 1)
                tn.wait(var_done)
                nc.scalar.activation(flat(sq[:, :, :]), bank[0][:, :], ACT.Ln, bias=g.eps[:, 2:3], scale=1.0 / HDA
                                     ).then_inc(var1, 1)
                tn.wait(var1)
                nc.scalar.activation(sq[:, :, :], sq[:, :, :], ACT.Exp, scale=-0.5).then_inc(rs_done, 1)
                tn.wait(normed)
                for j in range(PAIRS):
                    ins = nc.scalar.activation(oc[:, j, :], oc[:, j, :], ACT.Identity,
                                               bias=col("lnx_b")[:, j:j + 1], scale=col("lnx_w")[:, j:j + 1])
                ins.then_inc(affine_done, 1)
            each_tile(act, tile)

        @block.gpsimd
        def _(pool):
            tt = nc.gpsimd.tensor_tensor
            nc.gpsimd.tensor_scalar(one_minus_ka[:, :], col("k_a"), -1.0, 1.0, ALU.mult, ALU.add).then_inc(am1, 1)
            pool.wait_ge(am1, 1)
            pool.sem_inc(am2, 1)
            for h in range(2):
                part = slice(h * HDA, (h + 1) * HDA)
                ins = nc.gpsimd.tensor_copy(eye[part, :], g.ident[part, part])
            ins.then_inc(eye_done, 1)
            pool.wait_ge(eye_done, 1)

            def tile(tn, sample):
                tn.wait(sig_done)
                tn.wait(c_done)
                tt(cprev[:, :, :], c_[:, :, :], sig[:, :, :], ALU.subtract).then_inc(cprev_done, 1)
                tt(blocks(crem[:, :, :]), blocks(c_[:, :, :])[:, :, BLK - 1:BLK].to_broadcast([P, PAIRS * NB, BLK]),
                   blocks(c_[:, :, :]), ALU.subtract).then_inc(crem_done, 1)
                tn.wait(gates_done)
                tt(kmod[:, :, :], a_[:, :, :], bc(col("k_a"), 2, P), ALU.mult).then_inc(am1, 1)
                tn.wait(am1, 1, 2)
                tt(kmod[:, :, :], kmod[:, :, :], bc(one_minus_ka[:, :], 2, P), ALU.add).then_inc(am2, 1)
                tn.wait(am2, 1, 2)
                tt(kmod[:, :, :], kmod[:, :, :], k_, ALU.mult).then_inc(kmod_done, 1)
                tn.wait(kkn_done)
                tt(ba[:, :, :], kk, a_[:, :, :], ALU.mult).then_inc(ba_done, 1)
                tn.wait(exps_done)
                tn.wait(ba_done)
                tn.wait(kmod_done)
                tt(kend[:, :, :], kmod[:, :, :], crem[:, :, :], ALU.mult).then_inc(kend_done, 1)
                tn.wait(kend_done, 2, 1)
                tt(crem[:, :, :], ba[:, :, :], crem[:, :, :], ALU.mult).then_inc(kend_done, 1)
                tt(rk[:, :, :], r_, bc(col("r_k"), 2, P), ALU.mult).then_inc(rk1, 1)
                tn.wait(rk1)
                tt(rk[:, :, :], rk[:, :, :], kmod[:, :, :], ALU.mult).then_inc(rk_done, 1)
                tn.wait(tok_done)
                for q in range(GRP):
                    if q:
                        tn.wait(O_done, 2, 1)
                    for dst, tok in ((b_msk, b_tok), (k_msk, k_tok)):
                        ins = tt(dst, bc(tok[:, q * HG:(q + 1) * HG, :], 2, NB),
                                 bc(bc(g.blockmask[:, :], 1, HG), 3, HDA), ALU.mult)
                    ins.then_inc(msk_done, 1)
                    dend = dcum[:, q * JG_:(q + 1) * JG_, :].rearrange("p j (b c) -> p j b c", c=BLK)
                    for jj in range(JG_):
                        if jj == 0 and q:
                            tn.wait(GT_done, 4, JG_)
                        ins = tt(Dg[:, jj, :, :], bc(eye[:, :], 1, NB), bc(dend[:, jj, :, BLK - 1], 2, HDA), ALU.mult)
                    ins.then_inc(Dg_done, 1)
            each_tile(pool, tile)

        @block.vector
        def _(dve):
            tt, stt = nc.vector.tensor_tensor, nc.vector.scalar_tensor_tensor
            dve.sem_inc(raw_free, 1)
            nc.vector.memset(S[:, NB, :, :], 0.0).then_inc(saved, 1)

            def tile(tn, sample):
                at = tn.col(P)
                dve.wait_ge(loaded, tn.t * 16 + 16)
                now, before = raw[:, :, 1:1 + P], raw[:, :, 0:P]
                tt(diff[:, :, :], before, now, ALU.subtract).then_inc(diff_done, 1)
                tn.wait(diff_done)
                if sample:
                    first = lambda ap: ap.rearrange("p j (b c) -> p j b c", c=BLK)[:, :, :, 0]
                    tt(first(diff[:, :, :]), g.shiftT[:, :, :], first(now), ALU.subtract).then_inc(diff_done, 1)
                    dve.wait_ge(diff_done, NT + 1)
                for j in range(NA):
                    mu = g.colB[:, ROW_B["mu_a"] + j:ROW_B["mu_a"] + j + 1]
                    ins = stt(mixed[:, j, :], diff[:, j, :], mu, now[:, j, :], ALU.mult, ALU.add)
                ins.then_inc(mixed_done, 1)
                tn.wait(mixed_done)
                dve.sem_inc(raw_free, 1)
                tt(kk, k_, bc(col("k_k"), 2, P), ALU.mult).then_inc(kk_done, 1)
                tn.wait(kk_done)
                tt(kk2, kk, kk, ALU.mult).then_inc(kk2_done, 1)
                tn.wait(ss_done)
                nc.vector.tensor_scalar(flat(kinv), bank[3][:, :], 1e-24, None, ALU.max).then_inc(ssinv1, 1)
                tn.wait(sig_done)
                nc.vector.tensor_tensor_scan(flat(c_[:, :, :]), g.reset[:, :], flat(sig[:, :, :]), 0.0,
                                             ALU.mult, ALU.add).then_inc(c_done, 1)
                tn.wait(kinv_done)
                tt(kk, kk, kinv, ALU.mult).then_inc(kkn_done, 1)
                tn.wait(kkn_done)
                tn.wait(exps_done)
                stt(AR[:, :, 0, :], kk, -1.0, cprev[:, :, :], ALU.mult, ALU.mult)
                tt(AR[:, :, 1, :], r_, dcum[:, :, :], ALU.mult)
                tn.wait(ba_done)
                tt(bt[:, :, :], ba[:, :, :], dinv[:, :, :], ALU.mult)
                tn.wait(kmod_done)
                tt(kt[:, :, :], kmod[:, :, :], dinv[:, :, :], ALU.mult).then_inc(tilde_done, 1)
                if sample:
                    nc.vector.tensor_copy(S[:, 0:NS, :, :].rearrange("p b j v -> p (b j v)"),
                                          S_samples[:, :, :, :].rearrange("p b j v -> p (b j v)")).then_inc(state_in, 1)
                else:
                    tn.wait(saved)
                    nc.vector.tensor_copy(S[:, 0, :, :], S[:, NB, :, :]).then_inc(state_in, 1)
                tn.wait(state_in)
                for q in range(GRP):
                    for hh in range(HG):
                        h = q * HG + hh
                        tn.wait(gram_done, 8, h + 1)
                        tt(GM[:, hh, :, :].rearrange("p a c -> p (a c)"), bank[h % 2][:, :],
                           g.gram_mask[:, :, :, :].rearrange("p a b c -> p (a b c)"), ALU.mult)
                        tt(AM[:, hh, :], bank[2 + h % 2][:, 2 * P:3 * P], g.after[:, :], ALU.mult).then_inc(gm_done, 1)
                    for stage, (mm, out) in enumerate(((S1_done, x1), (S2_done, x2), (S3_done, x3), (S4_done, x4),
                                                       (S5_done, x5))):
                        for hh in range(HG):
                            h = q * HG + hh
                            tn.wait(mm, 8, h + 1)
                            if stage == 0:
                                nc.vector.tensor_copy(X[:, h, HDA:P], bank[6 + h % 2][:, 0:HDA]).then_inc(out, 1)
                            else:
                                tt(X[:, h, :], X[:, h, :], bank[6 + h % 2][:, 0:P], ALU.add).then_inc(out, 1)
                    js = slice(q * JG_, (q + 1) * JG_)
                    tn.wait(M_done, 2, q + 1)
                    tt(MT[:, js, :], bank[0][:, 0:JG_ * P].rearrange("p (j c) -> p j c", c=P), AR[:, js, 1, :],
                       ALU.add).then_inc(MT_done, 1)
                    tn.wait(Dg_done, 2, q + 1)
                    for jj in range(JG_):
                        tn.wait(GT_mm, 4, q * JG_ + jj + 1)
                        tt(GT[:, jj, :, :].rearrange("p b k -> p (b k)"), bank[1 + jj][:, :],
                           Dg[:, jj, :, :].rearrange("p b k -> p (b k)"), ALU.add).then_inc(GT_done, 1)
                    for b in range(NB):
                        tn.wait(chain_mm, 16, q * NB + b + 1)
                        dst = S_samples[:, b, js, :] if sample else S[:, b + 1, js, :]
                        nc.vector.tensor_copy(dst, bank[6 + b % 2][:, 0:JG_ * HDA].rearrange("p (j v) -> p j v", v=HDA)
                                              ).then_inc(chained, 1)
                if not sample:
                    dve.sem_inc(saved, 1)
                tn.wait(mean_done)
                stt(flat(oc[:, :, :]), bank[5][:, :], -1.0 / HDA, flat(o_[:, :, :]), ALU.mult, ALU.add
                    ).then_inc(oc_done, 1)
                tn.wait(oc_done)
                tt(sq[:, :, :], oc[:, :, :], oc[:, :, :], ALU.mult).then_inc(sq_done, 1)
                tt(flat(o_[:, :, :]), bank[4][:, :], flat(v_), ALU.mult).then_inc(bonus_mul, 1)
                tn.wait(rs_done)
                tt(oc[:, :, :], oc[:, :, :], sq[:, :, :], ALU.mult).then_inc(normed, 1)
                tn.wait(bonus_mul)
                tn.wait(affine_done)
                tt(oc[:, :, :], oc[:, :, :], o_[:, :, :], ALU.add).then_inc(summed_, 1)
                tn.wait(summed_)
                tt(g.act[:, 0:PAIRS, ds(at, P)], oc[:, :, :], gl[:, :, :], ALU.mult).then_inc(out_done, 1)
                tn.wait(out_done)
            each_tile(dve, tile)

        @block.tensor
        def _(pe):
            mm = nc.tensor.matmul
            pe.wait_ge(weights_in, 48)

            def tile(tn, sample):
                tn.wait(lora_in)
                for j in range(PAIRS):
                    js = slice(j * P, (j + 1) * P)
                    mm(bank[0][:, js], w2[0:64, js], tanh_in[:, :], start=True, stop=True)
                    mm(bank[1][:, js], w2[64:128, js], mixed[64:128, JWA, :], start=True, stop=True)
                    ins = mm(bank[2][:, js], g2[:, js], sig_in[:, :], start=True, stop=True)
                ins.then_inc(lora_done, 1)
                tn.wait(kk2_done)
                mm(bank[3][:, :], g.ones64[:, :], flat(kk2), start=True, stop=True).then_inc(ss_done, 1)
                tn.wait(tilde_done)
                tn.wait(kend_done, 2)
                for j in range(PAIRS):
                    js = slice(j * P, (j + 1) * P)
                    for i, x in enumerate((AR[:, j, 0, :], v_[:, j, :], crem[:, j, :], kend[:, j, :])):
                        ins = nc.tensor.transpose(bank[4 + i][:, js], x, g.ident[:, :])
                ins.then_inc(T_done, 1)
                for q in range(GRP):
                    for hh in range(HG):
                        h = q * HG + hh
                        j, part = h // 2, slice(64 * (h % 2), 64 * (h % 2) + 64)
                        if hh >= 2:
                            tn.wait(gm_done, 8, h - 1)
                        rhs = AR[part, j, :, :].rearrange("p a c -> p (a c)")
                        mm(bank[h % 2][:, 0:2 * P], bt[part, j, :], rhs, start=True, stop=True)
                        mm(bank[h % 2][:, 2 * P:4 * P], kt[part, j, :], rhs, start=True, stop=True)
                        mm(bank[2 + h % 2][:, 2 * P:3 * P], AR[part, j, 0, :], bt[part, j, :], start=True, stop=True
                           ).then_inc(gram_done, 1)
                    if q == 0:
                        tn.wait(tok_done)
                    stages = ((S1_done, None, gm_done), (S2_done, pw1, x1), (S3_done, pw2, x2),
                              (S4_done, pw3, x3), (S5_done, None, x4))
                    for stage, (done, powers, xs) in enumerate(stages):
                        for hh in range(HG):
                            h = q * HG + hh
                            if hh < 2 and stage:
                                tn.wait(xs, 8, (q + 1) * HG)
                                if stage < 4:
                                    tn.wait((None, pw1, pw2, pw3)[stage], 8, (q + 1) * HG)
                            else:
                                tn.wait(xs, 8, h + 1)
                                if powers is not None:
                                    tn.wait(powers, 8, h + 1)
                            if hh >= 2:
                                tn.wait((x1, x2, x3, x4, x5)[stage], 8, h - 1)
                                if stage < 3:
                                    tn.wait((pw1, pw2, pw3)[stage], 8, h - 1)
                            bp, bx = bank[4 + h % 2], bank[6 + h % 2]
                            AT, AakT, A_ = GM[:, hh, 0, :], GM[:, hh, 2, :], AM[:, hh, :]
                            A2T, A2, A4T, A4 = (pw[:, hh, i, :] for i in range(4))
                            A8T = A2
                            if stage == 0:
                                mm(bp[:, 0:P], A_, AT, start=True, stop=True)
                                mm(bp[:, P:2 * P], AT, A_, start=True, stop=True)
                                ins = mm(bx[:, 0:HDA], AakT, v_tok[:, h, :], start=True, stop=True)
                            else:
                                if stage == 1:
                                    mm(bp[:, 0:P], A2, A2T, start=True, stop=True)
                                    mm(bp[:, P:2 * P], A2T, A2, start=True, stop=True)
                                if stage == 2:
                                    mm(bp[:, 0:P], A4, A4T, start=True, stop=True)
                                ins = mm(bx[:, 0:P], (None, AT, A2T, A4T, A8T)[stage], X[:, h, :],
                                         start=True, stop=True)
                            ins.then_inc(done, 1)
                    tn.wait(x5, 8, (q + 1) * HG)
                    tn.wait(msk_done, 2, q + 1)
                    for hh in range(HG):
                        h = q * HG + hh
                        jj, part = hh // 2, slice(64 * (h % 2), 64 * (h % 2) + 64)
                        ins = mm(bank[0][part, jj * P:(jj + 1) * P], X[:, h, 0:HDA], GM[:, hh, 1, :],
                                 start=True, stop=True)
                    ins.then_inc(M_done, 1)
                    for hh in range(HG):
                        h = q * HG + hh
                        jj, part = hh // 2, slice(64 * (h % 2), 64 * (h % 2) + 64)
                        ins = mm(bank[1 + jj][part, :], X[:, h, 0:HDA],
                                 b_msk[:, hh, :, :].rearrange("p b k -> p (b k)"), start=True, stop=True)
                        if hh % 2:
                            ins.then_inc(GT_mm, 1)

                    def chain(b, with_state):
                        for hh in range(HG):
                            h = q * HG + hh
                            jj, part = hh // 2, slice(64 * (h % 2), 64 * (h % 2) + 64)
                            out = bank[6 + b % 2][part, jj * HDA:(jj + 1) * HDA]
                            if with_state:
                                ins = mm(out, GT[part, jj, b, :], S[part, b, h // 2, :], start=False, stop=(hh >= 2))
                            else:
                                mm(out, k_msk[:, hh, b, :], v_tok[:, h, :], start=(hh < 2), stop=False)
                                ins = mm(out, b_msk[:, hh, b, :], X[:, h, HDA:P], start=False, stop=False)
                        return ins
                    chain(0, False)
                    if q == 0:
                        held(tn, waited, state_in)
                    held(tn, waited, GT_done, 4, (q + 1) * JG_)
                    for b in range(NB):
                        if b:
                            held(tn, waited, chained, 16, q * NB + b)
                        chain(b, True).then_inc(chain_mm, 1)
                        if b + 1 < NB:
                            chain(b + 1, False)
                    tn.wait(MT_done, 2, q + 1)
                    for hh in range(HG):
                        h = q * HG + hh
                        j, part = h // 2, slice(64 * (h % 2), 64 * (h % 2) + 64)
                        out = bank[3][part, j * P:(j + 1) * P]
                        mm(out, X[:, h, HDA:P], GM[:, hh, 1, :], start=True, stop=False)
                        mm(out, v_tok[:, h, :], GM[:, hh, 3, :], start=False, stop=False)
                        for b in range(NB):
                            ins = mm(out[:, b * BLK:(b + 1) * BLK], S[part, b, j, :],
                                     MT[part, j, b * BLK:(b + 1) * BLK], start=False, stop=(b == NB - 1))
                    ins.then_inc(O_done, 1)
                tn.wait(rk_done)
                mm(bank[4][:, :], g.ones64[:, :], flat(rk[:, :, :]), start=True, stop=True).then_inc(bonus_done, 1)
                tn.wait(o_done)
                mm(bank[5][:, :], g.ones64[:, :], flat(o_[:, :, :]), start=True, stop=True).then_inc(mean_done, 1)
                tn.wait(sq_done)
                mm(bank[0][:, :], g.ones64[:, :], flat(sq[:, :, :]), start=True, stop=True).then_inc(var_done, 1)
            each_tile(pe, tile)


HDB, NBS = 64, 128
WB = HB * HDB
KB = WB // P
GH = HB // 2


def ssm_states_in(nc, g, A, S):
    with Phase(nc, "ssm_in") as ph:
        rows = ph.sb("rows", [P, 2, KB, NBS])
        pt = ph.ps("pt", [P, 2, 2, BANK])
        in0, in1, turned, copied = ph.sems("in0 in1 turned copied")
        loaded = (in0, in1)
        block = ph.block()

        @block.sync
        def _(sp):
            for b in range(NS):
                if b >= 2:
                    sp.wait_ge(turned, b - 1)
                sp.dma_start(rows[:, b % 2, :, :], A["state_ssm"][b, 0].rearrange("(j h) p n -> (h p) j n", h=2)
                             ).then_inc(loaded[b % 2], 16)

        @block.tensor
        def _(pe):
            for b in range(NS):
                pe.wait_ge(loaded[b % 2], 16 * (b // 2 + 1))
                if b >= 2:
                    pe.wait_ge(copied, b - 1)
                for j in range(KB):
                    ins = nc.tensor.transpose(pt[:, b % 2, j // 4, (j % 4) * P:(j % 4 + 1) * P],
                                              rows[:, b % 2, j, :], g.ident[:, :])
                ins.then_inc(turned, 1)

        @block.vector
        def _(dve):
            for b in range(NS):
                dve.wait_ge(turned, b + 1)
                nc.vector.tensor_copy(S[:, b, :].rearrange("p (a c) -> p a c", c=BANK), pt[:, b % 2, :, :]
                                      ).then_inc(copied, 1)


def ssm_states_out(nc, g, S, dsts, name):
    with Phase(nc, name) as ph:
        rows = ph.sb("rows", [P, 2, KB, NBS])
        pt = ph.ps("pt", [P, 2, 2, BANK])
        turned, copied, out0, out1 = ph.sems("turned copied out0 out1")
        stored = (out0, out1)
        block = ph.block()

        @block.tensor
        def _(pe):
            for b in range(len(dsts)):
                if b >= 2:
                    pe.wait_ge(copied, b - 1)
                for j in range(KB):
                    ins = nc.tensor.transpose(pt[:, b % 2, j // 4, (j % 4) * P:(j % 4 + 1) * P],
                                              S[:, b, j * P:(j + 1) * P], g.ident[:, :])
                ins.then_inc(turned, 1)

        @block.vector
        def _(dve):
            for b in range(len(dsts)):
                dve.wait_ge(turned, b + 1)
                if b >= 2:
                    dve.wait_ge(stored[b % 2], 16 * (b // 2))
                nc.vector.tensor_copy(rows[:, b % 2, :, :].rearrange("p (a j) n -> p a (j n)", a=2),
                                      pt[:, b % 2, :, :]).then_inc(copied, 1)

        @block.sync
        def _(sp):
            for b, dst in enumerate(dsts):
                sp.wait_ge(copied, b + 1)
                sp.dma_start(dst.rearrange("(j h) p n -> (h p) j n", h=2), rows[:, b % 2, :, :]
                             ).then_inc(stored[b % 2], 16)
            for u in range(min(2, len(dsts))):
                sp.wait_ge(stored[u], 16 * ((len(dsts) + 1 - u) // 2))


def mamba(nc, g, A, out_p, out_s):
    with ExitStack() as outer:
        S = outer.enter_context(nc.sbuf_tensor("mb_S", [P, 1, WB], F32))
        S_samples = outer.enter_context(nc.sbuf_tensor("mb_S_samples", [P, NS, WB], F32))
        ssm_states_in(nc, g, A, S_samples)
        mamba_tiles(nc, g, A, S, S_samples)
        ssm_states_out(nc, g, S, [out_p[0, 0]], "ssm_outp")
        ssm_states_out(nc, g, S_samples, [out_s[b, 0] for b in range(NS)], "ssm_outs")


def mamba_tiles(nc, g, A, S, S_samples):
    with Phase(nc, "mamba") as ph:
        raw = ph.sb("raw", [P, NXBC, NB * (BLK + 3)])
        zt = ph.sb("zt", [P, KB, P])
        xc = ph.sb("xc", [P, NXBC, P])
        dt_raw = ph.sb("dt_raw", [HB, P])
        dt_y, dt_e = ph.sb("dt_y", [HB, P]), ph.sb("dt_e", [HB, P])
        dtla = ph.sb("dtla", [HB, 2, P])
        exp_a = ph.sb("exp_a", [HB, 1])
        dtla_tok = ph.sb("dtla_tok", [P, 2, HB])
        RL = ph.sb("RL", [P, HB, P])
        att = ph.sb("att", [P, HB, P])
        CE = ph.sb("CE", [P, HB, P])
        dec = ph.sb("dec", [P, HB, NB])
        xd = ph.sb("xd", [P, HB, HDB])
        xde = ph.sb("xde", [P, HB, HDB])
        to_end = ph.sb("to_end", [P, HB])
        CBm = ph.sb("CBm", [P, 2, P])
        B_tok = ph.sb("B_tok", [P, 2, NBS])
        y = g.sumsq[:, 0:KB * P].rearrange("p (k c) -> p k c", c=P)
        rs = ph.sb("rs", [P, 2, P])
        bank = [ph.ps(f"bank{i}", [P, BANK]) for i in range(8)]
        rl_flat = RL[:, :, :].rearrange("p h l -> p (h l)")
        tap0, tap1 = xc, att[:, 0:NXBC, :]
        tap2, tap3 = RL[:, 0:NXBC, :], CE[:, 0:NXBC, :]
        B_blk = RL[:, :, :].rearrange("p (b u) l -> p b (u l)", u=2)
        squares = xde[:, :, :].rearrange("p h q -> p (h q)").rearrange("p (j c) -> p j c", c=P)
        (xbc_in, z_in, dt_in, raw_free, unfolded, dt_y_done, dt_abs, dt_exp, dt_ln, dt_done, ea, la_done, dtT, dt_tok,
         RL_done, t0, t1, t2, t3, t01, t23, conv_done, silu_done, z_done, seg_mm, seg_done, cum_mm, cum_done,
         CB_mm, CB_done, att_done, dec_done, CE_done, xT_done, xd_done, end_mm, end_done, xde_done, B_T, B_done,
         Bblk_done, y_mm, skip_done, y_done, yz_done, sq_done, ss_mm, var1, rs_done, rms_done, out_done,
         st_mm, st_dec, st_done, waited, yz_free, y_mm_credit, out_credit, st_mm_all) = ph.sems(
            "xbc_in z_in dt_in raw_free unfolded dt_y_done dt_abs dt_exp dt_ln dt_done ea la_done dtT dt_tok "
            "RL_done t0 t1 t2 t3 t01 t23 conv_done silu_done z_done seg_mm seg_done cum_mm cum_done "
            "CB_mm CB_done att_done dec_done CE_done xT_done xd_done end_mm end_done xde_done B_T B_done "
            "Bblk_done y_mm skip_done y_done yz_done sq_done ss_mm var1 rs_done rms_done out_done "
            "st_mm st_dec st_done waited "
            "yz_free y_mm_credit out_credit st_mm_all")
        block = ph.block()
        QH = BANK // P

        def window(w, sample):
            if sample:
                v = raw[:, :, :].rearrange("p j (b c) -> p j b c", c=BLK + 3)
                return v[:, :, :, w:w + BLK]
            return raw[:, :, w:w + P]

        def fold(ap, sample):
            return ap.rearrange("p j (b c) -> p j b c", c=BLK) if sample else ap

        def tap_w(w, sample):
            at = ROW_B["conv_w"] + w * NXBC
            v = bc(g.colB[:, at:at + NXBC], 2, P)
            return fold(v, True) if sample else v

        @block.sync
        def _(sp):
            def load(tn, sample):
                xbc = g.pT[JX * P:NAB * P, :].rearrange("(j p) c -> p j c", p=P)
                z = g.pT[JZ * P:JX * P, :].rearrange("(j p) c -> p j c", p=P)
                at = tn.col(P, HALO)
                tn.wait(raw_free)
                if sample:
                    sp.wait_ge(out_done, NT - 1)
                    sp.dma_start(y[:, :, :], xbc[:, 0:KB, ds(at, P)]).then_inc(xbc_in, 16)
                    sp.dma_start(xd[:, 0:(NXBC - KB) * 2, :].rearrange("p (j u) c -> p j (u c)", u=2),
                                 xbc[:, KB:NXBC, ds(at, P)]).then_inc(xbc_in, 16)
                else:
                    at3 = tn.col(P, 0)
                    sp.dma_start(raw[:, :, 0:3 + P], xbc[:, :, ds(at3, 3 + P)]).then_inc(xbc_in, 16)
                sp.dma_start(dt_raw[:, :], g.pT[NAB * P:NAB * P + HB, ds(at, P)]).then_inc(dt_in, 16)
                tn.wait(yz_free)
                sp.dma_start(zt[:, :, :], z[:, :, ds(at, P)]).then_inc(z_in, 16)
            each_tile(sp, load)

        @block.vector
        def _(dve):
            tt, stt = nc.vector.tensor_tensor, nc.vector.scalar_tensor_tensor
            dve.sem_inc(raw_free, 1)
            dve.sem_inc(yz_free, 1)
            dve.sem_inc(out_credit, 1)
            dve.wait_ge(ea, 1)
            nc.vector.memset(S[:, :, :], 0.0).then_inc(st_done, 1)

            def tile(tn, sample):
                at = tn.col(P)
                after, notafter = (g.after, g.notafter) if sample else (g.after128, g.notafter128)
                if sample:
                    dve.wait_ge(xbc_in, NTP * 16 + 32)
                    v = raw[:, :, :].rearrange("p j (b c) -> p j b c", c=BLK + 3)
                    nc.vector.tensor_copy(v[:, 0:KB, :, 3:], fold(y[:, :, :], True))
                    nc.vector.tensor_copy(v[:, KB:, :, 3:], fold(
                        xd[:, 0:(NXBC - KB) * 2, :].rearrange("p (j u) c -> p j (u c)", u=2), True))
                    nc.vector.tensor_copy(v[:, :, :, 0:3], g.convT[:, :, :].rearrange("p j (b c) -> p j b c", c=3)
                                          ).then_inc(unfolded, 1)
                    dve.wait_ge(unfolded, 1)
                else:
                    dve.wait_ge(xbc_in, tn.t * 16 + 16)
                dve.wait_ge(dt_in, tn.t * 16 + 16)
                nc.vector.tensor_scalar(dt_y[:, :], dt_raw[:, :], g.dt_bias[:, 0:1], None, ALU.add
                                        ).then_inc(dt_y_done, 1)
                tn.wait(dt_y_done)
                stt(dt_e[:, :], dt_y[:, :], -1.0, dt_y[:, :], ALU.mult, ALU.max).then_inc(dt_abs, 1)
                tn.wait(y_mm_credit)
                tt(fold(tap0[:, :, :], sample), window(0, sample), tap_w(0, sample), ALU.mult).then_inc(t0, 1)
                tt(fold(tap1, sample), window(1, sample), tap_w(1, sample), ALU.mult).then_inc(t1, 1)
                tn.wait(t1)
                tt(tap0[:, :, :], tap0[:, :, :], tap1, ALU.add).then_inc(t01, 1)
                tn.wait(t01)
                tn.wait(t23)
                tt(xc[:, :, :], tap0[:, :, :], tap2, ALU.add).then_inc(conv_done, 1)
                tn.wait(conv_done)
                dve.sem_inc(raw_free, 1)
                tn.wait(dt_ln)
                stt(dtla[:, 0, :], dt_y[:, :], 0.0, dt_e[:, :], ALU.max, ALU.add).then_inc(dt_done, 1)
                tn.wait(dt_done)
                nc.vector.tensor_scalar(dtla[:, 1, :], dtla[:, 0, :], exp_a[:, 0:1], None, ALU.mult
                                        ).then_inc(la_done, 1)
                tn.wait(dtT)
                nc.vector.tensor_copy(dtla_tok[:, :, :].rearrange("p a h -> p (a h)"), bank[6][:, 0:2 * HB]
                                      ).then_inc(dt_tok, 1)
                tn.wait(dt_tok)
                tt(RL[:, :, :], bc(dtla_tok[:, 1, :], 2, P), bc(notafter[:, :], 1, HB), ALU.mult).then_inc(RL_done, 1)
                tn.wait(xT_done)
                for i in range(2):
                    ins = tt(xd[:, i * GH:(i + 1) * GH, :], bank[4 + i][:, :].rearrange("p (h q) -> p h q", q=HDB),
                             bc(dtla_tok[:, 0, i * GH:(i + 1) * GH], 2, HDB), ALU.mult)
                ins.then_inc(xd_done, 1)
                tn.wait(B_T)
                nc.vector.tensor_copy(B_tok[:, :, :].rearrange("p g n -> p (g n)"), bank[7][:, 256:512]
                                      ).then_inc(B_done, 1)
                tt(CBm[:, :, :], bank[7][:, 0:256].rearrange("p (g c) -> p g c", c=P), bc(notafter[:, :], 1, 2),
                   ALU.mult).then_inc(CB_done, 1)
                tn.wait(CB_done)
                tn.wait(seg_done, 4)
                for i in range(2):
                    hs = slice(i * GH, (i + 1) * GH)
                    ins = tt(att[:, hs, :], att[:, hs, :], bc(CBm[:, i, :], 1, GH), ALU.mult)
                ins.then_inc(att_done, 1)
                tn.wait(skip_done)
                tn.wait(y_mm)
                for i in range(2):
                    ins = tt(y[:, 4 * i:4 * i + 4, :], y[:, 4 * i:4 * i + 4, :],
                             bank[4 + i][:, :].rearrange("p (j c) -> p j c", c=P), ALU.add)
                ins.then_inc(y_done, 1)
                if not sample:
                    tn.wait(dec_done)
                    tt(S[:, 0, :].rearrange("p (h q) -> p h q", q=HDB), S[:, 0, :].rearrange("p (h q) -> p h q", q=HDB),
                       bc(dec[:, :, 0], 2, HDB), ALU.mult).then_inc(st_dec, 1)
                    tn.wait(st_dec)
                    dve.wait_ge(st_mm, tn.t + 1)
                    for i in range(2):
                        ins = tt(S[:, 0, i * BANK:(i + 1) * BANK], S[:, 0, i * BANK:(i + 1) * BANK], bank[i][:, :],
                                 ALU.add)
                    ins.then_inc(st_done, 1)
                else:
                    for b in range(NB):
                        v = S_samples[:, b, :].rearrange("p (h q) -> p h q", q=HDB)
                        tt(v, v, bc(dec[:, :, b], 2, HDB), ALU.mult).then_inc(st_dec, 1)
                        dve.wait_ge(st_dec, NTP + b + 1)
                        dve.wait_ge(st_mm, NTP + b + 1)
                        for i in range(2):
                            ins = tt(S_samples[:, b, i * BANK:(i + 1) * BANK], S_samples[:, b, i * BANK:(i + 1) * BANK],
                                     bank[2 * (b % 2) + i][:, :], ALU.add)
                        ins.then_inc(st_done, 1)
                tn.wait(z_done)
                tn.wait(y_done)
                tt(y[:, :, :], y[:, :, :], zt[:, :, :], ALU.mult).then_inc(yz_done, 1)
                tn.wait(yz_done)
                dve.sem_inc(yz_free, 1)
                tn.wait(rs_done)
                for i in range(2):
                    ins = tt(y[:, 4 * i:4 * i + 4, :], y[:, 4 * i:4 * i + 4, :], bc(rs[:, i, :], 1, 4), ALU.mult)
                ins.then_inc(rms_done, 1)
                tn.wait(rms_done)
                at_w = ROW_B["norm_b_w"]
                tt(g.act[:, PAIRS:KACT, ds(at, P)], y[:, :, :], bc(g.colB[:, at_w:at_w + KB], 2, P), ALU.mult
                   ).then_inc(out_done, 1)
                tn.wait(out_done)
                dve.sem_inc(out_credit, 1)
            each_tile(dve, tile)

        @block.gpsimd
        def _(pool):
            tt = nc.gpsimd.tensor_tensor

            def tile(tn, sample):
                if sample:
                    pool.wait_ge(unfolded, 1)
                else:
                    pool.wait_ge(xbc_in, tn.t * 16 + 16)
                tn.wait(y_mm_credit)
                tt(fold(tap2, sample), window(2, sample), tap_w(2, sample), ALU.mult).then_inc(t2, 1)
                tt(fold(tap3, sample), window(3, sample), tap_w(3, sample), ALU.mult).then_inc(t3, 1)
                tn.wait(t2)
                tn.wait(t3)
                tt(tap2, tap2, tap3, ALU.add).then_inc(t23, 1)
                tn.wait(t23)
                tn.wait(silu_done)
                held(tn, waited, cum_done, 4)
                if sample:
                    nc.gpsimd.tensor_copy(dec[:, :, :], CE[:, :, :].rearrange("p h (b c) -> p h b c", c=BLK)[:, :, :, BLK - 1]
                                          ).then_inc(dec_done, 1)
                else:
                    nc.gpsimd.tensor_copy(dec[:, :, 0], CE[:, :, P - 1]).then_inc(dec_done, 1)
                tn.wait(dec_done)
                for i in range(2):
                    hs = slice(i * GH, (i + 1) * GH)
                    ins = tt(CE[:, hs, :], CE[:, hs, :], bc(xc[:, KB + 2 + i, :], 1, GH), ALU.mult)
                ins.then_inc(CE_done, 1)
                tn.wait(end_done)
                tn.wait(xd_done)
                tt(xde[:, :, :], xd[:, :, :], bc(to_end[:, :], 2, HDB), ALU.mult).then_inc(xde_done, 1)
                if sample:
                    tn.wait(B_done)
                    pool.wait_ge(seg_done, 4 * NT)
                    ins = tt(B_blk, bc(B_tok[:, :, :].rearrange("p g n -> p (g n)"), 1, NB),
                             bc(g.blockmask[:, :], 2, 2 * NBS), ALU.mult)
                    ins.then_inc(Bblk_done, 1)
                tn.wait(out_credit)
                tt(y[:, :, :], xc[:, 0:KB, :], bc(g.dskip[:, :], 2, P), ALU.mult).then_inc(skip_done, 1)
            each_tile(pool, tile)

        @block.scalar
        def _(act):
            nc.scalar.activation(exp_a[:, :], g.a_log[:, :], ACT.Exp).then_inc(ea, 1)

            def tile(tn, sample):
                tn.wait(dt_abs)
                nc.scalar.activation(dt_e[:, :], dt_e[:, :], ACT.Exp, scale=-1.0).then_inc(dt_exp, 1)
                tn.wait(dt_exp)
                nc.scalar.activation(dt_e[:, :], dt_e[:, :], ACT.Ln, bias=1.0).then_inc(dt_ln, 1)
                tn.wait(conv_done)
                for j in range(NXBC):
                    at = ROW_B["conv_b"] + j
                    ins = nc.scalar.activation(xc[:, j, :], xc[:, j, :], ACT.Silu, bias=g.colB[:, at:at + 1])
                ins.then_inc(silu_done, 1)
                act.wait_ge(z_in, tn.t * 16 + 16)
                nc.scalar.activation(zt[:, :, :], zt[:, :, :], ACT.Silu).then_inc(z_done, 1)
                for i in range(HB // QH):
                    tn.wait(seg_mm, 4, i + 1)
                    nc.scalar.activation(att[:, i * QH:(i + 1) * QH, :].rearrange("p h l -> p (h l)"),
                                         bank[i % 2][:, :], ACT.Exp, scale=-1.0).then_inc(seg_done, 1)
                    tn.wait(cum_mm, 4, i + 1)
                    nc.scalar.activation(CE[:, i * QH:(i + 1) * QH, :].rearrange("p h l -> p (h l)"),
                                         bank[2 + i % 2][:, :], ACT.Exp, scale=-1.0).then_inc(cum_done, 1)
                tn.wait(end_mm)
                nc.scalar.activation(to_end[:, :], bank[6][:, 32:32 + HB], ACT.Exp, scale=-1.0).then_inc(end_done, 1)
                tn.wait(yz_done)
                tn.wait(st_mm_all)
                nc.scalar.activation(squares, y[:, :, :], ACT.Square).then_inc(sq_done, 1)
                tn.wait(ss_mm)
                nc.scalar.activation(rs[:, :, :].rearrange("p g c -> p (g c)"), bank[6][:, 256:512], ACT.Ln,
                                     bias=g.eps[:, 1:2], scale=1.0 / (WB // 2)).then_inc(var1, 1)
                tn.wait(var1)
                nc.scalar.activation(rs[:, :, :], rs[:, :, :], ACT.Exp, scale=-0.5).then_inc(rs_done, 1)
            each_tile(act, tile)

        @block.tensor
        def _(pe):
            mm = nc.tensor.matmul

            def tile(tn, sample):
                after = g.after if sample else g.after128
                held(tn, waited, la_done)
                nc.tensor.transpose(bank[6][:, 0:HB], dtla[:, 0, :], g.ident[0:HB, 0:HB])
                nc.tensor.transpose(bank[6][:, HB:2 * HB], dtla[:, 1, :], g.ident[0:HB, 0:HB]).then_inc(dtT, 1)
                tn.wait(silu_done)
                for j in range(KB):
                    ins = nc.tensor.transpose(bank[4 + j // 4][:, (j % 4) * P:(j % 4 + 1) * P], xc[:, j, :], g.ident[:, :])
                ins.then_inc(xT_done, 1)
                for i in range(2):
                    mm(bank[7][:, i * P:(i + 1) * P], xc[:, KB + i, :], xc[:, KB + 2 + i, :], start=True, stop=True)
                for i in range(2):
                    ins = nc.tensor.transpose(bank[7][:, 256 + i * P:256 + (i + 1) * P], xc[:, KB + i, :], g.ident[:, :])
                ins.then_inc(B_T, 1)
                tn.wait(RL_done)
                if not sample:
                    tn.wait(st_done)
                for i in range(HB // QH):
                    if i >= 2:
                        tn.wait(seg_done, 4, i - 1)
                        tn.wait(cum_done, 4, i - 1)
                    rhs = rl_flat[:, i * BANK:(i + 1) * BANK]
                    mm(bank[i % 2][:, :], after[:, :], rhs, start=True, stop=True).then_inc(seg_mm, 1)
                    mm(bank[2 + i % 2][:, :], g.ones[:, :], rhs, start=True, stop=True).then_inc(cum_mm, 1)
                mm(bank[6][:, 32:32 + HB], after[:, :], dtla_tok[:, 1, :], start=True, stop=True).then_inc(end_mm, 1)
                tn.wait(att_done)
                tn.wait(CE_done)
                for h in range(HB):
                    part, j = slice(64 * (h % 2), 64 * (h % 2) + 64), h // 2
                    out = bank[4 + j // 4][part, (j % 4) * P:(j % 4 + 1) * P]
                    mm(out, xd[:, h, :], att[:, h, :], start=True, stop=False)
                    if sample:
                        for b in range(NB):
                            ins = mm(out[:, b * BLK:(b + 1) * BLK], S_samples[:, b, h * HDB:(h + 1) * HDB],
                                     CE[:, h, b * BLK:(b + 1) * BLK], start=False, stop=(b == NB - 1))
                    else:
                        ins = mm(out, S[:, 0, h * HDB:(h + 1) * HDB], CE[:, h, :], start=False, stop=True)
                ins.then_inc(y_mm, 1)
                pe.wait_ge(y_mm, tn.t + 1)
                pe.sem_inc(y_mm_credit, 1)
                tn.wait(xde_done)
                if sample:
                    tn.wait(seg_done, 4)
                    pe.wait_ge(Bblk_done, 1)
                    for b in range(NB):
                        if b >= 2:
                            pe.wait_ge(st_done, 1 + NTP + b - 1)
                        for i in range(2):
                            ins = mm(bank[2 * (b % 2) + i][:, :], B_blk[:, b, i * NBS:(i + 1) * NBS],
                                     xde[:, i * GH:(i + 1) * GH, :].rearrange("p h q -> p (h q)"), start=True, stop=True)
                        ins.then_inc(st_mm, 1)
                    pe.wait_ge(st_mm, NTP + NB)
                else:
                    for i in range(2):
                        ins = mm(bank[i][:, :], B_tok[:, i, :], xde[:, i * GH:(i + 1) * GH, :].rearrange("p h q -> p (h q)"),
                                 start=True, stop=True)
                    ins.then_inc(st_mm, 1)
                    pe.wait_ge(st_mm, tn.t + 1)
                pe.sem_inc(st_mm_all, 1)
                tn.wait(sq_done)
                for i in range(2):
                    for j in range(4):
                        ins = mm(bank[6][:, 256 + i * P:256 + (i + 1) * P], g.ones[:, :], squares[:, 4 * i + j, :],
                                 start=(j == 0), stop=(j == 3))
                ins.then_inc(ss_mm, 1)
            pe.sem_inc(y_mm_credit, 1)
            each_tile(pe, tile)


HC = 8
LEVELS = (8, 4, 2, 1)


def hgrn(nc, g, A, out_p, out_s):
    with Phase(nc, "hgrn") as ph:
        def arr(name):
            return ph.sb(name, [P, HC, P])
        raw = ph.sb("raw", [P, 4 * HC, P])
        q_, f_, i_, gg = (raw[:, n * HC:(n + 1) * HC, :] for n in range(4))
        sq_ = arr("sq")
        lf, b_, k_ = arr("lf"), arr("b"), arr("k")
        E = [arr("E0"), arr("E1")]
        QL, KL = [arr("QL0"), arr("QL1")], [arr("KL0"), arr("KL1")]
        Qe, rem = arr("Qe"), arr("rem")
        v_tok, k_tok = arr("v_tok"), lf
        sig_g = arr("sig_g")
        dend = ph.sb("dend", [P, HC, NB])
        Vm = ph.sb("Vm", [P, 2, NB, P])
        room = g.act[:, HC:KACT, :].rearrange("p a b -> p (a b)")
        S = room[:, 0:HC * P].rearrange("p (h v) -> p h v", v=P)
        Sb = ph.sb("Sb", [P, 3, NB + 1, P])
        S_new = room[:, HC * P:HC * P + 2 * NB * P].rearrange("p (a b v) -> p a b v", a=2, b=NB)
        att = room[:, (HC + 2 * NB) * P:(2 * HC + 2 * NB) * P].rearrange("p (h c) -> p h c", c=P)
        o_, osq = QL[0], KL[0]
        rs = QL[1]
        bank = [ph.ps(f"bank{i}", [P, BANK]) for i in range(8)]
        (loaded, raw_free, absf, e1, l1, lf_done, b_done, kx, k_done, sig_q, sig_g_done, q_done, rem_sub, exps, Qe_done,
         kend_done, D_done, E_done, QK_done, gram, att_out, T_done, tok_v, tok_k, Vm_done, H_mm, chained, state_in,
         o_mm, o_done, osq_done, ss_mm, var1, rs_done, normed, gm, out_done, samples_in, S_out, S_kept, waited,
         dend_done, level_used) = ph.sems(
            "loaded raw_free absf e1 l1 lf_done b_done kx k_done sig_q sig_g_done q_done rem_sub exps Qe_done "
            "kend_done D_done E_done QK_done gram att_out T_done tok_v tok_k Vm_done H_mm chained state_in "
            "o_mm o_done osq_done ss_mm var1 rs_done normed gm out_done samples_in S_out S_kept waited "
            "dend_done level_used")
        in0, in1, in2, so0, so1, tile_free = ph.sems("in0 in1 in2 so0 so1 tile_free")
        ins_, outs_ = (in0, in1, in2), (so0, so1)
        block = ph.block()
        flat = lambda ap: ap.rearrange("p h c -> p (h c)")
        two = lambda ap, i: ap[:, 4 * i:4 * i + 4, :].rearrange("p h c -> p (h c)")
        blocks = lambda ap: ap.rearrange("p h (b c) -> p (h b) c", c=BLK)

        @block.sync
        def _(sp):
            src = g.pT[0:NC_ * P, :].rearrange("(j p) c -> p j c", p=P)

            def load(tn, sample):
                at = tn.col(P, HALO)
                tn.wait(raw_free)
                sp.dma_start(raw[:, :, :], src[:, :, ds(at, P)]).then_inc(loaded, 16)
                if sample:
                    def load_states(h):
                        sp.dma_start(Sb[:, h % 3, 0:NB, :], A["state_hgrn"][:, 0, h].rearrange("b k v -> k b v")
                                     ).then_inc(ins_[h % 3], 16)
                    sp.wait_ge(o_mm, NTP * HC)
                    sp.wait_ge(S_kept, NTP * HC)
                    for h in range(3):
                        load_states(h)
                    for h in range(HC):
                        sp.wait_ge(chained, NTP * HC * NB + (h + 1) * NB)
                        sp.dma_start(out_s[:, 0, h].rearrange("b k v -> k b v"), S_new[:, h % 2, :, :]
                                     ).then_inc(outs_[h % 2], 16)
                        if h + 3 < HC:
                            sp.wait_ge(o_mm, NTP * HC + h + 1)
                            load_states(h + 3)
            each_tile(sp, load)
            sp.wait_ge(S_kept, NTP * HC)
            sp.dma_start(out_p[0, 0].rearrange("h k v -> k h v"), S).then_inc(S_out, 16)
            sp.wait_ge(so0, 64)
            sp.wait_ge(so1, 64)
            sp.wait_ge(S_out, 16)

        @block.scalar
        def _(act):
            def tile(tn, sample):
                tn.wait(absf)
                nc.scalar.activation(lf[:, :, :], lf[:, :, :], ACT.Exp, scale=-1.0).then_inc(e1, 1)
                tn.wait(e1)
                nc.scalar.activation(lf[:, :, :], lf[:, :, :], ACT.Ln, bias=1.0).then_inc(l1, 1)
                nc.scalar.activation(sq_[:, :, :], q_, ACT.Sigmoid).then_inc(sig_q, 1)
                nc.scalar.activation(k_[:, :, :], f_, ACT.Sigmoid, scale=-1.0).then_inc(k_done, 1)
                nc.scalar.activation(sig_g[:, :, :], gg, ACT.Sigmoid).then_inc(sig_g_done, 1)
                tn.wait(T_done, 2, 1)
                for i in range(2):
                    ins = nc.scalar.copy(two(v_tok, i), bank[4 + i][:, :])
                ins.then_inc(tok_v, 1)
                tn.wait(b_done)
                nc.scalar.activation(Qe[:, :, :], b_[:, :, :], ACT.Exp)
                tn.wait(rem_sub)
                nc.scalar.activation(rem[:, :, :], rem[:, :, :], ACT.Exp).then_inc(exps, 1)
                for L, h_ in enumerate(LEVELS):
                    tn.wait(D_done, 4, L + 1)
                    v = E[L % 2][:, :, :].rearrange("p h (m u c) -> p (h m) u c", u=2, c=h_)
                    nc.scalar.activation(v[:, :, 0, :], v[:, :, 0, :], ACT.Exp, scale=-1.0)
                    nc.scalar.activation(v[:, :, 1, :], v[:, :, 1, :], ACT.Exp).then_inc(E_done, 1)
                tn.wait(T_done, 2, 2)
                for i in range(2):
                    ins = nc.scalar.copy(two(k_tok, i), bank[6 + i][:, :])
                ins.then_inc(tok_k, 1)
                tn.wait(o_mm, HC)
                for i in range(2):
                    ins = nc.scalar.copy(two(o_, i), bank[i][:, :])
                ins.then_inc(o_done, 1)
                tn.wait(o_done)
                nc.scalar.activation(osq[:, :, :], o_[:, :, :], ACT.Square).then_inc(osq_done, 1)
                tn.wait(ss_mm)
                for i in range(2):
                    ins = nc.scalar.activation(two(rs, i), bank[2 + i][:, :], ACT.Ln, bias=g.eps[:, 1:2], scale=1.0 / P)
                ins.then_inc(var1, 1)
                tn.wait(var1)
                nc.scalar.activation(rs[:, :, :], rs[:, :, :], ACT.Exp, scale=-0.5).then_inc(rs_done, 1)
            each_tile(act, tile)

        @block.gpsimd
        def _(pool):
            tt = nc.gpsimd.tensor_tensor
            def tile(tn, sample):
                tn.wait(b_done)
                tt(blocks(rem[:, :, :]), blocks(b_[:, :, :])[:, :, BLK - 1:BLK].to_broadcast([P, HC * NB, BLK]),
                   blocks(b_[:, :, :]), ALU.subtract).then_inc(rem_sub, 1)
                for L, h_ in enumerate(LEVELS):
                    if L >= 2:
                        tn.wait(QK_done, 4, L - 1)
                    v = b_[:, :, :].rearrange("p h (m c) -> p (h m) c", c=2 * h_)
                    d = E[L % 2][:, :, :].rearrange("p h (m c) -> p (h m) c", c=2 * h_)
                    n = HC * P // (2 * h_)
                    tt(d, v, v[:, :, h_ - 1:h_].to_broadcast([P, n, 2 * h_]), ALU.subtract).then_inc(D_done, 1)
                tn.wait(exps)
                tn.wait(q_done)
                tt(dend[:, :, :], Qe[:, :, :].rearrange("p h (b c) -> p h b c", c=BLK)[:, :, :, BLK - 1],
                   bc(g.ones[:, 0:NB], 1, HC), ALU.mult).then_inc(dend_done, 1)
                tn.wait(k_done)
                tt(rem[:, :, :], rem[:, :, :], k_[:, :, :], ALU.mult).then_inc(kend_done, 1)
                tn.wait(dend_done)
                tt(Qe[:, :, :], Qe[:, :, :], sq_[:, :, :], ALU.mult).then_inc(Qe_done, 1)
                tn.wait(tok_v)
                for h in range(HC):
                    if h >= 2:
                        tn.wait(H_mm, 8, h - 1)
                    tt(Vm[:, h % 2, :, :], bc(v_tok[:, h, :], 1, NB), bc(g.blockmask[:, :], 2, P), ALU.mult
                       ).then_inc(Vm_done, 1)
            each_tile(pool, tile)

        @block.vector
        def _(dve):
            tt, stt = nc.vector.tensor_tensor, nc.vector.scalar_tensor_tensor
            dve.sem_inc(raw_free, 1)
            nc.vector.memset(S, 0.0).then_inc(state_in, 1)
            dve.wait_ge(state_in, 1)
            dve.sem_inc(tile_free, 1)

            def tile(tn, sample):
                at = tn.col(P)
                dve.wait_ge(loaded, tn.t * 16 + 16)
                stt(lf[:, :, :], f_, -1.0, f_, ALU.mult, ALU.max).then_inc(absf, 1)
                tn.wait(l1)
                stt(lf[:, :, :], f_, 0.0, lf[:, :, :], ALU.min, ALU.subtract).then_inc(lf_done, 1)
                tn.wait(lf_done)
                for i in range(2):
                    ins = nc.vector.tensor_tensor_scan(two(b_, i), g.reset[:, :], two(lf, i), 0.0, ALU.mult, ALU.add)
                ins.then_inc(b_done, 1)
                tn.wait(sig_q)
                tt(sq_[:, :, :], sq_[:, :, :], q_, ALU.mult).then_inc(q_done, 1)
                tn.wait(sig_g_done)
                tt(sig_g[:, :, :], sig_g[:, :, :], gg, ALU.mult).then_inc(gm, 1)
                tn.wait(k_done)
                tn.wait(q_done)
                tn.wait(T_done, 2, 1)
                tn.wait(gm)
                dve.sem_inc(raw_free, 1)

                def take(L):
                    for i in range(2):
                        src = bank[2 * (L % 2) + i][:, :].rearrange("p (h c) -> p h c", c=P)
                        dst = att[:, 4 * i:4 * i + 4, :]
                        if L == 0:
                            ins = tt(dst, src, bc(g.level_mask[:, 4, :], 1, 4), ALU.mult)
                        else:
                            ins = nc.vector.copy_predicated(
                                dst, bc(g.level_mask[:, L - 1, :], 1, 4).bitcast(mybir.dt.uint32), src)
                    ins.then_inc(att_out, 1)

                for L in range(4):
                    tn.wait(E_done, 4, L + 1)
                    if L >= 2:
                        tn.wait(gram, 5, L)
                    e, u = E[L % 2], L % 2
                    tt(QL[u][:, :, :], sq_[:, :, :], e[:, :, :], ALU.mult)
                    tt(KL[u][:, :, :], k_[:, :, :], e[:, :, :], ALU.mult).then_inc(QK_done, 1)
                    held(tn, waited, gram, 5, L + 1)
                    take(L)
                    tn.wait(att_out, 5, L + 1)
                held(tn, waited, gram, 5, 5)
                take(4)
                tn.wait(dend_done)
                for h in range(HC):
                    u = h % 3
                    if sample:
                        dve.wait_ge(ins_[u], 16 * (h // 3 + 1))
                        if h >= 2:
                            dve.wait_ge(outs_[h % 2], 16 * (h // 2))
                    else:
                        if h >= 3:
                            tn.wait(o_mm, 8, h - 2)
                        nc.vector.tensor_copy(Sb[:, u, 0, :], S[:, h, :]).then_inc(state_in, 1)
                        dve.wait_ge(state_in, tn.t * HC + (h + 2))
                    tn.wait(H_mm, 8, h + 1)
                    for b in range(NB):
                        src = bank[4 + 2 * (h % 2) + b // 4][:, (b % 4) * P:(b % 4 + 1) * P]
                        dst = S_new[:, h % 2, b, :] if sample else Sb[:, u, b + 1, :]
                        stt(dst, Sb[:, u, b, :], dend[:, h, b:b + 1], src, ALU.mult, ALU.add).then_inc(chained, 1)
                        if not sample:
                            dve.wait_ge(chained, tn.t * (HC * NB) + (h * NB + b + 1))
                    if not sample:
                        nc.vector.tensor_copy(S[:, h, :], Sb[:, u, NB, :]).then_inc(S_kept, 1)
                if not sample:
                    tn.wait(S_kept, 8)
                tn.wait(rs_done)
                for h in range(HC):
                    w = g.colB[:, ROW_B["norm_c_w"] + h:ROW_B["norm_c_w"] + h + 1]
                    ins = stt(o_[:, h, :], o_[:, h, :], w, rs[:, h, :], ALU.mult, ALU.mult)
                ins.then_inc(normed, 1)
                tn.wait(normed)
                tt(g.act[:, 0:HC, ds(at, P)], o_[:, :, :], sig_g[:, :, :], ALU.mult).then_inc(out_done, 1)
                tn.wait(out_done)
                dve.sem_inc(tile_free, 1)
            each_tile(dve, tile)

        @block.tensor
        def _(pe):
            mm = nc.tensor.matmul

            def tile(tn, sample):
                pe.wait_ge(loaded, tn.t * 16 + 16)
                tn.wait(tile_free)
                for h in range(HC):
                    ins = nc.tensor.transpose(bank[4 + h // 4][:, (h % 4) * P:(h % 4 + 1) * P], i_[:, h, :], g.ident[:, :])
                ins.then_inc(T_done, 1)

                def gram_level(L):
                    K, Q = (k_, sq_) if L == 0 else (KL[(L - 1) % 2], QL[(L - 1) % 2])
                    for h in range(HC):
                        ins = mm(bank[2 * (L % 2) + h // 4][:, (h % 4) * P:(h % 4 + 1) * P], K[:, h, :], Q[:, h, :],
                                 start=True, stop=True)
                    ins.then_inc(gram, 1)
                tn.wait(k_done)
                tn.wait(q_done)
                gram_level(0)
                for L in range(1, 5):
                    tn.wait(QK_done, 4, L)
                    if L >= 2:
                        tn.wait(att_out, 5, L - 1)
                    gram_level(L)
                    if L == 1:
                        tn.wait(kend_done)
                        for h in range(HC):
                            ins = nc.tensor.transpose(bank[6 + h // 4][:, (h % 4) * P:(h % 4 + 1) * P], rem[:, h, :],
                                                      g.ident[:, :])
                        ins.then_inc(T_done, 1)

                def states(h):
                    if h == 0:
                        tn.wait(tok_k)
                    tn.wait(Vm_done, 8, h + 1)
                    if h >= 2:
                        tn.wait(chained, HC * NB, (h - 1) * NB)
                    for i in range(2):
                        ins = mm(bank[4 + 2 * (h % 2) + i][:, :], k_tok[:, h, :],
                                 Vm[:, h % 2, 4 * i:4 * i + 4, :].rearrange("p b v -> p (b v)"), start=True, stop=True)
                    ins.then_inc(H_mm, 1)
                states(0)
                states(1)
                tn.wait(att_out, 5, 5)
                tn.wait(Qe_done)
                for h in range(HC):
                    if sample:
                        pe.wait_ge(ins_[h % 3], 16 * (h // 3 + 1))
                    else:
                        tn.wait(chained, HC * NB, (h + 1) * NB - 1)
                    out = bank[h // 4][:, (h % 4) * P:(h % 4 + 1) * P]
                    mm(out, v_tok[:, h, :], att[:, h, :], start=True, stop=False)
                    for b in range(NB):
                        ins = mm(out[:, b * BLK:(b + 1) * BLK], Sb[:, h % 3, b, :], Qe[:, h, b * BLK:(b + 1) * BLK],
                                 start=False, stop=(b == NB - 1))
                    ins.then_inc(o_mm, 1)
                    if h + 2 < HC:
                        states(h + 2)
                tn.wait(osq_done)
                for i in range(2):
                    ins = mm(bank[2 + i][:, :], g.ones[:, :], two(osq, i), start=True, stop=True)
                ins.then_inc(ss_mm, 1)
                tn.wait(ss_mm)
            each_tile(pe, tile)


def allocate(nc, g, ctx):
    def sb(name, shape):
        return ctx.enter_context(nc.sbuf_tensor(name, shape, F32))
    g.xT = sb("xT", [P, KD, T])
    g.sumsq = sb("sumsq", [P, T])
    g.ident = sb("ident", [P, P])
    g.ones = sb("ones", [P, P])
    g.eps = sb("eps", [P, 3])
    g.blockmask = sb("blockmask", [P, NB])
    g.reset = sb("reset", [P, 4 * P])
    g.level_mask = sb("level_mask", [P, 5, P])
    g.colA = sb("colA", [P, P])
    g.colB = sb("colB", [P, NROW_B])
    g.scT = sb("scT", [P, KD, SEQS])
    g.mod = sb("mod", [P, DEPTH * 6 * KD, SEQS])
    g.scale = sb("scale", [P, DEPTH, 2, KD, SEQS])
    g.modcol = lambda layer, j: g.mod[:, (layer * 6 + j) * KD:(layer * 6 + j + 1) * KD, :]


def allocate_first_mixers(nc, g, ctx):
    def sb(name, shape):
        return ctx.enter_context(nc.sbuf_tensor(name, shape, F32))
    g.ones64 = sb("ones64", [P, P])
    g.before = sb("before", [P, P])
    g.notafter = sb("notafter", [P, P])
    g.after = sb("after", [P, P])
    g.notafter128 = sb("notafter128", [P, P])
    g.after128 = sb("after128", [P, P])
    g.gram_mask = sb("gram_mask", [P, 2, 2, P])
    g.shiftT = sb("shiftT", [P, NA, NS])
    g.convT = sb("convT", [P, NXBC, NS * 3])
    g.tails = sb("tails", [P, NAB, SEQS * TAIL])
    g.dskip = sb("dskip", [P, KD])
    g.dt_bias = sb("dt_bias", [HB, 1])
    g.a_log = sb("a_log", [HB, 1])


def build(nc, A, outs):
    g = Core()
    (y_prompt, y_sample, rwkv_p, shift_p, ssm_p, conv_p, hgrn_p,
     rwkv_s, shift_s, ssm_s, conv_s, hgrn_s) = outs
    with ExitStack() as ctx:
        g.pT = nc.dram_tensor("pT", [NAB * P + HB, HALO + T], F32).ap()
        allocate(nc, g, ctx)
        first_mixers = ctx.enter_context(ExitStack())
        allocate_first_mixers(nc, g, first_mixers)
        constants(nc, g)
        load_inputs(nc, g, A)
        modulation(nc, g, A)
        with normed_x(nc, g):
            project_to_dram(nc, g, A["w_in_ab"][0], IN_AB, 0, "in_ab", True)
        new_shift_conv(nc, g, shift_p, conv_p, shift_s, conv_s)
        with mixer_output(nc, g):
            rwkv(nc, g, A, rwkv_p, rwkv_s)
            mamba(nc, g, A, ssm_p, ssm_s)
            mixer_out(nc, g, A["w_out_ab"][0], (6, 6), g.modcol(0, 2), "out_ab")
        first_mixers.close()
        ffn(nc, g, A, 0)
        with normed_x(nc, g):
            project_to_dram(nc, g, A["w_in_c"][0], IN_C, 1, "in_c", False)
        with mixer_output(nc, g):
            hgrn(nc, g, A, hgrn_p, hgrn_s)
            mixer_out(nc, g, A["w_out_c"][0], (4, 4), g.modcol(1, 2), "out_c")
        ffn(nc, g, A, 1)
        write_y(nc, g, y_prompt, y_sample)


@contextmanager
def mixer_output(nc, g):
    with nc.sbuf_tensor(f"act{nc.next_id()}", [P, KACT, T], F32) as g.act:
        yield


@contextmanager
def normed_x(nc, g):
    with nc.sbuf_tensor(f"hH{nc.next_id()}", [P, KD, T], F32R) as g.hH, \
            nc.sbuf_tensor(f"hL{nc.next_id()}", [P, KD, T], F32R) as g.hL:
        yield


_OUTS = [(1, 1024, 1024), (8, 16, 1024), (1, 1, 8, 64, 64), (1, 1, 1792), (1, 1, 16, 64, 128), (1, 1, 3, 1536),
         (1, 1, 8, 128, 128), (8, 1, 8, 64, 64), (8, 1, 1792), (8, 1, 16, 64, 128), (8, 1, 3, 1536),
         (8, 1, 8, 128, 128)]


def kernel(**inputs):
    import numpy as _np
    import concourse.bacc as _bacc
    from concourse import mybir as _mybir
    from concourse.bass_utils import run_bass_kernel_spmd as _run

    nc = _bacc.Bacc("TRN2", target_bir_lowering=False, num_devices=1)
    arrays, aps = {}, {}
    for name in inputs:
        a = _np.ascontiguousarray(inputs[name])
        arrays[f"in_{name}"] = a
        aps[name] = nc.dram_tensor(f"in_{name}", a.shape, _mybir.dt.from_np(a.dtype), kind="ExternalInput").ap()
    outs = [nc.dram_tensor(f"out_{i}", shape, _mybir.dt.float32, kind="ExternalOutput").ap()
            for i, shape in enumerate(_OUTS)]
    build(nc, aps, outs)
    r = _run(nc, [arrays], core_ids=[0])
    return tuple(r.results[0][f"out_{i}"] for i in range(len(_OUTS)))
```
